# Optimizing a Trainium2 kernel written in Bass

```python
import jax, jax.numpy as jnp
from jax import lax
import numpy as np

D_MODEL = 1024
BATCH = 1
SEQ = 1024
DEPTH = 1

CTX_LEN = 256
GRID_W = 64
POOL_WIDTH = D_MODEL
POOL_GROUPS = 4
POOL_GROUP_DIM = POOL_WIDTH // POOL_GROUPS
POOL_WINDOWS = (2, 4, 8, 16)
N_HEADS = 16
QK_NOPE = 128
QK_ROPE = 64
V_DIM = 128
Q_LORA = 256
KV_LORA = 128
MLA_WIDTH = N_HEADS * V_DIM
ROPE_THETA = 10000.0
Q_BLOCK = 128
NORM_EPS = 1e-6
IN_SPLITS = (POOL_WIDTH, POOL_WIDTH, Q_LORA, KV_LORA + QK_ROPE, MLA_WIDTH, D_MODEL, D_MODEL)
IN_WIDTH = sum(IN_SPLITS)

kernel_name = "hybrid_pool_mla_prefix_dit_block"

def rms_norm(x, g):
    xf = x.astype(jnp.float32)
    y = xf * lax.rsqrt(jnp.mean(xf * xf, axis=-1, keepdims=True) + NORM_EPS)
    return y.astype(x.dtype) * g

def ada_params(cond, w, b):
    m = jax.nn.silu(cond) @ w + b
    return jnp.split(m, 3, axis=-1)

def split_in(p):
    offsets = [int(o) for o in np.cumsum(IN_SPLITS)[:-1]]
    return jnp.split(p, offsets, axis=-1)

def axial_rope_tables(n_tokens):
    rows = n_tokens // GRID_W
    t_row = jnp.repeat(jnp.arange(rows, dtype=jnp.float32), GRID_W)
    t_col = jnp.tile(jnp.arange(GRID_W, dtype=jnp.float32), rows)
    half = QK_ROPE // 2
    inv = 1.0 / (ROPE_THETA ** (jnp.arange(0, half, 2, dtype=jnp.float32) / half))
    ang_r = t_row[:, None] * inv
    ang_c = t_col[:, None] * inv
    ang = jnp.concatenate([ang_r, ang_r, ang_c, ang_c], axis=-1)
    return jnp.cos(ang), jnp.sin(ang)

def apply_rope(x, cos, sin):
    xr1, xr2, xc1, xc2 = jnp.split(x, 4, axis=-1)
    rot = jnp.concatenate([-xr2, xr1, -xc2, xc1], axis=-1)
    return (x * cos + rot * sin).astype(x.dtype)

def pool_mix(u, w_pool, pool_scale):
    B, L, _ = u.shape
    ug = u.reshape(B, L, POOL_GROUPS, POOL_GROUP_DIM)
    cs = jnp.cumsum(ug.astype(jnp.float32), axis=1)
    cs = jnp.concatenate([jnp.zeros_like(cs[:, :1]), cs], axis=1)
    t = jnp.arange(L)
    pooled = []
    for gi, w in enumerate(POOL_WINDOWS):
        lo = jnp.clip(t - w // 2, 0, L)
        hi = jnp.clip(t + w // 2, 0, L)
        cnt = (hi - lo).astype(jnp.float32)
        csg = cs[:, :, gi]
        pooled.append((csg[:, hi] - csg[:, lo]) / cnt[:, None])
    pooled = jnp.stack(pooled, axis=2).astype(u.dtype)
    d = pooled - ug
    out = jnp.einsum('blgc,gcd->blgd', d, w_pool).reshape(B, L, POOL_WIDTH)
    return out * pool_scale

def mla_project(q_a, kv_a, q_norm_g, w_qb, kv_norm_g, w_kvb, rope):
    B, L, _ = q_a.shape
    q = (rms_norm(q_a, q_norm_g) @ w_qb).reshape(B, L, N_HEADS, QK_NOPE + QK_ROPE)
    q_nope, q_rope = q[..., :QK_NOPE], q[..., QK_NOPE:]
    c_kv, k_rope = kv_a[..., :KV_LORA], kv_a[..., KV_LORA:]
    kv = (rms_norm(c_kv, kv_norm_g) @ w_kvb).reshape(B, L, N_HEADS, QK_NOPE + V_DIM)
    k_nope, v = kv[..., :QK_NOPE], kv[..., QK_NOPE:]
    if rope is not None:
        cos, sin = rope
        q_rope = apply_rope(q_rope, cos[:, None, :], sin[:, None, :])
        k_rope = apply_rope(k_rope, cos, sin)
    return q_nope, q_rope, k_nope, k_rope, v

def block_attention(q_nope, q_rope, k_nope, k_rope, v):
    B, L, H, _ = q_nope.shape
    nb = L // Q_BLOCK
    scale = (QK_NOPE + QK_ROPE) ** -0.5

    def to_blocks(q):
        return q.reshape(B, nb, Q_BLOCK, H, q.shape[-1]).transpose(1, 0, 2, 3, 4)

    def one_block(qs):
        qn, qr = qs
        s = jnp.einsum('bqhd,bkhd->bhqk', qn, k_nope) + jnp.einsum('bqhr,bkr->bhqk', qr, k_rope)
        p = jax.nn.softmax(s.astype(jnp.float32) * scale, axis=-1).astype(v.dtype)
        return jnp.einsum('bhqk,bkhd->bqhd', p, v)

    o = lax.map(one_block, (to_blocks(q_nope), to_blocks(q_rope)))
    return o.transpose(1, 0, 2, 3, 4).reshape(B, L, H * V_DIM)

def merge_branches(pool_out, pool_gate, attn_out, mla_gate, m_pool, m_mla, b_gate, w_proj_pool, w_proj_mla, w_out):
    y_pool = (pool_out * jax.nn.silu(pool_gate)) @ w_proj_pool
    y_mla = (attn_out * jax.nn.silu(mla_gate)) @ w_proj_mla
    g_pool = jax.nn.sigmoid(m_pool + b_gate[:D_MODEL])
    g_mla = jax.nn.sigmoid(m_mla + b_gate[D_MODEL:])
    return (g_pool * y_pool + g_mla * y_mla) @ w_out

def setup_inputs(seed: int = 0) -> dict:
    key = jax.random.key(seed)
    ks = jax.random.split(key, 20)
    f32 = jnp.float32
    n = lambda k, shape, s: jax.random.normal(k, shape, f32) * s
    return {
        "x": n(ks[0], (BATCH, SEQ, D_MODEL), 1.0),
        "c": n(ks[1], (BATCH, D_MODEL), 1.0),
        "ctx": n(ks[2], (BATCH, CTX_LEN, D_MODEL), 1.0),
        "c_ctx": n(ks[3], (D_MODEL,), 1.0),
        "ada_w": n(ks[4], (DEPTH, D_MODEL, 3 * D_MODEL), D_MODEL ** -0.5),
        "ada_b": n(ks[5], (DEPTH, 3 * D_MODEL), 0.02),
        "norm_g": 1.0 + n(ks[6], (DEPTH, D_MODEL), 0.05),
        "w_in": n(ks[7], (DEPTH, D_MODEL, IN_WIDTH), D_MODEL ** -0.5),
        "b_gate": n(ks[8], (DEPTH, 2 * D_MODEL), 0.02),
        "w_pool": n(ks[9], (DEPTH, POOL_GROUPS, POOL_GROUP_DIM, POOL_GROUP_DIM), POOL_GROUP_DIM ** -0.5),
        "pool_scale": 1.0 + n(ks[10], (DEPTH, POOL_WIDTH), 0.1),
        "q_norm_g": 1.0 + n(ks[11], (DEPTH, Q_LORA), 0.05),
        "w_qb": n(ks[12], (DEPTH, Q_LORA, N_HEADS * (QK_NOPE + QK_ROPE)), Q_LORA ** -0.5),
        "kv_norm_g": 1.0 + n(ks[13], (DEPTH, KV_LORA), 0.05),
        "w_kvb": n(ks[14], (DEPTH, KV_LORA, N_HEADS * (QK_NOPE + V_DIM)), KV_LORA ** -0.5),
        "w_proj_pool": n(ks[15], (DEPTH, POOL_WIDTH, D_MODEL), POOL_WIDTH ** -0.5),
        "w_proj_mla": n(ks[16], (DEPTH, MLA_WIDTH, D_MODEL), MLA_WIDTH ** -0.5),
        "w_out": n(ks[17], (DEPTH, D_MODEL, D_MODEL), D_MODEL ** -0.5),
        "final_g": 1.0 + n(ks[18], (D_MODEL,), 0.05),
    }

def reference(x, c, ctx, c_ctx, ada_w, ada_b, norm_g, w_in, b_gate, w_pool, pool_scale, q_norm_g, w_qb,
              kv_norm_g, w_kvb, w_proj_pool, w_proj_mla, w_out, final_g):
    rope = axial_rope_tables(x.shape[1])
    for l in range(DEPTH):
        last = l == DEPTH - 1
        shift, scale, gate = ada_params(c, ada_w[l], ada_b[l])
        shift_c, scale_c, gate_c = ada_params(c_ctx, ada_w[l], ada_b[l])
        hx = rms_norm(x, norm_g[l]) * (1.0 + scale[:, None]) + shift[:, None]
        hc = rms_norm(ctx, norm_g[l]) * (1.0 + scale_c) + shift_c
        ux, gpx, qax, kvax, gmx, mpx, mmx = split_in(hx @ w_in[l])
        uc, gpc, qac, kvac, gmc, mpc, mmc = split_in(hc @ w_in[l])
        qn_x, qr_x, kn_x, kr_x, v_x = mla_project(qax, kvax, q_norm_g[l], w_qb[l], kv_norm_g[l], w_kvb[l], rope)
        qn_c, qr_c, kn_c, kr_c, v_c = mla_project(qac, kvac, q_norm_g[l], w_qb[l], kv_norm_g[l], w_kvb[l], None)
        attn_x = block_attention(qn_x, qr_x,
                                 jnp.concatenate([kn_x, kn_c], axis=1),
                                 jnp.concatenate([kr_x, kr_c], axis=1),
                                 jnp.concatenate([v_x, v_c], axis=1))
        pool_x = pool_mix(ux, w_pool[l], pool_scale[l])
        if not last:
            attn_c = block_attention(qn_c, qr_c, kn_c, kr_c, v_c)
            pool_c = pool_mix(uc, w_pool[l], pool_scale[l])
            ctx = ctx + gate_c * merge_branches(pool_c, gpc, attn_c, gmc, mpc, mmc, b_gate[l],
                                                w_proj_pool[l], w_proj_mla[l], w_out[l])
        x = x + gate[:, None] * merge_branches(pool_x, gpx, attn_x, gmx, mpx, mmx, b_gate[l],
                                               w_proj_pool[l], w_proj_mla[l], w_out[l])
    return rms_norm(x, final_g)


_drawn_inputs = setup_inputs


def setup_inputs(seed=0):
    import zlib

    import numpy as np

    out = dict(_drawn_inputs(seed))
    spreads = {}
    factors = {'ctx': 8.0,
     'ada_b': 4.093,
     'norm_g': 2.679,
     'b_gate': 8.0,
     'q_norm_g': 8.0,
     'kv_norm_g': 8.0}
    for name, (base, spread) in spreads.items():
        noise = np.random.default_rng([zlib.crc32(name.encode()), seed]).standard_normal(out[name].shape)
        drawn = base * np.exp(spread * noise) if base else spread * noise
        out[name] = __import__('jax').numpy.asarray(drawn.astype(out[name].dtype))
    for name, factor in factors.items():
        out[name] = (out[name] * factor).astype(out[name].dtype)
    return out
```

```python
from contextlib import ExitStack

import concourse.bass as bass
from concourse import mybir

F32 = mybir.dt.float32
F32R = mybir.dt.float32r
BF16 = mybir.dt.bfloat16
ACT = mybir.ActivationFunctionType
ALU = mybir.AluOpType
AX_X = mybir.AxisListType.X

P = 128
D = 1024
KT = D // P
SEQ = 1024
CTX = 256
XT = SEQ // P
CT = CTX // P
KEYS = SEQ + CTX
NKT = KEYS // P
HALF = 512
NHALF = SEQ // HALF
QT = HALF // P
HEADS = 16
PAIRS = HEADS // 2
NOPE = 128
ROPE = 64
RH = ROPE // 2
VD = 128
QL = 256
QLT = QL // P
KVL = 128
LORA = QL + KVL + ROPE
MLA = HEADS * VD
WINDOWS = (2, 4, 8, 16)
GROUPS = len(WINDOWS)
PAD = max(WINDOWS) // 2
UW = SEQ + 2 * PAD
EPS = 1e-6
SCALE = float(NOPE + ROPE) ** -0.5

O_U = 0
O_GP = O_U + D
O_QA = O_GP + D
O_KV = O_QA + QL
O_GM = O_KV + KVL + ROPE
O_MP = O_GM + MLA
O_MM = O_MP + D

R_ADAB, R_NG, R_BG, R_PS, R_QG, R_C, R_CC, R_END = 0, 24, 32, 48, 56, 58, 66, 74


class Chip:
    pass


def mm3(nc, out, ah, al, bh, bl, first, last):
    nc.tensor.matmul(out, ah, bh, start=first, stop=False)
    nc.tensor.matmul(out, ah, bl, start=False, stop=False)
    return nc.tensor.matmul(out, al, bh, start=False, stop=last)


def stage_tokens(nc, k):
    GT = [(0, QT), (QT, QT), (XT, CT)]
    NG = len(GT)
    with ExitStack() as ctx:
        def sb(name, shape, dt=F32):
            return ctx.enter_context(nc.sbuf_tensor(name, shape, dt))

        def sem(name):
            return ctx.enter_context(nc.semaphore(name))

        vecs = sb("vecs", [R_END, P])
        xs = sb("xs", [P, QT, D])
        junk = sb("junk", [P, D], BF16)
        ada = sb("ada", [P, 2, 2 * D])
        wlH = sb("wlH", [P, KT, LORA], F32R)
        wlL = sb("wlL", [P, KT, LORA], F32R)
        hcH = sb("hcH", [P, KT, CTX], F32R)
        hcL = sb("hcL", [P, KT, CTX], F32R)
        htmp = sb("htmp", [P, 2, HALF])
        kcos = sb("kcos", [P, XT, RH])
        ksin = sb("ksin", [P, XT, RH])
        kvg = sb("kvg", [P, KVL])
        condT = sb("condT", [P, 2 * KT])
        cond = sb("cond", [P, KT, 2])
        mod = sb("mod", [P, 2 * KT, 2])
        gain = sb("gain", [P, KT, 2])
        ssq = sb("ssq", [P, XT + CT])
        rst = sb("rst", [P, XT + CT])
        rstd = sb("rstd", [P, XT + CT])
        lms = sb("lms", [P, XT + CT, 2])
        lsd = sb("lsd", [P, XT + CT, 2])
        lrs = sb("lrs", [P, XT + CT, 2])
        qn = sb("qn", [P, 2, QL])
        cn = sb("cn", [P, 2, KVL])
        rp1 = sb("rp1", [P, 2, ROPE])
        rp2 = sb("rp2", [P, 2, ROPE])
        kr = sb("kr", [P, 2, ROPE])
        krH = sb("krH", [P, 2, 2, ROPE], F32R)
        krL = sb("krL", [P, 2, 2, ROPE], F32R)

        def pb(name):
            return ctx.enter_context(nc.psum_tensor(name, [P, 512], F32))

        ps_ada = pb("ps_ada")
        ps_x = [pb("ps_x0"), pb("ps_x1")]
        ps_p = [pb("ps_p0"), pb("ps_p1")]
        ps_t = pb("ps_t")
        ps_u = pb("ps_u")
        ps_v = pb("ps_v")

        vec_in = sem("vec_in")
        tab_in = sem("tab_in")
        ada_in = [sem("ada_in0"), sem("ada_in1")]
        gate_in = [sem("gate_in0"), sem("gate_in1")]
        x_in = [sem(f"x_in{j}") for j in range(QT)]
        wl_in = sem("wl_in")
        vt_ps = sem("vt_ps")
        vt_rdy = sem("vt_rdy")
        th_rdy = sem("th_rdy")
        cond_rdy = sem("cond_rdy")
        ada_used = sem("ada_used")
        gate_used = sem("gate_used")
        mod_rdy = sem("mod_rdy")
        gain_rdy = sem("gain_rdy")
        gate_rdy = sem("gate_rdy")
        ssq_rdy = sem("ssq_rdy")
        rst_rdy = sem("rst_rdy")
        rstd_rdy = sem("rstd_rdy")
        xn_rdy = sem("xn_rdy")
        x_ps = sem("x_ps")
        hH_rdy = sem("hH_rdy")
        ht_rdy = sem("ht_rdy")
        hL_rdy = sem("hL_rdy")
        wlH_rdy = sem("wlH_rdy")
        wlL_rdy = sem("wlL_rdy")
        p_ps = sem("p_ps")
        lms_rdy = sem("lms_rdy")
        lsd_rdy = sem("lsd_rdy")
        lrs_rdy = sem("lrs_rdy")
        rope_step = sem("rope_step")
        lat_rdy = sem("lat_rdy")
        latH_rdy = sem("latH_rdy")
        latL_rdy = sem("latL_rdy")
        t_ps = sem("t_ps")
        tH_rdy = sem("tH_rdy")
        tL_rdy = sem("tL_rdy")

        block = ctx.enter_context(nc.Block())

        def x_tile(t):
            return k.x[t * P:(t + 1) * P, :] if t < XT else k.ctx[(t - XT) * P:(t - XT + 1) * P, :]

        def hslice(g, ft):
            t0, n = GT[g]
            if t0 < XT:
                return k.hH[:, ft, t0 * P:(t0 + n) * P], k.hL[:, ft, t0 * P:(t0 + n) * P], n * P
            return hcH[:, ft, :], hcL[:, ft, :], n * P

        @block.sync
        def _(sp):
            rows = [(k.c, R_C), (k.c_ctx, R_CC), (k.ada_b, R_ADAB), (k.norm_g, R_NG), (k.b_gate, R_BG),
                    (k.pool_scale, R_PS), (k.q_norm_g, R_QG)]
            sp.dma_start(k.ident[:], k.ident_d).then_inc(vec_in, 16)
            for v, r in rows:
                sp.dma_start(vecs[r:r + v.shape[0], :], v).then_inc(vec_in, 16)
            for kt in range(KT):
                if kt >= 2:
                    sp.wait_ge(ada_used, kt - 1)
                sp.dma_start(ada[:, kt % 2, :], k.ada_w[kt * P:(kt + 1) * P, 0:2 * D]).then_inc(ada_in[kt % 2], 16)
                if kt < QT:
                    sp.dma_start(xs[:, kt, :], x_tile(kt)).then_inc(x_in[kt], 16)
            sp.dma_start(kcos[:], k.kcos_d.rearrange("(t p) d -> p t d", p=P)).then_inc(tab_in, 16)
            sp.dma_start(ksin[:], k.ksin_d.rearrange("(t p) d -> p t d", p=P)).then_inc(tab_in, 16)
            sp.dma_start(kvg[:], k.kv_norm_g.to_broadcast([P, KVL])).then_inc(tab_in, 16)
            sp.wait_ge(ada_used, KT)
            sp.dma_start(ada[:].rearrange("p a b -> p (a b)")[:, 0:KT * LORA].rearrange("p (a b) -> p a b", a=KT),
                         k.w_in[:, O_QA:O_QA + LORA].rearrange("(a p) n -> p a n", p=P)).then_inc(wl_in, 16)
            for g in range(1, NG):
                sp.wait_ge(x_ps, KT * g)
                for j in range(GT[g][1]):
                    sp.dma_start(xs[:, j, :], x_tile(GT[g][0] + j)).then_inc(x_in[j], 16)
            sp.wait_ge(wlL_rdy, KT)
            for kp in range(KT // 2):
                if kp >= 2:
                    sp.wait_ge(gate_used, kp - 1)
                sp.dma_start(ada[:, kp % 2, :].rearrange("p (a b) -> p a b", a=2),
                             k.ada_w[2 * kp * P:2 * (kp + 1) * P, 2 * D:3 * D].rearrange("(a p) n -> p a n", p=P)
                             ).then_inc(gate_in[kp % 2], 16)

        @block.scalar
        def _(act):
            act.wait_ge(vt_rdy, 1)
            nc.scalar.activation(condT[:], k.vt[:, R_C:R_END], ACT.Tanh, scale=0.5).then_inc(th_rdy, 1)

            def token_stats(g):
                t0, n = GT[g]
                for j in range(n):
                    act.wait_ge(x_in[j], 16 * (g + 1))
                    if t0 + j > 0:
                        act.wait_ge(ssq_rdy, t0 + j)
                    nc.scalar.activation(junk[:], xs[:, j, :], ACT.Square,
                                         accum_out=ssq[:, t0 + j:t0 + j + 1]).then_inc(ssq_rdy, 1)
                act.wait_ge(ssq_rdy, t0 + n)
                nc.scalar.activation(rst[:, t0:t0 + n], ssq[:, t0:t0 + n], ACT.Sqrt, scale=1.0 / D,
                                     bias=k.eps[:, 0:1]).then_inc(rst_rdy, 1)

            def modulate(g):
                if g == 0:
                    act.wait_ge(gain_rdy, 1)
                for ft in range(KT):
                    act.wait_ge(x_ps, KT * g + ft + 1)
                    hi, _, n = hslice(g, ft)
                    j = int(g == NG - 1)
                    nc.scalar.activation(hi, ps_x[ft % 2][:, 0:n], ACT.Identity, scale=gain[:, ft, j:j + 1],
                                         bias=mod[:, ft, j:j + 1]).then_inc(hH_rdy, 1)

            def w_lora():
                act.wait_ge(wl_in, 16)
                st = ada[:].rearrange("p a b -> p (a b)")
                for kt in range(KT):
                    nc.scalar.activation(wlH[:, kt, :], st[:, kt * LORA:(kt + 1) * LORA], ACT.Copy
                                         ).then_inc(wlH_rdy, 1)

            def latent_stats(t):
                act.wait_ge(p_ps, t + 1)
                ps = ps_p[t % 2]
                n = 2 * t if t < XT else 2 * XT + (t - XT)
                if t < XT:
                    act.wait_ge(lms_rdy, n) if n else None
                    nc.scalar.activation(junk[:, 0:QL], ps[:, 0:QL], ACT.Square, scale=QL ** -0.5,
                                         accum_out=lms[:, t, 0:1]).then_inc(lms_rdy, 1)
                    n += 1
                    c0 = QL
                else:
                    c0 = 0
                act.wait_ge(lms_rdy, n)
                nc.scalar.activation(junk[:, 0:KVL], ps[:, c0:c0 + KVL], ACT.Square, scale=KVL ** -0.5,
                                     accum_out=lms[:, t, 1:2]).then_inc(lms_rdy, 1)
                act.wait_ge(lms_rdy, n + 1)
                a = 0 if t < XT else 1
                nc.scalar.activation(lsd[:, t, a:2], lms[:, t, a:2], ACT.Sqrt, bias=k.eps[:, 0:1]).then_inc(lsd_rdy, 1)

            def latent_hi(t):
                act.wait_ge(lat_rdy, t + 1)
                if t >= 2:
                    act.wait_ge(t_ps, t - 1)
                nc.scalar.activation(k.ctokH[:, t, :], cn[:, t % 2, :], ACT.Copy)
                nc.scalar.activation(krH[:, t % 2, :, :], kr[:, t % 2, :].unsqueeze(1).to_broadcast([P, 2, ROPE]),
                                     ACT.Copy).then_inc(latH_rdy, 1)

            def latent_T_hi(t):
                act.wait_ge(t_ps, t + 1)
                c = slice(t * P, (t + 1) * P)
                if t < XT:
                    for i in range(QLT):
                        nc.scalar.activation(k.qnH[:, i, c], ps_t[:, i * P:(i + 1) * P], ACT.Copy,
                                             scale=k.qgs[:, i:i + 1])
                nc.scalar.activation(k.k2H[:, c], ps_t[:, 3 * P:4 * P], ACT.Copy)
                nc.scalar.activation(k.cH[:, c], ps_t[:, 2 * P:3 * P], ACT.Copy).then_inc(tH_rdy, 1)

            token_stats(0)
            modulate(0)
            w_lora()
            for t in range(XT + CT):
                if t == 2:
                    token_stats(1)
                    modulate(1)
                if t == 6:
                    token_stats(2)
                    modulate(2)
                latent_stats(t)
                if t:
                    latent_T_hi(t - 1)
                latent_hi(t)
            latent_T_hi(XT + CT - 1)

        @block.vector
        def _(dve):
            nc.vector.memset(k.eps[:], EPS)
            dve.wait_ge(vt_ps, 1)
            nc.vector.tensor_copy(k.vt[:, 0:R_END], ps_v[:, 0:R_END]).then_inc(vt_rdy, 1)
            dve.wait_ge(th_rdy, 1)
            nc.vector.scalar_tensor_tensor(out=cond[:].rearrange("p a j -> p j a"),
                                           in0=condT[:].rearrange("p (j a) -> p j a", j=2), scalar=1.0,
                                           in1=k.vt[:, R_C:R_END].rearrange("p (j a) -> p j a", j=2),
                                           op0=ALU.add, op1=ALU.mult).then_inc(cond_rdy, 1)
            nc.vector.tensor_scalar(k.qgs[:], k.vt[:, R_QG:R_QG + QLT], SCALE, None, ALU.mult)
            nc.vector.tensor_scalar(k.bgh[:], k.vt[:, R_BG:R_BG + 2 * KT], 0.5, None, ALU.mult)

            def normalise(g):
                t0, n = GT[g]
                dve.wait_ge(rst_rdy, g + 1)
                nc.vector.reciprocal(rstd[:, t0:t0 + n], rst[:, t0:t0 + n]).then_inc(rstd_rdy, 1)
                dve.wait_ge(rstd_rdy, g + 1)
                for j in range(n):
                    nc.vector.tensor_scalar(xs[:, j, :], xs[:, j, :], rstd[:, t0 + j:t0 + j + 1], None,
                                            ALU.mult).then_inc(xn_rdy, 1)

            def modulate(g):
                for ft in range(KT):
                    i = KT * g + ft
                    dve.wait_ge(x_ps, i + 1)
                    dve.wait_ge(hH_rdy, i + 1)
                    if i >= 2:
                        dve.wait_ge(hL_rdy, i - 1)
                    _, _, n = hslice(g, ft)
                    j = int(g == NG - 1)
                    nc.vector.tensor_scalar(htmp[:, ft % 2, 0:n], ps_x[ft % 2][:, 0:n], gain[:, ft, j:j + 1],
                                            mod[:, ft, j:j + 1], ALU.mult, ALU.add).then_inc(ht_rdy, 1)

            def latents(t):
                s = t % 2
                a = 0 if t < XT else 1
                ps = ps_p[s]
                c0 = QL if t < XT else 0
                dve.wait_ge(lsd_rdy, t + 1)
                nc.vector.reciprocal(lrs[:, t, a:2], lsd[:, t, a:2]).then_inc(lrs_rdy, 1)
                if t >= 2:
                    dve.wait_ge(t_ps, t - 1)
                dve.wait_ge(lrs_rdy, t + 1)
                if t < XT:
                    nc.vector.tensor_scalar(qn[:, s, :], ps[:, 0:QL], lrs[:, t, 0:1], None, ALU.mult)
                if t == 0:
                    dve.wait_ge(tab_in, 48)
                nc.vector.scalar_tensor_tensor(out=cn[:, s, :], in0=ps[:, c0:c0 + KVL], scalar=lrs[:, t, 1:2],
                                               in1=kvg[:], op0=ALU.mult, op1=ALU.mult)
                raw = ps[:, c0 + KVL:c0 + KVL + ROPE].rearrange("p (a b c) -> p b a c", a=2, b=2)

                def half(tile, b):
                    return tile[:, s, b * RH:(b + 1) * RH].rearrange("p (a c) -> p a c", a=2)

                if t < XT:
                    cs = kcos[:, t, :].rearrange("p (a c) -> p a c", a=2)
                    sn = ksin[:, t, :].rearrange("p (a c) -> p a c", a=2)
                    for b in range(2):
                        nc.vector.tensor_tensor(half(rp1, b), raw[:, b], cs, ALU.mult)
                        last = nc.vector.tensor_tensor(half(rp2, b), raw[:, 1 - b], sn, ALU.mult)
                    last.then_inc(rope_step, 1)
                    dve.wait_ge(rope_step, t + 1)
                    nc.vector.tensor_tensor(kr[:, s, 0:RH], rp1[:, s, 0:RH], rp2[:, s, 0:RH], ALU.subtract)
                    nc.vector.tensor_tensor(kr[:, s, RH:ROPE], rp1[:, s, RH:ROPE], rp2[:, s, RH:ROPE],
                                            ALU.add).then_inc(lat_rdy, 1)
                else:
                    nc.vector.tensor_copy(half(kr, 0), raw[:, 0])
                    nc.vector.tensor_copy(half(kr, 1), raw[:, 1]).then_inc(lat_rdy, 1)

            def latents_lo(t):
                s = t % 2
                dve.wait_ge(latH_rdy, t + 1)
                nc.vector.tensor_tensor(k.ctokL[:, t, :], cn[:, s, :], k.ctokH[:, t, :].bitcast(F32), ALU.subtract)
                nc.vector.tensor_tensor(krL[:, s, :, :], kr[:, s, :].unsqueeze(1).to_broadcast([P, 2, ROPE]),
                                        krH[:, s, :, :].bitcast(F32), ALU.subtract).then_inc(latL_rdy, 1)

            def latents_T_lo(t):
                c = slice(t * P, (t + 1) * P)
                dve.wait_ge(tH_rdy, t + 1)
                if t < XT:
                    for i in range(QLT):
                        nc.vector.scalar_tensor_tensor(out=k.qnL[:, i, c], in0=ps_t[:, i * P:(i + 1) * P],
                                                       scalar=k.qgs[:, i:i + 1], in1=k.qnH[:, i, c].bitcast(F32),
                                                       op0=ALU.mult, op1=ALU.subtract)
                nc.vector.tensor_copy(k.k2L[:, c], ps_u[:, 0:P])
                nc.vector.tensor_tensor(k.cL[:, c], ps_t[:, 2 * P:3 * P], k.cH[:, c].bitcast(F32),
                                        ALU.subtract).then_inc(tL_rdy, 1)

            normalise(0)
            dve.wait_ge(ada_used, KT)
            b = k.vt[:, R_ADAB:R_ADAB + 2 * KT].unsqueeze(2).to_broadcast([P, 2 * KT, 2])
            nc.vector.scalar_tensor_tensor(out=mod[:], in0=ps_ada[:, 0:4 * KT].rearrange("p (a j) -> p a j", j=2),
                                           scalar=0.5, in1=b, op0=ALU.mult, op1=ALU.add).then_inc(mod_rdy, 1)
            dve.wait_ge(mod_rdy, 1)
            nc.vector.scalar_tensor_tensor(out=gain[:], in0=mod[:, KT:2 * KT, :], scalar=1.0,
                                           in1=k.vt[:, R_NG:R_NG + KT].unsqueeze(2).to_broadcast([P, KT, 2]),
                                           op0=ALU.add, op1=ALU.mult).then_inc(gain_rdy, 1)
            dve.wait_ge(gain_rdy, 1)
            modulate(0)
            for t in range(XT + CT):
                if t == 2:
                    normalise(1)
                    modulate(1)
                if t == 6:
                    normalise(2)
                    modulate(2)
                latents(t)
                if t:
                    latents_T_lo(t - 1)
                latents_lo(t)
            latents_T_lo(XT + CT - 1)
            dve.wait_ge(gate_used, KT // 2)
            nc.vector.scalar_tensor_tensor(out=k.gateT[:], in0=ps_v[:, 0:KT],
                                           scalar=0.5, in1=k.vt[:, R_ADAB + 2 * KT:R_ADAB + 3 * KT],
                                           op0=ALU.mult, op1=ALU.add).then_inc(gate_rdy, 1)

        @block.gpsimd
        def _(pool):
            def modulated_lo(g):
                for ft in range(KT):
                    i = KT * g + ft
                    pool.wait_ge(ht_rdy, i + 1)
                    hi, lo, n = hslice(g, ft)
                    nc.gpsimd.tensor_tensor(lo, htmp[:, ft % 2, 0:n], hi.bitcast(F32), ALU.subtract
                                            ).then_inc(hL_rdy, 1)

            modulated_lo(0)
            st = ada[:].rearrange("p a b -> p (a b)")
            for kt in range(KT):
                pool.wait_ge(wlH_rdy, kt + 1)
                nc.gpsimd.tensor_tensor(wlL[:, kt, :], st[:, kt * LORA:(kt + 1) * LORA], wlH[:, kt, :].bitcast(F32),
                                        ALU.subtract).then_inc(wlL_rdy, 1)
            modulated_lo(1)
            modulated_lo(2)

        @block.tensor
        def _(pe):
            pe.wait_ge(vec_in, 16 * 8)
            nc.tensor.transpose(ps_v[:, 0:R_END], vecs[:], k.ident[0:R_END, 0:R_END]).then_inc(vt_ps, 1)
            pe.wait_ge(cond_rdy, 1)
            for kt in range(KT):
                pe.wait_ge(ada_in[kt % 2], 16 * (kt // 2 + 1))
                for o in range(2 * KT):
                    last = nc.tensor.matmul(ps_ada[:, 2 * o:2 * o + 2], ada[:, kt % 2, o * P:(o + 1) * P],
                                            cond[:, kt, :], start=(kt == 0 and o == 0), stop=(kt == KT - 1),
                                            skip_group_check=True)
                last.then_inc(ada_used, 1)

            def transposes(g):
                t0, n = GT[g]
                pe.wait_ge(xn_rdy, t0 + n)
                for ft in range(KT):
                    i = KT * g + ft
                    if i >= 2:
                        pe.wait_ge(ht_rdy, i - 1)
                    for j in range(n):
                        last = nc.tensor.transpose(ps_x[ft % 2][:, j * P:(j + 1) * P],
                                                   xs[:, j, ft * P:(ft + 1) * P], k.ident[:])
                    last.then_inc(x_ps, 1)

            def project(t):
                w = LORA if t < XT else LORA - QL
                hi, lo = (k.hH, k.hL) if t < XT else (hcH, hcL)
                c = slice(t * P, (t + 1) * P) if t < XT else slice((t - XT) * P, (t - XT + 1) * P)
                if t >= 2:
                    pe.wait_ge(lat_rdy, t - 1)
                for kt in range(KT):
                    last = mm3(nc, ps_p[t % 2][:, 0:w], hi[:, kt, c], lo[:, kt, c], wlH[:, kt, LORA - w:],
                               wlL[:, kt, LORA - w:], kt == 0, kt == KT - 1)
                last.then_inc(p_ps, 1)

            def turn(t):
                s = t % 2
                pe.wait_ge(latL_rdy, t + 1)
                if t:
                    pe.wait_ge(tL_rdy, t)
                if t < XT:
                    for i in range(QLT):
                        nc.tensor.transpose(ps_t[:, i * P:(i + 1) * P], qn[:, s, i * P:(i + 1) * P], k.ident[:])
                nc.tensor.transpose(ps_t[:, 2 * P:3 * P], cn[:, s, :], k.ident[:])
                nc.tensor.transpose(ps_t[:, 3 * P:4 * P], krH[:, s, :, :].rearrange("p a b -> p (a b)").bitcast(F32),
                                    k.ident[:])
                nc.tensor.transpose(ps_u[:, 0:P], krL[:, s, :, :].rearrange("p a b -> p (a b)").bitcast(F32),
                                    k.ident[:]).then_inc(t_ps, 1)

            transposes(0)
            pe.wait_ge(wlL_rdy, KT)
            pe.wait_ge(hL_rdy, KT)
            for t in range(XT + CT):
                if t == 2:
                    transposes(1)
                if t == 6:
                    transposes(2)
                if t == QT:
                    pe.wait_ge(hL_rdy, 2 * KT)
                if t == XT:
                    pe.wait_ge(hL_rdy, 3 * KT)
                project(t)
                if t:
                    turn(t - 1)
            turn(XT + CT - 1)
            for kp in range(KT // 2):
                pe.wait_ge(gate_in[kp % 2], 16 * (kp // 2 + 1))
                for a in range(2):
                    for o in range(KT):
                        last = nc.tensor.matmul(ps_v[:, o:o + 1], ada[:, kp % 2, a * D + o * P:a * D + (o + 1) * P],
                                                cond[:, 2 * kp + a, 0:1], start=(kp == 0 and a == 0 and o == 0),
                                                stop=(kp == KT // 2 - 1 and a == 1), skip_group_check=True)
                last.then_inc(gate_used, 1)


def stage_gates(nc, k):
    G_PER = HEADS // GROUPS
    G0 = KT
    GP0 = G0 + GROUPS * (G_PER + 1)
    MM0, MP0, PA0 = GP0 + KT, GP0 + 2 * KT, GP0 + 3 * KT
    UNITS = PA0 + KT
    GM = 2 * KT
    G_USES = 2 * G_PER + 4
    GPM = GM + GROUPS * G_USES
    MMM = GPM + 2 * KT
    GPH = KT + GROUPS * (G_PER + 3)
    assert UNITS % 2 == 0 and GM % 4 == 0 and G_USES % 4 == 0

    with ExitStack() as ctx:
        def sb(name, shape, dt=F32):
            return ctx.enter_context(nc.sbuf_tensor(name, shape, dt))

        def sem(name):
            return ctx.enter_context(nc.semaphore(name))

        wst = sb("wst", [P, 2, D])
        wH = sb("wH", [P, 2, D], F32R)
        wL = sb("wL", [P, 2, D], F32R)
        up = sb("up", [P, KT, UW])
        dH = sb("dH", [P, 2, SEQ], F32R)
        dL = sb("dL", [P, 2, SEQ], F32R)
        pA = sb("pA", [P, UW])
        pB = sb("pB", [P, UW])
        inv = sb("inv", [P, SEQ])
        th = sb("th", [P, 2, HALF])
        ob = sb("ob", [P, 2, HALF])
        bank = [ctx.enter_context(nc.psum_tensor(f"ps_g{i}", [P, HALF], F32)) for i in range(4)]

        w_in = [sem("w_in0"), sem("w_in1")]
        wH_rdy = sem("wH_rdy2")
        wL_rdy = sem("wL_rdy2")
        used = sem("w_used")
        half_ps = sem("half_ps")
        ev_dve = sem("ev_dve")
        ev_act = sem("ev_act")
        pads = sem("pads")
        th_rdy = sem("th_rdy2")
        stored = [sem("stored0"), sem("stored1")]
        inv_in = sem("inv_in")
        win = sem("win")
        d_rdy = sem("d_rdy")
        dH_rdy = sem("dH_rdy")
        dL_rdy = sem("dL_rdy")
        zp_rdy = sem("zp_rdy")
        zpH_rdy = sem("zpH_rdy")
        zpL_rdy = sem("zpL_rdy")
        thp_in = [sem("thp_in0"), sem("thp_in1")]

        block = ctx.enter_context(nc.Block())

        def w_cols(c0):
            return k.w_in[:, bass.ds(c0, P)].rearrange("(a p) n -> p a n", p=P)

        @block.sync
        def _(sp):
            def load(slot, src):
                sp.dma_start(wst[:, slot, :].rearrange("p (a n) -> p a n", a=KT), src).then_inc(w_in[slot], 16)

            for n in range(2):
                load(n, w_cols(O_U + n * P))
            with sp.Fori(1, KT // 2) as i:
                for b in range(2):
                    sp.wait_ge(wL_rdy, 2 * i + (b - 1))
                    load(b, w_cols((2 * i + b) * P + O_U))
            for g in range(GROUPS):
                if g:
                    sp.wait_ge(d_rdy, 2 * g)
                sp.dma_start(inv[:], k.pool_inv[g:g + 1, :].to_broadcast([P, SEQ])).then_inc(inv_in, 16)
                n = G0 + (G_PER + 1) * g
                with sp.Fori(0, G_PER // 2) as i:
                    for b in range(2):
                        sp.wait_ge(wL_rdy, 2 * i + (n + b - 1))
                        load((n + b) % 2, w_cols((2 * i + (G_PER * g + b)) * P + O_GM))
                n += G_PER
                sp.wait_ge(wL_rdy, n - 1)
                sp.dma_start(wst[:, n % 2, 0:2 * 2 * P].rearrange("p (a n) -> p a n", a=2),
                             k.w_pool[g].rearrange("(a p) n -> p a n", p=P)).then_inc(w_in[n % 2], 16)
            for n0, off in ((GP0, O_GP), (MM0, O_MM), (MP0, O_MP)):
                with sp.Fori(0, KT // 2) as i:
                    for b in range(2):
                        sp.wait_ge(wL_rdy, 2 * i + (n0 + b - 1))
                        load(b, w_cols((2 * i + b) * P + off))
            for h in range(2):
                sp.wait_ge(stored[h], 16 * (HEADS + 2 * KT))
            with sp.Fori(0, KT // 2) as i:
                for b in range(2):
                    sp.wait_ge(wL_rdy, 2 * i + (PA0 + b - 1))
                    load(b, k.w_proj_pool[:, bass.ds((2 * i + b) * P, P)].rearrange("(a p) n -> p a n", p=P))
                    for h in range(2):
                        sp.wait_ge(ev_dve, 4 * i + (MMM + 2 * b + h - 1))
                        sp.dma_start(th[:, h, :], k.thp_d[bass.ds(2 * i + b, 1), :, h * HALF:(h + 1) * HALF]
                                     .rearrange("a p n -> p (a n)")).then_inc(thp_in[h], 16)

        @block.gpsimd
        def _(pool):
            def split(slot, n):
                pool.wait_ge(w_in[slot], (n - slot) * 8 + 16)
                if n >= 2:
                    pool.wait_ge(used, n - 1)
                nc.gpsimd.tensor_copy(wH[:, slot, :], wst[:, slot, :]).then_inc(wH_rdy, 1)
                pool.wait_ge(wH_rdy, n + 1)
                nc.gpsimd.tensor_tensor(wL[:, slot, :], wst[:, slot, :], wH[:, slot, :].bitcast(F32),
                                        ALU.subtract).then_inc(wL_rdy, 1)

            for n in range(2):
                split(n, n)
            nc.gpsimd.memset(up[:, :, 0:PAD], 0.0)
            nc.gpsimd.memset(up[:, :, PAD + SEQ:UW], 0.0).then_inc(pads, 1)
            for n in range(2, UNITS):
                split(n % 2, n)

        @block.scalar
        def _(act):
            for g in range(GROUPS):
                for q in range(G_PER):
                    for h in range(2):
                        m = GM + G_USES * g + 2 * q + h
                        act.wait_ge((half_ps, used)[h], (KT + (G_PER + 3) * g, G0 + (G_PER + 1) * g)[h] + q + 1)
                        if g or q:
                            act.wait_ge(ev_dve, m - 1 if q else m - 5)
                        nc.scalar.activation(th[:, h, :], bank[m % 4][:], ACT.Tanh, scale=0.5).then_inc(th_rdy, 1)
                        act.wait_ge(ev_dve, m + 1)
                        act.dma_start(k.sg_d[G_PER * g + q, :, h * HALF:(h + 1) * HALF], ob[:, h, :]
                                      ).then_inc(stored[h], 16)
                    if q in (1, 2):
                        j = 2 * g + q - 1
                        act.wait_ge(d_rdy, j + 1)
                        if g:
                            act.wait_ge(used, G0 + (G_PER + 1) * g)
                        nc.scalar.activation(dH[:, q - 1, :], (pA if g % 2 else pB)[:, 0:SEQ], ACT.Copy
                                             ).then_inc(dH_rdy, 1)
            with act.Fori(0, KT // 2) as i:
                for b in range(2):
                    for h in range(2):
                        act.wait_ge((half_ps, used)[h], 2 * i + ((GPH, GP0)[h] + b + 1))
                        act.wait_ge(ev_dve, 4 * i + (GPM + 2 * b + h - 1))
                        nc.scalar.activation(th[:, h, :], bank[2 * b + h][:], ACT.Tanh, scale=0.5).then_inc(th_rdy, 1)
            act.wait_ge(zp_rdy, 2 * KT)
            for seg, (dst, bg) in enumerate(((k.th_d, KT), (k.thp_d, 0))):
                for j in range(KT):
                    for h in range(2):
                        r = seg * 2 * KT + 2 * j + h
                        act.wait_ge((half_ps, used)[h], (GPH, GP0)[h] + (seg + 1) * KT + j + 1)
                        act.wait_ge(stored[h], 16 * (HEADS + seg * KT + j))
                        nc.scalar.activation(ob[:, h, :], bank[r % 4][:], ACT.Tanh, scale=0.5,
                                             bias=k.bgh[:, bg + j:bg + j + 1]).then_inc(ev_act, 1)
                        act.wait_ge(ev_act, r + 1)
                        act.dma_start(dst[j, :, h * HALF:(h + 1) * HALF], ob[:, h, :]).then_inc(stored[h], 16)
            act.wait_ge(used, PA0)
            for kt in range(KT):
                nc.scalar.activation(k.hH[:, kt, :], up[:, kt, PAD:PAD + SEQ], ACT.Copy).then_inc(zpH_rdy, 1)
            with act.Fori(0, KT // 2) as i:
                for b in range(2):
                    for h in range(2):
                        act.wait_ge(ev_dve, 4 * i + (MMM + 2 * b + h + 1))
                        act.dma_start(k.yp_d[bass.ds(2 * i + b, 1), :, h * HALF:(h + 1) * HALF]
                                      .rearrange("a p n -> p (a n)"), ob[:, h, :]).then_inc(stored[h], 16)
            for h in range(2):
                act.wait_ge(stored[h], 16 * (HEADS + 3 * KT))

        @block.vector
        def _(dve):
            dve.wait_ge(pads, 1)
            with dve.Fori(0, KT // 2) as i:
                for b in range(2):
                    for h in range(2):
                        dve.wait_ge((half_ps, used)[h], 2 * i + (b + 1))
                        nc.vector.tensor_copy(up[:, bass.ds(2 * i + b, 1), PAD + h * HALF:PAD + (h + 1) * HALF],
                                              bank[2 * b + h][:].unsqueeze(1)).then_inc(ev_dve, 1)
            steps = 0

            def pool_tile(g, j):
                nonlocal steps
                src = up[:, j, :]
                bufs = [pA, pB]
                lo, hi = 0, UW
                for lvl in range(g + 1):
                    shift = (1, 1, 2, 4)[lvl]
                    right = 0 if lvl == 0 else shift
                    lo, hi = lo + shift, hi - right
                    dst = bufs[lvl % 2]
                    if steps:
                        dve.wait_ge(win, steps)
                    nc.vector.tensor_tensor(dst[:, lo:hi], src[:, lo - shift:hi - shift],
                                            src[:, lo + right:hi + right], ALU.add).then_inc(win, 1)
                    steps += 1
                    src = dst
                cur, oth = bufs[g % 2], bufs[(g + 1) % 2]
                dve.wait_ge(win, steps)
                nc.vector.tensor_tensor(oth[:, 0:SEQ], cur[:, PAD:PAD + SEQ], inv[:], ALU.mult).then_inc(win, 1)
                steps += 1
                dve.wait_ge(win, steps)
                nc.vector.tensor_tensor(oth[:, 0:SEQ], oth[:, 0:SEQ], up[:, j, PAD:PAD + SEQ], ALU.subtract
                                        ).then_inc(d_rdy, 1)
                dve.wait_ge(d_rdy, j + 1)
                return oth

            for g in range(GROUPS):
                for q in range(G_PER):
                    for h in range(2):
                        m = GM + G_USES * g + 2 * q + h
                        gi = G_PER * g + q
                        dve.wait_ge(th_rdy, 2 * gi + h + 1)
                        if gi:
                            dve.wait_ge(stored[h], 16 * gi)
                        nc.vector.scalar_tensor_tensor(out=ob[:, h, :], in0=th[:, h, :], scalar=1.0,
                                                       in1=bank[m % 4][:], op0=ALU.add, op1=ALU.mult
                                                       ).then_inc(ev_dve, 1)
                    if q in (1, 2):
                        j = 2 * g + q - 1
                        dve.wait_ge(dH_rdy, j + 1)
                        nc.vector.tensor_tensor(dL[:, q - 1, :], (pA if g % 2 else pB)[:, 0:SEQ],
                                                dH[:, q - 1, :].bitcast(F32), ALU.subtract).then_inc(dL_rdy, 1)
                        dve.wait_ge(dL_rdy, j + 1)
                    if q < 2:
                        if q == 0:
                            dve.wait_ge(inv_in, 16 * (g + 1))
                        pool_tile(g, 2 * g + q)
                for dt in range(2):
                    for h in range(2):
                        m = GM + G_USES * g + 2 * G_PER + 2 * dt + h
                        dve.wait_ge(*((used, G0 + (G_PER + 1) * (g + 1)) if dt and h else
                                      (half_ps, KT + (G_PER + 3) * g + G_PER + 2 * dt + h + 1)))
                        nc.vector.tensor_scalar(up[:, 2 * g + dt, PAD + h * HALF:PAD + (h + 1) * HALF], bank[m % 4][:],
                                                k.vt[:, R_PS + 2 * g + dt:R_PS + 2 * g + dt + 1], None,
                                                ALU.mult).then_inc(ev_dve, 1)
            for h in range(2):
                dve.wait_ge(stored[h], 16 * HEADS)
            with dve.Fori(0, KT // 2) as i:
                for b in range(2):
                    for h in range(2):
                        a = 2 * b + h
                        dve.wait_ge(th_rdy, 4 * i + (2 * HEADS + a + 1))
                        nc.vector.scalar_tensor_tensor(out=ob[:, h, :], in0=th[:, h, :], scalar=1.0,
                                                       in1=bank[a][:], op0=ALU.add, op1=ALU.mult).then_inc(ev_dve, 1)
                        dve.wait_ge(ev_dve, 4 * i + (GPM + a + 1))
                        t = up[:, bass.ds(2 * i + b, 1), PAD + h * HALF:PAD + (h + 1) * HALF]
                        nc.vector.scalar_tensor_tensor(out=t, in0=t, scalar=0.5, in1=ob[:, h, :].unsqueeze(1),
                                                       op0=ALU.mult, op1=ALU.mult).then_inc(zp_rdy, 1)
            for kt in range(KT):
                dve.wait_ge(zpH_rdy, kt + 1)
                nc.vector.tensor_tensor(k.hL[:, kt, :], up[:, kt, PAD:PAD + SEQ], k.hH[:, kt, :].bitcast(F32),
                                        ALU.subtract).then_inc(zpL_rdy, 1)
            with dve.Fori(0, KT // 2) as i:
                for b in range(2):
                    for h in range(2):
                        a = 2 * b + h
                        dve.wait_ge((half_ps, used)[h], 2 * i + ((GPH, GP0)[h] + 3 * KT + b + 1))
                        dve.wait_ge(thp_in[h], 32 * i + 16 * (b + 1))
                        dve.wait_ge(stored[h], 32 * i + 16 * (HEADS + 2 * KT + b))
                        nc.vector.scalar_tensor_tensor(out=ob[:, h, :], in0=th[:, h, :], scalar=1.0,
                                                       in1=bank[a][:], op0=ALU.add, op1=ALU.mult).then_inc(ev_dve, 1)

        @block.tensor
        def _(pe):
            def unit(slot, n, b0, free=None, free_at=0, tiles=False):
                pe.wait_ge(wL_rdy, n + 1)
                for h in range(2):
                    if free is not None:
                        pe.wait_ge(free, free_at + h)
                    c = slice(h * HALF, (h + 1) * HALF)
                    for kt in range(KT):
                        if tiles and h == 0:
                            pe.wait_ge(zpL_rdy, kt + 1)
                        w = slice(kt * P, (kt + 1) * P)
                        last = mm3(nc, bank[b0 + h][:], wH[:, slot, w], wL[:, slot, w], k.hH[:, kt, c], k.hL[:, kt, c],
                                   kt == 0, kt == KT - 1)
                    last.then_inc((half_ps, used)[h], 1)

            def units(n0, free, free_at, first=0):
                with pe.Fori(first, KT // 2) as i:
                    for b in range(2):
                        unit(b, 2 * i + (n0 + b), 2 * b, free, 4 * i + (free_at + 2 * b))

            for n in range(2):
                unit(n, n, 2 * n)
            units(0, ev_dve, -3, first=1)
            for g in range(GROUPS):
                n, m = G0 + (G_PER + 1) * g, GM + G_USES * g
                with pe.Fori(0, G_PER // 2) as i:
                    for b in range(2):
                        unit((n + b) % 2, 2 * i + (n + b), 2 * b, ev_dve, 4 * i + (m + 2 * b - 3))
                n, m = n + G_PER, m + 2 * G_PER
                pe.wait_ge(wL_rdy, n + 1)
                pe.wait_ge(dL_rdy, 2 * g + 2)
                for dt in range(2):
                    for h in range(2):
                        pe.wait_ge(ev_dve, m + 2 * dt + h - 3)
                        for kt in range(2):
                            w = slice(kt * 2 * P + dt * P, kt * 2 * P + (dt + 1) * P)
                            c = slice(h * HALF, (h + 1) * HALF)
                            last = mm3(nc, bank[2 * dt + h][:], wH[:, n % 2, w], wL[:, n % 2, w], dH[:, kt, c],
                                       dL[:, kt, c], kt == 0, kt == 1)
                        last.then_inc(used if dt and h else half_ps, 1)
            units(GP0, ev_dve, GPM - 3)
            pe.wait_ge(ev_dve, MMM)
            for b in range(2):
                unit(b, MM0 + b, 2 * b)
            units(MM0, ev_act, -3, first=1)
            units(MP0, ev_act, 2 * KT - 3)
            pe.wait_ge(ev_act, 4 * KT)
            for b in range(2):
                unit(b, PA0 + b, 2 * b, ev_dve, MMM + 2 * b - 3, tiles=(b == 0))
            units(PA0, ev_dve, MMM - 3, first=1)


QCHUNKS = ((0, 512), (512, 1024), (1024, KEYS))
QKT = ((0, 1, 2), (3, 4, 5), (6, 7), (8, 9))
M_PRO = 4


def unit_products(j, kind):
    y = kind != "first" and j < 2
    prep = j % 2 == 0 and not (kind == "last" and j == 2)
    prev = not (kind == "first" and j == 0)
    rope = j == 0 or (j == 3 and kind != "last")
    qn = not (kind == "last" and j == 3)
    q0 = ["rope"] * (rope and j == 0) + ["turn"] * prep + ["y0", "y1"] * y
    q1 = ["q"] * qn + ["absorb"] * prep + ["y2", "y3"] * y
    q2 = ["rope"] * (rope and j == 3) + ["y4", "y5"] * y
    q3 = ["y6", "y7"] * y + ["R", "o"] * prev
    return [q0, q1, q2, q3]


def body_size(kind):
    return sum(len(q) for j in range(4) for q in unit_products(j, kind))


def product_index(i, j, name, kind):
    off = 0
    for jj in range(4):
        for q in unit_products(jj, kind):
            for n in q:
                if jj == j and n == name:
                    first = M_PRO + body_size("first")
                    if kind == "first":
                        return M_PRO + off
                    if kind == "last":
                        return first + (PAIRS - 2) * body_size("mid") + off
                    return i * body_size("mid") + (first - body_size("mid") + off)
                off += 1
    raise KeyError(name)


def product_bank(j, name, kind):
    return (product_index(1, j, name, kind) if kind == "mid" else product_index(0, j, name, kind)) % 2


def stage_attention(nc, k):
    assert body_size("mid") % 2 == 0
    TAIL0 = M_PRO + body_size("first") + (PAIRS - 2) * body_size("mid") + body_size("last")
    UNITS = 4 * PAIRS

    with ExitStack() as ctx:
        def sb(name, shape, dt=F32):
            return ctx.enter_context(nc.sbuf_tensor(name, shape, dt))

        def sem(name):
            return ctx.enter_context(nc.semaphore(name))

        E = sb("E", [P, 2, QT, KEYS])
        ptH = sb("ptH", [P, 2, HALF], F32R)
        ptL = sb("ptL", [P, 2, HALF], F32R)
        qpH = sb("qpH", [P, 2, HALF], F32R)
        qpL = sb("qpL", [P, 2, HALF], F32R)
        q2 = [sb("q2a", [P, SEQ], F32R), sb("q2b", [P, SEQ], F32R)]
        cs = sb("cs", [P, 2, HALF])
        wp_st = sb("wp_st", [P, D])
        wpH = sb("wpH", [P, 2, D], F32R)
        wpL = sb("wpL", [P, 2, D], F32R)
        zH = sb("zH", [P, 2, 2, HALF], F32R)
        zL = sb("zL", [P, 2, 2, HALF], F32R)
        wq_st = sb("wq_st", [P, 2, QLT, NOPE + ROPE])
        wkv_st = sb("wkv_st", [P, 2, NOPE + VD])
        wcH = sb("wcH", [P, 2, QL], F32R)
        wcL = sb("wcL", [P, 2, QL], F32R)
        wrH = sb("wrH", [P, QLT, 2, ROPE], F32R)
        wrL = sb("wrL", [P, QLT, 2, ROPE], F32R)
        wvH = sb("wvH", [P, 2, VD], F32R)
        wvL = sb("wvL", [P, 2, VD], F32R)
        sw = sb("sw", [P, HALF])
        t1 = sb("t1", [P, HALF])
        sg = sb("sg", [P, HALF])
        opH = sb("opH", [P, HALF], F32R)
        opL = sb("opL", [P, HALF], F32R)
        mx = sb("mx", [P, 2, QT, 2])
        nm = sb("nm", [P, 2, QT])
        sums = sb("sums", [P, 2, QT])
        rinv = sb("rinv", [P, 2, QT])

        ps_s = ctx.enter_context(nc.psum_tensor("ps_s", [P, 3 * 512], F32))
        ps_pt = [ctx.enter_context(nc.psum_tensor(f"ps_pt{b}", [P, HALF], F32)) for b in range(2)]
        ps_o = ctx.enter_context(nc.psum_tensor("ps_o", [P, HALF], F32))
        ps_m = [ctx.enter_context(nc.psum_tensor(f"ps_m{b}", [P, HALF], F32)) for b in range(2)]

        wq_in = [sem("wq_in0"), sem("wq_in1")]
        wp_in = sem("wp_in")
        cs_in = sem("cs_in")
        sg_in = sem("sg_in")
        s_c1 = sem("s_c1")
        s_c2 = sem("s_c2")
        mx_rdy = sem("mx_rdy")
        nm_rdy = sem("nm_rdy")
        e_rdy = sem("e_rdy")
        pt_ps = sem("pt_ps")
        ptH_rdy = sem("ptH_rdy")
        ptL_rdy = sem("ptL_rdy")
        pv = sem("pv")
        opH_rdy = sem("opH_rdy")
        opL_rdy = sem("opL_rdy")
        rinv_rdy = sem("rinv_rdy")
        m_ps = sem("m_ps")
        mH_rdy = sem("mH_rdy")
        m_free = sem("m_free")
        sw_rdy = sem("sw_rdy")
        sn_rdy = sem("sn_rdy")
        tq_rdy = sem("tq_rdy")
        q2H_rdy = sem("q2H_rdy")
        q2_rdy = sem("q2_rdy")
        wrH_rdy = sem("wrH_rdy")
        wrL_rdy = sem("wrL_rdy")
        wvH_rdy = sem("wvH_rdy")
        wvL_rdy = sem("wvL_rdy")
        wpH_rdy = sem("wpH_rdy")
        wpL_rdy = sem("wpL_rdy")
        zH_rdy = sem("zH_rdy")
        z_rdy = sem("z_rdy")

        block = ctx.enter_context(nc.Block())

        def static(v):
            return isinstance(v, int)

        def positive(eng, s, v):
            if not static(v) or v > 0:
                eng.wait_ge(s, v)

        def bodies(eng, body):
            body(0, "first")
            with eng.Fori(1, PAIRS - 1) as i:
                body(i, "mid")
            body(PAIRS - 1, "last")

        def mhi_count(i, kind, j, name):
            n = 0
            for jj in range(4):
                for q in unit_products(jj, kind):
                    for nm_ in q:
                        if nm_ in ("turn", "absorb", "q"):
                            n += 1
                        if jj == j and nm_ == name:
                            per = 8
                            return i * per + (3 + n)
            raise KeyError(name)

        def raw_rope(t):
            return t.rearrange("p k (a b c) -> p b k a c", a=2, b=2)

        def rope_half(t, b):
            return t[:, :, b * RH:(b + 1) * RH].rearrange("p k (a c) -> p k a c", a=2)

        @block.sync
        def _(sp):
            def head_weights(h, slot):
                sp.dma_start(wq_st[:, slot, :, :],
                             k.w_qb[:, bass.ds(h * (NOPE + ROPE), NOPE + ROPE)].rearrange("(a p) n -> p a n", p=P)
                             ).then_inc(wq_in[slot], 16)
                sp.dma_start(wkv_st[:, slot, :], k.w_kvb[:, bass.ds(h * (NOPE + VD), NOPE + VD)]
                             ).then_inc(wq_in[slot], 16)

            def tables(half):
                c = slice(half * HALF, (half + 1) * HALF)
                sp.dma_start(cs[:, 0, :], k.qcos_d[:, c]).then_inc(cs_in, 16)
                sp.dma_start(cs[:, 1, :], k.qsin_d[:, c]).then_inc(cs_in, 16)

            def proj_weights(h):
                sp.dma_start(wp_st[:], k.w_proj_mla[bass.ds(h * VD, VD), :]).then_inc(wp_in, 16)

            def gate_tile(h, half):
                sp.dma_start(sg[:], k.sg_d[bass.ds(h, 1), :, half * HALF:(half + 1) * HALF]
                             .rearrange("a p n -> p (a n)")).then_inc(sg_in, 16)

            head_weights(0, 0)
            head_weights(1, 1)
            tables(0)
            sp.wait_ge(tq_rdy, 1)
            tables(1)

            def body(i, kind):
                for j in range(4):
                    if j == 0:
                        positive(sp, wpL_rdy, 2 * i)
                        proj_weights(2 * i)
                        if kind != "first":
                            sp.wait_ge(z_rdy, 4 * i - 1)
                            gate_tile(2 * i - 1, 1)
                        if kind != "last":
                            sp.wait_ge(wvL_rdy, 2 * i + 1)
                            head_weights(2 * i + 2, 0)
                    elif j == 1:
                        positive(sp, z_rdy, 4 * i)
                        gate_tile(2 * i, 0)
                        if kind != "last":
                            sp.wait_ge(tq_rdy, 2 * i + 2)
                            tables(0)
                    elif j == 2:
                        sp.wait_ge(z_rdy, 4 * i + 1)
                        gate_tile(2 * i, 1)
                        if kind != "last":
                            sp.wait_ge(wvL_rdy, 2 * i + 2)
                            head_weights(2 * i + 3, 1)
                    else:
                        sp.wait_ge(wpL_rdy, 2 * i + 1)
                        proj_weights(2 * i + 1)
                        sp.wait_ge(z_rdy, 4 * i + 2)
                        gate_tile(2 * i + 1, 0)
                        if kind != "last":
                            sp.wait_ge(tq_rdy, 2 * i + 3)
                            tables(1)

            bodies(sp, body)
            sp.wait_ge(z_rdy, UNITS - 1)
            gate_tile(HEADS - 1, 1)

        @block.gpsimd
        def _(pool):
            def lo(out, x, hi):
                return nc.gpsimd.tensor_tensor(out, x, hi.bitcast(F32), ALU.subtract)

            def wr_lo(h, slot):
                pool.wait_ge(wrH_rdy, h + 1)
                for b in range(2):
                    last = lo(rope_half(wrL[:, :, slot, :], b), raw_rope(wq_st[:, slot, :, NOPE:])[:, b],
                              rope_half(wrH[:, :, slot, :], b))
                last.then_inc(wrL_rdy, 1)

            def wv_lo(h, slot):
                pool.wait_ge(wvH_rdy, h + 1)
                lo(wvL[:, slot, :], wkv_st[:, slot, NOPE:], wvH[:, slot, :]).then_inc(wvL_rdy, 1)

            def wp_lo(h, slot):
                pool.wait_ge(wpH_rdy, h + 1)
                lo(wpL[:, slot, :], wp_st[:], wpH[:, slot, :]).then_inc(wpL_rdy, 1)

            def rotate(r, at):
                pool.wait_ge(cs_in, 32 * r + 32)
                pool.wait_ge(sw_rdy, r + 1)
                nc.gpsimd.tensor_tensor(sw[:], sw[:], cs[:, 1, :], ALU.mult).then_inc(sn_rdy, 1)
                pool.wait_ge(m_free, at)
                pool.wait_ge(sn_rdy, r + 1)
                nc.gpsimd.tensor_tensor(t1[:], t1[:], sw[:], ALU.add).then_inc(tq_rdy, 1)

            def z_lo(v, hp, half):
                pool.wait_ge(zH_rdy, v + 1)
                lo(zL[:, hp, half, :], sg[:], zH[:, hp, half, :]).then_inc(z_rdy, 1)

            wr_lo(0, 0)
            wr_lo(1, 1)
            wv_lo(0, 0)
            rotate(0, M_PRO)

            def body(i, kind):
                for j in range(4):
                    if j == 0:
                        if kind != "first":
                            z_lo(4 * i - 2, 1, 0)
                        rotate(2 * i + 1, product_index(i, 0, "rope", kind) + 1)
                    elif j == 1:
                        if kind != "last":
                            wr_lo(2 * i + 2, 0)
                        wv_lo(2 * i + 1, 1)
                        if kind != "first":
                            z_lo(4 * i - 1, 1, 1)
                    elif j == 2:
                        z_lo(4 * i, 0, 0)
                        wp_lo(2 * i, 0)
                    else:
                        if kind != "last":
                            wr_lo(2 * i + 3, 1)
                            wv_lo(2 * i + 2, 0)
                        z_lo(4 * i + 1, 0, 1)
                        wp_lo(2 * i + 1, 1)
                        if kind != "last":
                            rotate(2 * i + 2, product_index(i, 3, "rope", kind) + 1)

            bodies(pool, body)
            z_lo(UNITS - 2, 1, 0)
            z_lo(UNITS - 1, 1, 1)

        @block.scalar
        def _(act):
            def copy(out, x):
                return nc.scalar.activation(out, x, ACT.Copy)

            def wr_hi(h, slot):
                act.wait_ge(wq_in[slot], (h - slot) * 16 + 32)
                for b in range(2):
                    last = copy(rope_half(wrH[:, :, slot, :], b), raw_rope(wq_st[:, slot, :, NOPE:])[:, b])
                last.then_inc(wrH_rdy, 1)

            def wv_hi(h, slot):
                copy(wvH[:, slot, :], wkv_st[:, slot, NOPE:]).then_inc(wvH_rdy, 1)

            def wp_hi(h, slot):
                act.wait_ge(wp_in, h * 16 + 16)
                copy(wpH[:, slot, :], wp_st[:]).then_inc(wpH_rdy, 1)

            def small_hi(name, at, b, half=0, slot=0, r=None):
                if name in ("turn", "absorb", "q", "rope"):
                    act.wait_ge(m_ps, at + 1)
                if name == "turn":
                    copy(opH[:, 0:3 * P], ps_m[b][:, 0:3 * P]).then_inc(mH_rdy, 1)
                elif name == "absorb":
                    copy(wcH[:, slot, :], ps_m[b][:, 0:QL]).then_inc(mH_rdy, 1)
                elif name == "q":
                    copy(qpH[:, half, :], ps_m[b][:]).then_inc(mH_rdy, 1)
                elif name == "rope":
                    for q in range(4):
                        o = q ^ 1
                        last = copy(sw[q * RH:(q + 1) * RH, :], ps_m[b][o * RH:(o + 1) * RH, :])
                    last.then_inc(sw_rdy, 1)

            def rope_hi(r, half):
                act.wait_ge(tq_rdy, r + 1)
                c = slice(half * HALF, (half + 1) * HALF)
                copy(q2[0][0:ROPE, c], t1[0:ROPE, :])
                copy(q2[1][ROPE:P, c], t1[ROPE:P, :]).then_inc(q2H_rdy, 1)

            def z_hi(v, hp, half, at):
                act.wait_ge(m_free, at)
                copy(zH[:, hp, half, :], sg[:]).then_inc(zH_rdy, 1)

            def exponent(u, j, qt):
                act.wait_ge(nm_rdy, 4 * u + (qt + 1))
                if qt == 0:
                    positive(act, pt_ps, 10 * (u - 1))
                nc.scalar.activation(E[:, j % 2, qt, :], ps_s[:, 0:KEYS], ACT.Exp, bias=nm[:, j % 2, qt:qt + 1],
                                     accum_out=sums[:, j % 2, qt:qt + 1]).then_inc(e_rdy, 1)

            def turned_hi(v, kt):
                act.wait_ge(pt_ps, NKT * v + (kt + 1))
                positive(act, pv, NKT * v + (kt - 1))
                copy(ptH[:, kt % 2, :], ps_pt[kt % 2][:]).then_inc(ptH_rdy, 1)

            def latent_hi(v):
                act.wait_ge(pv, NKT * (v + 1))
                copy(opH[:], ps_o[:]).then_inc(opH_rdy, 1)

            wr_hi(0, 0)
            wr_hi(1, 1)
            wv_hi(0, 0)
            small_hi("turn", 0, 0)
            small_hi("absorb", 1, 1)
            small_hi("q", 2, 0)
            small_hi("rope", 3, 1)
            rope_hi(0, 0)

            def body(i, kind):
                for j in range(4):
                    u = 4 * i + j
                    v = u - 1
                    prev = not (kind == "first" and j == 0)

                    def at(name, jj=None):
                        return product_index(i, j if jj is None else jj, name, kind)

                    if j == 1:
                        if kind != "last":
                            act.wait_ge(m_ps, at("rope", 0) + 1)
                            wr_hi(2 * i + 2, 0)
                        if kind != "first":
                            act.wait_ge(m_ps, at("o", 0) + 1)
                        wv_hi(2 * i + 1, 1)
                    if j == 3 and kind != "last":
                        wr_hi(2 * i + 3, 1)
                        act.wait_ge(m_ps, at("o", 2) + 1)
                        wv_hi(2 * i + 2, 0)
                    for qt in range(QT):
                        if prev:
                            turned_hi(v, QKT[qt][0])
                        exponent(u, j, qt)
                        if qt == 0 and not (kind == "first" and j < 2):
                            free = at("o", j - 1) + 1 if j else at(unit_products(0, kind)[0][0])
                            z_hi(u - 2, ((j - 2) % 4) // 2, j % 2, free)
                        if prev:
                            for kt in QKT[qt][1:]:
                                turned_hi(v, kt)
                        if qt == 1:
                            if j == 0:
                                rope_hi(2 * i + 1, 1)
                            if j == 2 or j == 3:
                                if j == 2 and kind != "first":
                                    act.wait_ge(m_ps, at("y7", 1) + 1)
                                wp_hi(2 * i + j - 2, j - 2)
                        for name in unit_products(j, kind)[qt]:
                            small_hi(name, at(name), product_bank(j, name, kind), half=(j + 1) % 2,
                                     slot=(j // 2 + 1) % 2)
                        if qt == 3 and j == 3 and kind != "last":
                            rope_hi(2 * i + 2, 0)
                    if prev:
                        latent_hi(v)

            bodies(act, body)
            v = UNITS - 1
            turned_hi(v, 0)
            z_hi(UNITS - 2, 1, 0, product_index(0, 3, "o", "last") + 1)
            for kt in range(1, NKT):
                turned_hi(v, kt)
            latent_hi(v)
            z_hi(v, 1, 1, TAIL0 + KT + 2)

        @block.vector
        def _(dve):
            def lo(out, x, hi):
                return nc.vector.tensor_tensor(out, x, hi.bitcast(F32), ALU.subtract)

            def small(name, at, b, i=0, j=0, half=0, slot=0, hi=None, v=None, y_half=None):
                ps = ps_m[b]
                if hi is not None:
                    dve.wait_ge(mH_rdy, hi)
                if name == "turn":
                    lo(opL[:, 0:3 * P], ps[:, 0:3 * P], opH[:, 0:3 * P]).then_inc(m_free, 1)
                elif name == "absorb":
                    lo(wcL[:, slot, :], ps[:, 0:QL], wcH[:, slot, :]).then_inc(m_free, 1)
                elif name == "q":
                    lo(qpL[:, half, :], ps[:], qpH[:, half, :]).then_inc(m_free, 1)
                elif name == "R":
                    dve.wait_ge(m_ps, at + 1)
                    dve.wait_ge(sg_in, 16 * (v + 1))
                    nc.vector.tensor_tensor(sg[:], sg[:], ps[:], ALU.mult).then_inc(m_free, 1)
                elif name == "o":
                    dve.wait_ge(m_ps, at + 1)
                    dve.wait_ge(m_free, at)
                    nc.vector.scalar_tensor_tensor(out=sg[:], in0=ps[:], scalar=0.5, in1=sg[:], op0=ALU.mult,
                                                   op1=ALU.mult).then_inc(m_free, 1)
                elif name[0] == "y":
                    t = k.yacc[:, int(name[1]), y_half * HALF:(y_half + 1) * HALF]
                    dve.wait_ge(m_ps, at + 1)
                    nc.vector.tensor_tensor(t, t, ps[:], ALU.add).then_inc(m_free, 1)

            def rope(r, at, b):
                dve.wait_ge(sw_rdy, r + 1)
                dve.wait_ge(cs_in, 32 * r + 32)
                nc.vector.tensor_tensor(t1[:], ps_m[b][:], cs[:, 0, :], ALU.mult).then_inc(m_free, 1)

            def rope_lo(r, half):
                dve.wait_ge(q2H_rdy, r + 1)
                c = slice(half * HALF, (half + 1) * HALF)
                lo(q2[0][ROPE:P, c], t1[0:ROPE, :], q2[0][0:ROPE, c])
                lo(q2[1][0:ROPE, c], t1[ROPE:P, :], q2[1][ROPE:P, c]).then_inc(q2_rdy, 1)

            def turned_lo(v, kt):
                dve.wait_ge(ptH_rdy, NKT * v + (kt + 1))
                lo(ptL[:, kt % 2, :], ps_pt[kt % 2][:], ptH[:, kt % 2, :]).then_inc(ptL_rdy, 1)

            def maximum(u, j, qt):
                n = 4 * u + qt
                dve.wait_ge(s_c1, n + 1)
                nc.vector.tensor_reduce(mx[:, j % 2, qt, 0:1], ps_s[:, 0:QCHUNKS[1][1]], AX_X, ALU.max)
                dve.wait_ge(s_c2, n + 1)
                nc.vector.tensor_reduce(mx[:, j % 2, qt, 1:2], ps_s[:, QCHUNKS[1][1]:KEYS], AX_X, ALU.max
                                        ).then_inc(mx_rdy, 1)
                dve.wait_ge(mx_rdy, n + 1)
                nc.vector.tensor_reduce(nm[:, j % 2, qt:qt + 1], mx[:, j % 2, qt, :], AX_X, ALU.max, negate=True
                                        ).then_inc(nm_rdy, 1)

            def inverse_sums(v, jv):
                dve.wait_ge(e_rdy, 4 * (v + 1))
                nc.vector.reciprocal(rinv[:, jv % 2, :], sums[:, jv % 2, :]).then_inc(rinv_rdy, 1)

            def latent_lo(v):
                dve.wait_ge(opH_rdy, v + 1)
                lo(opL[:], ps_o[:], opH[:]).then_inc(opL_rdy, 1)

            nc.vector.memset(k.yacc[:], 0.0)
            small("turn", 0, 0, hi=1)
            small("absorb", 1, 1, hi=2)
            small("q", 2, 0, hi=3)
            rope(0, 3, 1)
            rope_lo(0, 0)

            def body(i, kind):
                for j in range(4):
                    u = 4 * i + j
                    v = u - 1
                    prev = not (kind == "first" and j == 0)
                    if prev:
                        inverse_sums(v, (j - 1) % 4)
                    for qt in range(QT):
                        if prev:
                            turned_lo(v, QKT[qt][0])
                        maximum(u, j, qt)
                        if prev:
                            for kt in QKT[qt][1:]:
                                turned_lo(v, kt)
                        if qt == 1 and j == 0:
                            rope_lo(2 * i + 1, 1)
                        for name in unit_products(j, kind)[qt]:
                            at = product_index(i, j, name, kind)
                            b = product_bank(j, name, kind)
                            if name == "rope":
                                rope(2 * i + (1 if j == 0 else 2), at, b)
                                continue
                            if name == "R":
                                latent_lo(v)
                            hi = mhi_count(i, kind, j, name) if name in ("turn", "absorb", "q") else None
                            small(name, at, b, half=(j + 1) % 2, slot=(j // 2 + 1) % 2, hi=hi, v=v, y_half=j)
                        if qt == 3 and j == 3 and kind != "last":
                            rope_lo(2 * i + 2, 0)

            bodies(dve, body)
            v = UNITS - 1
            inverse_sums(v, 3)
            for kt in range(NKT):
                turned_lo(v, kt)
                if 1 <= kt <= KT:
                    small(f"y{kt - 1}", TAIL0 + kt - 1, (TAIL0 + kt - 1) % 2, y_half=0)
            latent_lo(v)
            small("R", TAIL0 + KT, (TAIL0 + KT) % 2, v=v)
            small("o", TAIL0 + KT + 1, (TAIL0 + KT + 1) % 2, v=v)
            for ft in range(KT):
                at = TAIL0 + KT + 2 + ft
                small(f"y{ft}", at, at % 2, y_half=1)

        @block.tensor
        def _(pe):
            def small(name, at, b, half=0, slot=0, v=None, jv=None, pair=None, y_half=None, r=None, first=False):
                if not (static(at) and at < 2):
                    pe.wait_ge(m_free, at - 1)
                ps = ps_m[b]
                if name == "turn":
                    for kt in range(QLT):
                        nc.tensor.transpose(ps[:, kt * P:(kt + 1) * P], wq_st[:, slot, kt, 0:NOPE], k.ident[:])
                    last = nc.tensor.transpose(ps[:, 2 * P:3 * P], wkv_st[:, slot, 0:NOPE], k.ident[:])
                elif name == "absorb":
                    for kt in range(QLT):
                        w = slice(kt * P, (kt + 1) * P)
                        last = mm3(nc, ps[:, w], opH[:, w], opL[:, w], opH[:, 2 * P:3 * P], opL[:, 2 * P:3 * P],
                                   True, True)
                elif name == "q":
                    for kt in range(QLT):
                        w = slice(kt * P, (kt + 1) * P)
                        c = slice(half * HALF, (half + 1) * HALF)
                        last = mm3(nc, ps[:], wcH[:, slot, w], wcL[:, slot, w], k.qnH[:, kt, c], k.qnL[:, kt, c],
                                   kt == 0, kt == QLT - 1)
                elif name == "rope":
                    for kt in range(QLT):
                        c = slice(half * HALF, (half + 1) * HALF)
                        last = mm3(nc, ps[:], wrH[:, kt, :, :].rearrange("p a b -> p (a b)"),
                                   wrL[:, kt, :, :].rearrange("p a b -> p (a b)"), k.qnH[:, kt, c], k.qnL[:, kt, c],
                                   kt == 0, kt == QLT - 1)
                elif name == "R":
                    pe.wait_ge(rinv_rdy, v + 1)
                    for t in range(QT):
                        last = nc.tensor.transpose(ps[:, t * P:(t + 1) * P],
                                                   rinv[:, jv % 2, t:t + 1].to_broadcast([P, P]), k.ident[:])
                elif name == "o":
                    pe.wait_ge(opL_rdy, v + 1)
                    last = mm3(nc, ps[:], wvH[:, slot, :], wvL[:, slot, :], opH[:], opL[:], True, True)
                else:
                    w = slice(int(name[1]) * P, (int(name[1]) + 1) * P)
                    for hp in range(2):
                        last = mm3(nc, ps[:], wpH[:, hp, w], wpL[:, hp, w], zH[:, hp, y_half, :], zL[:, hp, y_half, :],
                                   hp == 0, hp == 1)
                last.then_inc(m_ps, 1)

            def scores(j, qt, c):
                half, hp = j % 2, j // 2
                lo_, hi_ = QCHUNKS[c]
                t = slice(qt * P, (qt + 1) * P)
                t2 = slice(half * HALF + qt * P, half * HALF + (qt + 1) * P)
                kc = slice(lo_, hi_)
                out = ps_s[:, kc]
                nc.tensor.matmul(out, qpH[:, half, t], k.cH[:, kc], start=True, stop=False)
                nc.tensor.matmul(out, qpH[:, half, t], k.cL[:, kc], start=False, stop=False)
                nc.tensor.matmul(out, qpL[:, half, t], k.cH[:, kc], start=False, stop=False)
                nc.tensor.matmul(out, q2[hp][:, t2], k.k2H[:, kc], start=False, stop=False)
                return nc.tensor.matmul(out, q2[hp][:, t2], k.k2L[:, kc], start=False, stop=True)

            def turn_weights(v, jv, kt):
                if kt == 0:
                    pe.wait_ge(e_rdy, 4 * (v + 1))
                positive(pe, ptL_rdy, NKT * v + (kt - 1))
                for t in range(QT):
                    last = nc.tensor.transpose(ps_pt[kt % 2][:, t * P:(t + 1) * P],
                                               E[:, jv % 2, t, kt * P:(kt + 1) * P], k.ident[:])
                last.then_inc(pt_ps, 1)

            def values(v, kt):
                pe.wait_ge(ptL_rdy, NKT * v + (kt + 1))
                if kt == 0:
                    positive(pe, opL_rdy, v)
                mm3(nc, ps_o[:], k.ctokH[:, kt, :], k.ctokL[:, kt, :], ptH[:, kt % 2, :], ptL[:, kt % 2, :],
                    kt == 0, kt == NKT - 1).then_inc(pv, 1)

            pe.wait_ge(wq_in[0], 32)
            small("turn", 0, 0, slot=0)
            pe.wait_ge(m_free, 1)
            small("absorb", 1, 1)
            pe.wait_ge(m_free, 2)
            small("q", 2, 0, half=0, slot=0)
            pe.wait_ge(wrL_rdy, 2)
            small("rope", 3, 1, half=0)

            def body(i, kind):
                for j in range(4):
                    u = 4 * i + j
                    v = u - 1
                    prev = not (kind == "first" and j == 0)

                    def at(name, jj=None):
                        return product_index(i, j if jj is None else jj, name, kind)

                    def filler(name):
                        a, b = at(name), product_bank(j, name, kind)
                        if name == "turn":
                            slot = (j // 2 + 1) % 2
                            pe.wait_ge(wq_in[slot], 32 * i + (32 if j == 0 else 64))
                            small(name, a, b, slot=slot)
                        elif name == "absorb":
                            pe.wait_ge(m_free, at("turn") + 1)
                            small(name, a, b)
                        elif name == "q":
                            if j % 2:
                                pe.wait_ge(m_free, at("absorb", j - 1) + 1)
                            small(name, a, b, half=(j + 1) % 2, slot=((j + 1) // 2) % 2)
                        elif name == "rope":
                            pe.wait_ge(wrL_rdy, 2 * i + (2 if j == 0 else 4))
                            small(name, a, b, half=1 if j == 0 else 0)
                        elif name == "o":
                            hv = ((j - 1) % 4) // 2
                            pe.wait_ge(wvL_rdy, 2 * i + (hv + 1 if j else 0))
                            small(name, a, b, slot=hv, v=v)
                        elif name == "R":
                            small(name, a, b, v=v, jv=(j - 1) % 4)
                        else:
                            if name == "y0":
                                pe.wait_ge(wpL_rdy, 2 * i)
                                pe.wait_ge(z_rdy, 4 * i - 1 + j)
                            small(name, a, b, y_half=j)

                    for qt in range(QT):
                        n = 4 * u + qt
                        positive(pe, e_rdy, n)
                        if qt == 0:
                            pe.wait_ge(m_free, (product_index(i, j - 1, "q", kind) + 1) if j else
                                       (3 if kind == "first" else at(unit_products(0, kind)[0][0]) - 3))
                            if j < 2:
                                pe.wait_ge(q2_rdy, 2 * i + (j + 1))
                        scores(j, qt, 0)
                        if prev:
                            turn_weights(v, (j - 1) % 4, QKT[qt][0])
                        scores(j, qt, 1).then_inc(s_c1, 1)
                        if prev and qt:
                            values(v, QKT[qt][0] - 1)
                        scores(j, qt, 2).then_inc(s_c2, 1)
                        names = list(unit_products(j, kind)[qt])
                        rest = QKT[qt][1:] if prev else ()
                        for kt in rest:
                            turn_weights(v, (j - 1) % 4, kt)
                            if names and names[0] not in ("R", "o"):
                                pass
                            values(v, kt - 1)
                        if prev and qt == QT - 1:
                            values(v, NKT - 1)
                        for name in names:
                            filler(name)

            bodies(pe, body)
            v = UNITS - 1
            pe.wait_ge(wpL_rdy, 2 * PAIRS)
            for kt in range(NKT):
                turn_weights(v, 3, kt)
                if kt:
                    values(v, kt - 1)
                    if kt == 1:
                        pe.wait_ge(z_rdy, UNITS - 1)
                    if kt <= KT:
                        at = TAIL0 + kt - 1
                        small(f"y{kt - 1}", at, at % 2, y_half=0)
            values(v, NKT - 1)
            small("R", TAIL0 + KT, (TAIL0 + KT) % 2, v=v, jv=3)
            small("o", TAIL0 + KT + 1, (TAIL0 + KT + 1) % 2, slot=1, v=v)
            pe.wait_ge(z_rdy, UNITS)
            for ft in range(KT):
                at = TAIL0 + KT + 2 + ft
                small(f"y{ft}", at, at % 2, y_half=1)


def stage_output(nc, k):
    with ExitStack() as ctx:
        def sb(name, shape, dt=F32):
            return ctx.enter_context(nc.sbuf_tensor(name, shape, dt))

        def sem(name):
            return ctx.enter_context(nc.semaphore(name))

        yH = sb("yH", [P, KT, SEQ], F32R)
        yL = sb("yL", [P, KT, SEQ], F32R)
        woH = sb("woH", [P, KT, D], F32R)
        woL = sb("woL", [P, KT, D], F32R)
        st = sb("wo_st", [P, D])
        br = sb("br", [P, 2, SEQ])
        gate = sb("gate", [P, D])
        fg = sb("fg", [P, D])
        xr = sb("xr", [P, D])
        res = sb("res", [P, D])
        fsq = sb("fsq", [P, XT, 3])
        ps_r = [ctx.enter_context(nc.psum_tensor(f"ps_r{b}", [P, HALF], F32)) for b in range(4)]
        ps_g = [ctx.enter_context(nc.psum_tensor(f"ps_gt{b}", [P, HALF], F32)) for b in range(2)]
        ps_j = ctx.enter_context(nc.psum_tensor("ps_j", [P, 2 * HALF], F32))

        br_in = [sem("br_in0"), sem("br_in1")]
        wo_in = sem("wo_in")
        fg_in = sem("fg_in")
        xr_in = sem("xr_in")
        br_step = sem("br_step")
        y_rdy = sem("y_rdy")
        yH_rdy = sem("yH_rdy")
        yL_rdy = sem("yL_rdy")
        woH_rdy = sem("woH_rdy")
        woL_rdy = sem("woL_rdy")
        gt_ps = sem("gt_ps")
        gt_rdy = sem("gt_rdy")
        r_ps = sem("r_ps")
        r_read = sem("r_read")
        r_step = sem("r_step")
        sq_rdy = sem("sq_rdy")
        rt_rdy = sem("rt_rdy")
        ri_rdy = sem("ri_rdy")
        res_rdy = sem("res_rdy")
        out_done = sem("out_done")

        block = ctx.enter_context(nc.Block())

        @block.sync
        def _(sp):
            for kt in range(KT):
                if kt:
                    sp.wait_ge(y_rdy, kt)
                sp.dma_start(br[:, 0, :], k.th_d[kt]).then_inc(br_in[0], 16)
                sp.dma_start(br[:, 1, :], k.yp_d[kt]).then_inc(br_in[1], 16)
                if kt:
                    sp.wait_ge(woL_rdy, kt)
                sp.dma_start(st[:], k.w_out[kt * P:(kt + 1) * P, :]).then_inc(wo_in, 16)
            sp.dma_start(fg[:], k.final_g.to_broadcast([P, D])).then_inc(fg_in, 16)
            for t in range(XT):
                if t:
                    sp.wait_ge(r_step, 2 * t)
                sp.dma_start(xr[:], k.x[t * P:(t + 1) * P, :]).then_inc(xr_in, 16)
                if t:
                    sp.wait_ge(res_rdy, t)
                    sp.dma_start(k.out[(t - 1) * P:t * P, :], res[:]).then_inc(out_done, 16)
            sp.wait_ge(res_rdy, XT)
            sp.dma_start(k.out[(XT - 1) * P:XT * P, :], res[:]).then_inc(out_done, 16)
            sp.wait_ge(out_done, 16 * XT)

        @block.gpsimd
        def _(pool):
            for kt in range(KT):
                pool.wait_ge(woH_rdy, kt + 1)
                nc.gpsimd.tensor_tensor(woL[:, kt, :], st[:], woH[:, kt, :].bitcast(F32), ALU.subtract
                                        ).then_inc(woL_rdy, 1)

        @block.scalar
        def _(act):
            for kt in range(KT):
                act.wait_ge(wo_in, 16 * (kt + 1))
                nc.scalar.activation(woH[:, kt, :], st[:], ACT.Copy).then_inc(woH_rdy, 1)
                act.wait_ge(y_rdy, kt + 1)
                nc.scalar.activation(yH[:, kt, :], k.yacc[:, kt, :], ACT.Copy).then_inc(yH_rdy, 1)
            for t in range(XT):
                act.wait_ge(r_step, 2 * (t + 1))
                nc.scalar.activation(ps_j[:], res[:], ACT.Square, accum_out=fsq[:, t, 0:1]).then_inc(sq_rdy, 1)
                act.wait_ge(sq_rdy, t + 1)
                nc.scalar.activation(fsq[:, t, 1:2], fsq[:, t, 0:1], ACT.Sqrt, scale=1.0 / D, bias=k.eps[:, 0:1]
                                     ).then_inc(rt_rdy, 1)

        @block.vector
        def _(dve):
            for kt in range(KT):
                t = k.yacc[:, kt, :]
                dve.wait_ge(br_in[0], 16 * (kt + 1))
                nc.vector.scalar_tensor_tensor(out=t, in0=br[:, 0, :], scalar=1.0, in1=t, op0=ALU.add,
                                               op1=ALU.mult).then_inc(br_step, 1)
                dve.wait_ge(br_in[1], 16 * (kt + 1))
                dve.wait_ge(br_step, kt + 1)
                nc.vector.tensor_tensor(t, t, br[:, 1, :], ALU.add).then_inc(y_rdy, 1)
                dve.wait_ge(yH_rdy, kt + 1)
                nc.vector.tensor_tensor(yL[:, kt, :], t, yH[:, kt, :].bitcast(F32), ALU.subtract).then_inc(yL_rdy, 1)
            for h in range(2):
                dve.wait_ge(gt_ps, h + 1)
                nc.vector.tensor_scalar(gate[:, h * HALF:(h + 1) * HALF], ps_g[h][:], 0.5, None, ALU.mult
                                        ).then_inc(gt_rdy, 1)
            dve.wait_ge(gt_rdy, 2)
            for t in range(XT):
                if t:
                    dve.wait_ge(out_done, 16 * t)
                for h in range(2):
                    dve.wait_ge(r_ps, 2 * t + h + 1)
                    c = slice(h * HALF, (h + 1) * HALF)
                    nc.vector.tensor_tensor(res[:, c], ps_r[(2 * t + h) % 4][:], gate[:, c], ALU.mult
                                            ).then_inc(r_read, 1)
                    dve.wait_ge(r_read, 2 * t + h + 1)
                    if h == 0:
                        dve.wait_ge(xr_in, 16 * (t + 1))
                    nc.vector.tensor_tensor(res[:, c], res[:, c], xr[:, c], ALU.add).then_inc(r_step, 1)
                if t == 0:
                    dve.wait_ge(fg_in, 16)
                dve.wait_ge(rt_rdy, t + 1)
                nc.vector.reciprocal(fsq[:, t, 2:3], fsq[:, t, 1:2]).then_inc(ri_rdy, 1)
                dve.wait_ge(ri_rdy, t + 1)
                nc.vector.scalar_tensor_tensor(out=res[:], in0=res[:], scalar=fsq[:, t, 2:3], in1=fg[:],
                                               op0=ALU.mult, op1=ALU.mult).then_inc(res_rdy, 1)

        @block.tensor
        def _(pe):
            for h in range(2):
                for f in range(QT):
                    ft = h * QT + f
                    last = nc.tensor.transpose(ps_g[h][:, f * P:(f + 1) * P],
                                               k.gateT[:, ft:ft + 1].to_broadcast([P, P]), k.ident[:])
                last.then_inc(gt_ps, 1)
            for t in range(XT):
                for h in range(2):
                    n = 2 * t + h
                    if n >= 4:
                        pe.wait_ge(r_read, n - 3)
                    for kt in range(KT):
                        if n == 0:
                            pe.wait_ge(yL_rdy, kt + 1)
                            pe.wait_ge(woL_rdy, kt + 1)
                        ts, c = slice(t * P, (t + 1) * P), slice(h * HALF, (h + 1) * HALF)
                        last = mm3(nc, ps_r[n % 4][:], yH[:, kt, ts], yL[:, kt, ts], woH[:, kt, c], woL[:, kt, c],
                                   kt == 0, kt == KT - 1)
                    last.then_inc(r_ps, 1)


def build_program(nc, k):
    with ExitStack() as ctx:
        def sb(name, shape, dt=F32):
            return ctx.enter_context(nc.sbuf_tensor(name, shape, dt))

        k.ident = sb("ident", [P, P])
        k.vt = sb("vt", [P, R_END])
        k.eps = sb("eps", [P, 1])
        k.qgs = sb("qgs", [P, QLT])
        k.bgh = sb("bgh", [P, 2 * KT])
        k.gateT = sb("gateT", [P, KT])
        with ExitStack() as latents:
            def lat(name, shape, dt=F32R):
                return latents.enter_context(nc.sbuf_tensor(name, shape, dt))

            k.qnH = lat("qnH", [P, QLT, SEQ])
            k.qnL = lat("qnL", [P, QLT, SEQ])
            k.cH = lat("cH", [P, KEYS])
            k.cL = lat("cL", [P, KEYS])
            k.k2H = lat("k2H", [P, KEYS])
            k.k2L = lat("k2L", [P, KEYS])
            k.ctokH = lat("ctokH", [P, NKT, KVL])
            k.ctokL = lat("ctokL", [P, NKT, KVL])
            with ExitStack() as early:
                k.hH = early.enter_context(nc.sbuf_tensor("hH", [P, KT, SEQ], F32R))
                k.hL = early.enter_context(nc.sbuf_tensor("hL", [P, KT, SEQ], F32R))
                stage_tokens(nc, k)
                stage_gates(nc, k)
            k.yacc = ctx.enter_context(nc.sbuf_tensor("yacc", [P, KT, SEQ], F32, side="right"))
            stage_attention(nc, k)
        stage_output(nc, k)


def rope_tables():
    import numpy as np
    half = ROPE // 2
    inv = (1.0 / (np.float32(10000.0) ** (np.arange(0, half, 2, dtype=np.float32) / np.float32(half)))).astype(np.float32)
    t = np.arange(SEQ)
    ang = np.concatenate([(t // 64).astype(np.float32)[:, None] * inv, (t % 64).astype(np.float32)[:, None] * inv], axis=1)
    cos, sin = np.cos(ang).astype(np.float32), np.sin(ang).astype(np.float32)
    q_cos = np.tile(cos.T, (P // RH, 1))
    q_sin = np.concatenate([-sin.T, sin.T] * (P // ROPE), axis=0)
    return cos, sin, np.ascontiguousarray(q_cos), np.ascontiguousarray(q_sin)


def pool_counts():
    import numpy as np
    t = np.arange(SEQ)
    rows = [1.0 / (np.clip(t + w // 2, 0, SEQ) - np.clip(t - w // 2, 0, SEQ)).astype(np.float32) for w in WINDOWS]
    return np.stack(rows).astype(np.float32)


def kernel(x, c, ctx, c_ctx, ada_w, ada_b, norm_g, w_in, b_gate, w_pool, pool_scale, q_norm_g, w_qb,
           kv_norm_g, w_kvb, w_proj_pool, w_proj_mla, w_out, final_g):
    import numpy as np
    import concourse.bacc as bacc
    from concourse.bass_utils import run_bass_kernel_spmd

    nc = bacc.Bacc("TRN2", target_bir_lowering=False, num_devices=1)
    cos, sin, q_cos, q_sin = rope_tables()
    arrays = {
        "x": np.asarray(x).reshape(SEQ, D), "ctx": np.asarray(ctx).reshape(CTX, D),
        "c": np.asarray(c).reshape(KT, P), "c_ctx": np.asarray(c_ctx).reshape(KT, P),
        "ada_w": np.asarray(ada_w)[0], "ada_b": np.asarray(ada_b).reshape(3 * KT, P),
        "norm_g": np.asarray(norm_g).reshape(KT, P), "w_in": np.asarray(w_in)[0],
        "b_gate": np.asarray(b_gate).reshape(2 * KT, P), "w_pool": np.asarray(w_pool)[0],
        "pool_scale": np.asarray(pool_scale).reshape(KT, P), "q_norm_g": np.asarray(q_norm_g).reshape(QLT, P),
        "w_qb": np.asarray(w_qb)[0], "kv_norm_g": np.asarray(kv_norm_g).reshape(1, KVL),
        "w_kvb": np.asarray(w_kvb)[0], "w_proj_pool": np.asarray(w_proj_pool)[0],
        "w_proj_mla": np.asarray(w_proj_mla)[0], "w_out": np.asarray(w_out)[0],
        "final_g": np.asarray(final_g).reshape(1, D),
        "ident_d": np.eye(P, dtype=np.float32), "kcos_d": cos, "ksin_d": sin, "qcos_d": q_cos, "qsin_d": q_sin,
        "pool_inv": pool_counts(),
    }
    arrays = {n: np.ascontiguousarray(a) for n, a in arrays.items()}
    k = Chip()
    for n, a in arrays.items():
        k.__dict__[n] = nc.dram_tensor("in_" + n, a.shape, F32, kind="ExternalInput").ap()
    k.out = nc.dram_tensor("out", (SEQ, D), F32, kind="ExternalOutput").ap()
    k.sg_d = nc.dram_tensor("sg_scratch", (HEADS, P, SEQ), F32, kind="Internal").ap()
    k.yp_d = nc.dram_tensor("yp_scratch", (KT, P, SEQ), F32, kind="Internal").ap()
    k.thp_d = nc.dram_tensor("thp_scratch", (KT, P, SEQ), F32, kind="Internal").ap()
    k.th_d = nc.dram_tensor("th_scratch", (KT, P, SEQ), F32, kind="Internal").ap()
    build_program(nc, k)
    result = run_bass_kernel_spmd(nc, [{"in_" + n: a for n, a in arrays.items()}], core_ids=[0]).results[0]["out"]
    return result.reshape(1, SEQ, D)
```

```python
from contextlib import ExitStack

import concourse.bass as bass
from concourse import mybir

F32 = mybir.dt.float32
F32R = mybir.dt.float32r
BF16 = mybir.dt.bfloat16
ACT = mybir.ActivationFunctionType
ALU = mybir.AluOpType
AX_X = mybir.AxisListType.X

P = 128
D = 1024
KT = D // P
SEQ = 1024
CTX = 256
XT = SEQ // P
CT = CTX // P
KEYS = SEQ + CTX
NKT = KEYS // P
HALF = 512
NHALF = SEQ // HALF
QT = HALF // P
HEADS = 16
PAIRS = HEADS // 2
NOPE = 128
ROPE = 64
RH = ROPE // 2
VD = 128
QL = 256
QLT = QL // P
KVL = 128
LORA = QL + KVL + ROPE
MLA = HEADS * VD
WINDOWS = (2, 4, 8, 16)
GROUPS = len(WINDOWS)
PAD = max(WINDOWS) // 2
UW = SEQ + 2 * PAD
EPS = 1e-6
SCALE = float(NOPE + ROPE) ** -0.5

O_U = 0
O_GP = O_U + D
O_QA = O_GP + D
O_KV = O_QA + QL
O_GM = O_KV + KVL + ROPE
O_MP = O_GM + MLA
O_MM = O_MP + D

R_ADAB, R_NG, R_BG, R_PS, R_QG, R_C, R_CC, R_END = 0, 24, 32, 48, 56, 58, 66, 74


class Chip:
    pass


def mm3(nc, out, ah, al, bh, bl, first, last):
    nc.tensor.matmul(out, ah, bh, start=first, stop=False)
    nc.tensor.matmul(out, ah, bl, start=False, stop=False)
    return nc.tensor.matmul(out, al, bh, start=False, stop=last)


def stage_tokens(nc, k):
    GT = [(0, QT), (QT, QT), (XT, CT)]
    NG = len(GT)
    with ExitStack() as ctx:
        def sb(name, shape, dt=F32):
            return ctx.enter_context(nc.sbuf_tensor(name, shape, dt))

        def sem(name):
            return ctx.enter_context(nc.semaphore(name))

        vecs = sb("vecs", [R_END, P])
        xs = sb("xs", [P, QT, D])
        junk = sb("junk", [P, D], BF16)
        ada = sb("ada", [P, 2, 2 * D])
        wlH = sb("wlH", [P, KT, LORA], F32R)
        wlL = sb("wlL", [P, KT, LORA], F32R)
        hcH = sb("hcH", [P, KT, CTX], F32R)
        hcL = sb("hcL", [P, KT, CTX], F32R)
        htmp = sb("htmp", [P, 2, HALF])
        kcos = sb("kcos", [P, XT, RH])
        ksin = sb("ksin", [P, XT, RH])
        kvg = sb("kvg", [P, KVL])
        condT = sb("condT", [P, 2 * KT])
        cond = sb("cond", [P, KT, 2])
        mod = sb("mod", [P, 2 * KT, 2])
        gain = sb("gain", [P, KT, 2])
        ssq = sb("ssq", [P, XT + CT])
        rst = sb("rst", [P, XT + CT])
        rstd = sb("rstd", [P, XT + CT])
        lms = sb("lms", [P, XT + CT, 2])
        lsd = sb("lsd", [P, XT + CT, 2])
        lrs = sb("lrs", [P, XT + CT, 2])
        qn = sb("qn", [P, 2, QL])
        cn = sb("cn", [P, 2, KVL])
        rp1 = sb("rp1", [P, 2, ROPE])
        rp2 = sb("rp2", [P, 2, ROPE])
        kr = sb("kr", [P, 2, ROPE])
        krH = sb("krH", [P, 2, 2, ROPE], F32R)
        krL = sb("krL", [P, 2, 2, ROPE], F32R)

        def pb(name):
            return ctx.enter_context(nc.psum_tensor(name, [P, 512], F32))

        ps_ada = pb("ps_ada")
        ps_x = [pb("ps_x0"), pb("ps_x1")]
        ps_p = [pb("ps_p0"), pb("ps_p1")]
        ps_t = pb("ps_t")
        ps_u = pb("ps_u")
        ps_v = pb("ps_v")

        vec_in = sem("vec_in")
        tab_in = sem("tab_in")
        ada_in = [sem("ada_in0"), sem("ada_in1")]
        gate_in = [sem("gate_in0"), sem("gate_in1")]
        x_in = [sem(f"x_in{j}") for j in range(QT)]
        wl_in = sem("wl_in")
        vt_ps = sem("vt_ps")
        vt_rdy = sem("vt_rdy")
        th_rdy = sem("th_rdy")
        cond_rdy = sem("cond_rdy")
        ada_used = sem("ada_used")
        gate_used = sem("gate_used")
        mod_rdy = sem("mod_rdy")
        gain_rdy = sem("gain_rdy")
        gate_rdy = sem("gate_rdy")
        ssq_rdy = sem("ssq_rdy")
        rst_rdy = sem("rst_rdy")
        rstd_rdy = sem("rstd_rdy")
        xn_rdy = sem("xn_rdy")
        x_ps = sem("x_ps")
        hH_rdy = sem("hH_rdy")
        ht_rdy = sem("ht_rdy")
        hL_rdy = sem("hL_rdy")
        wlH_rdy = sem("wlH_rdy")
        wlL_rdy = sem("wlL_rdy")
        p_ps = sem("p_ps")
        lms_rdy = sem("lms_rdy")
        lsd_rdy = sem("lsd_rdy")
        lrs_rdy = sem("lrs_rdy")
        rope_step = sem("rope_step")
        lat_rdy = sem("lat_rdy")
        latH_rdy = sem("latH_rdy")
        latL_rdy = sem("latL_rdy")
        t_ps = sem("t_ps")
        tH_rdy = sem("tH_rdy")
        tL_rdy = sem("tL_rdy")

        block = ctx.enter_context(nc.Block())

        def x_tile(t):
            return k.x[t * P:(t + 1) * P, :] if t < XT else k.ctx[(t - XT) * P:(t - XT + 1) * P, :]

        def hslice(g, ft):
            t0, n = GT[g]
            if t0 < XT:
                return k.hH[:, ft, t0 * P:(t0 + n) * P], k.hL[:, ft, t0 * P:(t0 + n) * P], n * P
            return hcH[:, ft, :], hcL[:, ft, :], n * P

        @block.sync
        def _(sp):
            rows = [(k.c, R_C), (k.c_ctx, R_CC), (k.ada_b, R_ADAB), (k.norm_g, R_NG), (k.b_gate, R_BG),
                    (k.pool_scale, R_PS), (k.q_norm_g, R_QG)]
            sp.dma_start(k.ident[:], k.ident_d).then_inc(vec_in, 16)
            for v, r in rows:
                sp.dma_start(vecs[r:r + v.shape[0], :], v).then_inc(vec_in, 16)
            for kt in range(KT):
                if kt >= 2:
                    sp.wait_ge(ada_used, kt - 1)
                sp.dma_start(ada[:, kt % 2, :], k.ada_w[kt * P:(kt + 1) * P, 0:2 * D]).then_inc(ada_in[kt % 2], 16)
                if kt < QT:
                    sp.dma_start(xs[:, kt, :], x_tile(kt)).then_inc(x_in[kt], 16)
            sp.dma_start(kcos[:], k.kcos_d.rearrange("(t p) d -> p t d", p=P)).then_inc(tab_in, 16)
            sp.dma_start(ksin[:], k.ksin_d.rearrange("(t p) d -> p t d", p=P)).then_inc(tab_in, 16)
            sp.dma_start(kvg[:], k.kv_norm_g.to_broadcast([P, KVL])).then_inc(tab_in, 16)
            sp.wait_ge(ada_used, KT)
            sp.dma_start(ada[:].rearrange("p a b -> p (a b)")[:, 0:KT * LORA].rearrange("p (a b) -> p a b", a=KT),
                         k.w_in[:, O_QA:O_QA + LORA].rearrange("(a p) n -> p a n", p=P)).then_inc(wl_in, 16)
            for g in range(1, NG):
                sp.wait_ge(x_ps, KT * g)
                for j in range(GT[g][1]):
                    sp.dma_start(xs[:, j, :], x_tile(GT[g][0] + j)).then_inc(x_in[j], 16)
            sp.wait_ge(wlL_rdy, KT)
            for kp in range(KT // 2):
                if kp >= 2:
                    sp.wait_ge(gate_used, kp - 1)
                sp.dma_start(ada[:, kp % 2, :].rearrange("p (a b) -> p a b", a=2),
                             k.ada_w[2 * kp * P:2 * (kp + 1) * P, 2 * D:3 * D].rearrange("(a p) n -> p a n", p=P)
                             ).then_inc(gate_in[kp % 2], 16)

        @block.scalar
        def _(act):
            act.wait_ge(vt_rdy, 1)
            nc.scalar.activation(condT[:], k.vt[:, R_C:R_END], ACT.Tanh, scale=0.5).then_inc(th_rdy, 1)

            def token_stats(g):
                t0, n = GT[g]
                for j in range(n):
                    act.wait_ge(x_in[j], 16 * (g + 1))
                    if t0 + j > 0:
                        act.wait_ge(ssq_rdy, t0 + j)
                    nc.scalar.activation(junk[:], xs[:, j, :], ACT.Square,
                                         accum_out=ssq[:, t0 + j:t0 + j + 1]).then_inc(ssq_rdy, 1)
                act.wait_ge(ssq_rdy, t0 + n)
                nc.scalar.activation(rst[:, t0:t0 + n], ssq[:, t0:t0 + n], ACT.Sqrt, scale=1.0 / D,
                                     bias=k.eps[:, 0:1]).then_inc(rst_rdy, 1)

            def modulate(g):
                if g == 0:
                    act.wait_ge(gain_rdy, 1)
                for ft in range(KT):
                    act.wait_ge(x_ps, KT * g + ft + 1)
                    hi, _, n = hslice(g, ft)
                    j = int(g == NG - 1)
                    nc.scalar.activation(hi, ps_x[ft % 2][:, 0:n], ACT.Identity, scale=gain[:, ft, j:j + 1],
                                         bias=mod[:, ft, j:j + 1]).then_inc(hH_rdy, 1)

            def w_lora():
                act.wait_ge(wl_in, 16)
                st = ada[:].rearrange("p a b -> p (a b)")
                for kt in range(KT):
                    nc.scalar.activation(wlH[:, kt, :], st[:, kt * LORA:(kt + 1) * LORA], ACT.Copy
                                         ).then_inc(wlH_rdy, 1)

            def latent_stats(t):
                act.wait_ge(p_ps, t + 1)
                ps = ps_p[t % 2]
                n = 2 * t if t < XT else 2 * XT + (t - XT)
                if t < XT:
                    act.wait_ge(lms_rdy, n) if n else None
                    nc.scalar.activation(junk[:, 0:QL], ps[:, 0:QL], ACT.Square, scale=QL ** -0.5,
                                         accum_out=lms[:, t, 0:1]).then_inc(lms_rdy, 1)
                    n += 1
                    c0 = QL
                else:
                    c0 = 0
                act.wait_ge(lms_rdy, n)
                nc.scalar.activation(junk[:, 0:KVL], ps[:, c0:c0 + KVL], ACT.Square, scale=KVL ** -0.5,
                                     accum_out=lms[:, t, 1:2]).then_inc(lms_rdy, 1)
                act.wait_ge(lms_rdy, n + 1)
                a = 0 if t < XT else 1
                nc.scalar.activation(lsd[:, t, a:2], lms[:, t, a:2], ACT.Sqrt, bias=k.eps[:, 0:1]).then_inc(lsd_rdy, 1)

            def latent_hi(t):
                act.wait_ge(lat_rdy, t + 1)
                if t >= 2:
                    act.wait_ge(t_ps, t - 1)
                nc.scalar.activation(k.ctokH[:, t, :], cn[:, t % 2, :], ACT.Copy)
                nc.scalar.activation(krH[:, t % 2, :, :], kr[:, t % 2, :].unsqueeze(1).to_broadcast([P, 2, ROPE]),
                                     ACT.Copy).then_inc(latH_rdy, 1)

            def latent_T_hi(t):
                act.wait_ge(t_ps, t + 1)
                c = slice(t * P, (t + 1) * P)
                if t < XT:
                    for i in range(QLT):
                        nc.scalar.activation(k.qnH[:, i, c], ps_t[:, i * P:(i + 1) * P], ACT.Copy,
                                             scale=k.qgs[:, i:i + 1])
                nc.scalar.activation(k.k2H[:, c], ps_t[:, 3 * P:4 * P], ACT.Copy)
                nc.scalar.activation(k.cH[:, c], ps_t[:, 2 * P:3 * P], ACT.Copy).then_inc(tH_rdy, 1)

            token_stats(0)
            modulate(0)
            w_lora()
            for t in range(XT + CT):
                if t == 2:
                    token_stats(1)
                    modulate(1)
                if t == 6:
                    token_stats(2)
                    modulate(2)
                latent_stats(t)
                if t:
                    latent_T_hi(t - 1)
                latent_hi(t)
            latent_T_hi(XT + CT - 1)

        @block.vector
        def _(dve):
            nc.vector.memset(k.eps[:], EPS)
            dve.wait_ge(vt_ps, 1)
            nc.vector.tensor_copy(k.vt[:, 0:R_END], ps_v[:, 0:R_END]).then_inc(vt_rdy, 1)
            dve.wait_ge(th_rdy, 1)
            nc.vector.scalar_tensor_tensor(out=cond[:].rearrange("p a j -> p j a"),
                                           in0=condT[:].rearrange("p (j a) -> p j a", j=2), scalar=1.0,
                                           in1=k.vt[:, R_C:R_END].rearrange("p (j a) -> p j a", j=2),
                                           op0=ALU.add, op1=ALU.mult).then_inc(cond_rdy, 1)
            nc.vector.tensor_scalar(k.qgs[:], k.vt[:, R_QG:R_QG + QLT], SCALE, None, ALU.mult)
            nc.vector.tensor_scalar(k.bgh[:], k.vt[:, R_BG:R_BG + 2 * KT], 0.5, None, ALU.mult)

            def normalise(g):
                t0, n = GT[g]
                dve.wait_ge(rst_rdy, g + 1)
                nc.vector.reciprocal(rstd[:, t0:t0 + n], rst[:, t0:t0 + n]).then_inc(rstd_rdy, 1)
                dve.wait_ge(rstd_rdy, g + 1)
                for j in range(n):
                    nc.vector.tensor_scalar(xs[:, j, :], xs[:, j, :], rstd[:, t0 + j:t0 + j + 1], None,
                                            ALU.mult).then_inc(xn_rdy, 1)

            def modulate(g):
                for ft in range(KT):
                    i = KT * g + ft
                    dve.wait_ge(x_ps, i + 1)
                    dve.wait_ge(hH_rdy, i + 1)
                    if i >= 2:
                        dve.wait_ge(hL_rdy, i - 1)
                    _, _, n = hslice(g, ft)
                    j = int(g == NG - 1)
                    nc.vector.tensor_scalar(htmp[:, ft % 2, 0:n], ps_x[ft % 2][:, 0:n], gain[:, ft, j:j + 1],
                                            mod[:, ft, j:j + 1], ALU.mult, ALU.add).then_inc(ht_rdy, 1)

            def latents(t):
                s = t % 2
                a = 0 if t < XT else 1
                ps = ps_p[s]
                c0 = QL if t < XT else 0
                dve.wait_ge(lsd_rdy, t + 1)
                nc.vector.reciprocal(lrs[:, t, a:2], lsd[:, t, a:2]).then_inc(lrs_rdy, 1)
                if t >= 2:
                    dve.wait_ge(t_ps, t - 1)
                dve.wait_ge(lrs_rdy, t + 1)
                if t < XT:
                    nc.vector.tensor_scalar(qn[:, s, :], ps[:, 0:QL], lrs[:, t, 0:1], None, ALU.mult)
                if t == 0:
                    dve.wait_ge(tab_in, 48)
                nc.vector.scalar_tensor_tensor(out=cn[:, s, :], in0=ps[:, c0:c0 + KVL], scalar=lrs[:, t, 1:2],
                                               in1=kvg[:], op0=ALU.mult, op1=ALU.mult)
                raw = ps[:, c0 + KVL:c0 + KVL + ROPE].rearrange("p (a b c) -> p b a c", a=2, b=2)

                def half(tile, b):
                    return tile[:, s, b * RH:(b + 1) * RH].rearrange("p (a c) -> p a c", a=2)

                if t < XT:
                    cs = kcos[:, t, :].rearrange("p (a c) -> p a c", a=2)
                    sn = ksin[:, t, :].rearrange("p (a c) -> p a c", a=2)
                    for b in range(2):
                        nc.vector.tensor_tensor(half(rp1, b), raw[:, b], cs, ALU.mult)
                        last = nc.vector.tensor_tensor(half(rp2, b), raw[:, 1 - b], sn, ALU.mult)
                    last.then_inc(rope_step, 1)
                    dve.wait_ge(rope_step, t + 1)
                    nc.vector.tensor_tensor(kr[:, s, 0:RH], rp1[:, s, 0:RH], rp2[:, s, 0:RH], ALU.subtract)
                    nc.vector.tensor_tensor(kr[:, s, RH:ROPE], rp1[:, s, RH:ROPE], rp2[:, s, RH:ROPE],
                                            ALU.add).then_inc(lat_rdy, 1)
                else:
                    nc.vector.tensor_copy(half(kr, 0), raw[:, 0])
                    nc.vector.tensor_copy(half(kr, 1), raw[:, 1]).then_inc(lat_rdy, 1)

            def latents_lo(t):
                s = t % 2
                dve.wait_ge(latH_rdy, t + 1)
                nc.vector.tensor_tensor(k.ctokL[:, t, :], cn[:, s, :], k.ctokH[:, t, :].bitcast(F32), ALU.subtract)
                nc.vector.tensor_tensor(krL[:, s, :, :], kr[:, s, :].unsqueeze(1).to_broadcast([P, 2, ROPE]),
                                        krH[:, s, :, :].bitcast(F32), ALU.subtract).then_inc(latL_rdy, 1)

            def latents_T_lo(t):
                c = slice(t * P, (t + 1) * P)
                dve.wait_ge(tH_rdy, t + 1)
                if t < XT:
                    for i in range(QLT):
                        nc.vector.scalar_tensor_tensor(out=k.qnL[:, i, c], in0=ps_t[:, i * P:(i + 1) * P],
                                                       scalar=k.qgs[:, i:i + 1], in1=k.qnH[:, i, c].bitcast(F32),
                                                       op0=ALU.mult, op1=ALU.subtract)
                nc.vector.tensor_copy(k.k2L[:, c], ps_u[:, 0:P])
                nc.vector.tensor_tensor(k.cL[:, c], ps_t[:, 2 * P:3 * P], k.cH[:, c].bitcast(F32),
                                        ALU.subtract).then_inc(tL_rdy, 1)

            normalise(0)
            dve.wait_ge(ada_used, KT)
            b = k.vt[:, R_ADAB:R_ADAB + 2 * KT].unsqueeze(2).to_broadcast([P, 2 * KT, 2])
            nc.vector.scalar_tensor_tensor(out=mod[:], in0=ps_ada[:, 0:4 * KT].rearrange("p (a j) -> p a j", j=2),
                                           scalar=0.5, in1=b, op0=ALU.mult, op1=ALU.add).then_inc(mod_rdy, 1)
            dve.wait_ge(mod_rdy, 1)
            nc.vector.scalar_tensor_tensor(out=gain[:], in0=mod[:, KT:2 * KT, :], scalar=1.0,
                                           in1=k.vt[:, R_NG:R_NG + KT].unsqueeze(2).to_broadcast([P, KT, 2]),
                                           op0=ALU.add, op1=ALU.mult).then_inc(gain_rdy, 1)
            dve.wait_ge(gain_rdy, 1)
            modulate(0)
            for t in range(XT + CT):
                if t == 2:
                    normalise(1)
                    modulate(1)
                if t == 6:
                    normalise(2)
                    modulate(2)
                latents(t)
                if t:
                    latents_T_lo(t - 1)
                latents_lo(t)
            latents_T_lo(XT + CT - 1)
            dve.wait_ge(gate_used, KT // 2)
            nc.vector.scalar_tensor_tensor(out=k.gateT[:], in0=ps_v[:, 0:KT],
                                           scalar=0.5, in1=k.vt[:, R_ADAB + 2 * KT:R_ADAB + 3 * KT],
                                           op0=ALU.mult, op1=ALU.add).then_inc(gate_rdy, 1)

        @block.gpsimd
        def _(pool):
            def modulated_lo(g):
                for ft in range(KT):
                    i = KT * g + ft
                    pool.wait_ge(ht_rdy, i + 1)
                    hi, lo, n = hslice(g, ft)
                    nc.gpsimd.tensor_tensor(lo, htmp[:, ft % 2, 0:n], hi.bitcast(F32), ALU.subtract
                                            ).then_inc(hL_rdy, 1)

            modulated_lo(0)
            st = ada[:].rearrange("p a b -> p (a b)")
            for kt in range(KT):
                pool.wait_ge(wlH_rdy, kt + 1)
                nc.gpsimd.tensor_tensor(wlL[:, kt, :], st[:, kt * LORA:(kt + 1) * LORA], wlH[:, kt, :].bitcast(F32),
                                        ALU.subtract).then_inc(wlL_rdy, 1)
            modulated_lo(1)
            modulated_lo(2)

        @block.tensor
        def _(pe):
            pe.wait_ge(vec_in, 16 * 8)
            nc.tensor.transpose(ps_v[:, 0:R_END], vecs[:], k.ident[0:R_END, 0:R_END]).then_inc(vt_ps, 1)
            pe.wait_ge(cond_rdy, 1)
            for kt in range(KT):
                pe.wait_ge(ada_in[kt % 2], 16 * (kt // 2 + 1))
                for o in range(2 * KT):
                    last = nc.tensor.matmul(ps_ada[:, 2 * o:2 * o + 2], ada[:, kt % 2, o * P:(o + 1) * P],
                                            cond[:, kt, :], start=(kt == 0 and o == 0), stop=(kt == KT - 1),
                                            skip_group_check=True)
                last.then_inc(ada_used, 1)

            def transposes(g):
                t0, n = GT[g]
                pe.wait_ge(xn_rdy, t0 + n)
                for ft in range(KT):
                    i = KT * g + ft
                    if i >= 2:
                        pe.wait_ge(ht_rdy, i - 1)
                    for j in range(n):
                        last = nc.tensor.transpose(ps_x[ft % 2][:, j * P:(j + 1) * P],
                                                   xs[:, j, ft * P:(ft + 1) * P], k.ident[:])
                    last.then_inc(x_ps, 1)

            def project(t):
                w = LORA if t < XT else LORA - QL
                hi, lo = (k.hH, k.hL) if t < XT else (hcH, hcL)
                c = slice(t * P, (t + 1) * P) if t < XT else slice((t - XT) * P, (t - XT + 1) * P)
                if t >= 2:
                    pe.wait_ge(lat_rdy, t - 1)
                for kt in range(KT):
                    last = mm3(nc, ps_p[t % 2][:, 0:w], hi[:, kt, c], lo[:, kt, c], wlH[:, kt, LORA - w:],
                               wlL[:, kt, LORA - w:], kt == 0, kt == KT - 1)
                last.then_inc(p_ps, 1)

            def turn(t):
                s = t % 2
                pe.wait_ge(latL_rdy, t + 1)
                if t:
                    pe.wait_ge(tL_rdy, t)
                if t < XT:
                    for i in range(QLT):
                        nc.tensor.transpose(ps_t[:, i * P:(i + 1) * P], qn[:, s, i * P:(i + 1) * P], k.ident[:])
                nc.tensor.transpose(ps_t[:, 2 * P:3 * P], cn[:, s, :], k.ident[:])
                nc.tensor.transpose(ps_t[:, 3 * P:4 * P], krH[:, s, :, :].rearrange("p a b -> p (a b)").bitcast(F32),
                                    k.ident[:])
                nc.tensor.transpose(ps_u[:, 0:P], krL[:, s, :, :].rearrange("p a b -> p (a b)").bitcast(F32),
                                    k.ident[:]).then_inc(t_ps, 1)

            transposes(0)
            pe.wait_ge(wlL_rdy, KT)
            pe.wait_ge(hL_rdy, KT)
            for t in range(XT + CT):
                if t == 2:
                    transposes(1)
                if t == 6:
                    transposes(2)
                if t == QT:
                    pe.wait_ge(hL_rdy, 2 * KT)
                if t == XT:
                    pe.wait_ge(hL_rdy, 3 * KT)
                project(t)
                if t:
                    turn(t - 1)
            turn(XT + CT - 1)
            for kp in range(KT // 2):
                pe.wait_ge(gate_in[kp % 2], 16 * (kp // 2 + 1))
                for a in range(2):
                    for o in range(KT):
                        last = nc.tensor.matmul(ps_v[:, o:o + 1], ada[:, kp % 2, a * D + o * P:a * D + (o + 1) * P],
                                                cond[:, 2 * kp + a, 0:1], start=(kp == 0 and a == 0 and o == 0),
                                                stop=(kp == KT // 2 - 1 and a == 1), skip_group_check=True)
                last.then_inc(gate_used, 1)


def stage_gates(nc, k):
    G_PER = HEADS // GROUPS
    G0 = KT
    GP0 = G0 + GROUPS * (G_PER + 1)
    MM0, MP0, PA0 = GP0 + KT, GP0 + 2 * KT, GP0 + 3 * KT
    UNITS = PA0 + KT
    GM = 2 * KT
    G_USES = 2 * G_PER + 4
    GPM = GM + GROUPS * G_USES
    MMM = GPM + 2 * KT
    GPH = KT + GROUPS * (G_PER + 3)
    assert UNITS % 2 == 0 and GM % 4 == 0 and G_USES % 4 == 0

    with ExitStack() as ctx:
        def sb(name, shape, dt=F32):
            return ctx.enter_context(nc.sbuf_tensor(name, shape, dt))

        def sem(name):
            return ctx.enter_context(nc.semaphore(name))

        wst = sb("wst", [P, 2, D])
        wH = sb("wH", [P, 2, D], F32R)
        wL = sb("wL", [P, 2, D], F32R)
        up = sb("up", [P, KT, UW])
        dH = sb("dH", [P, 2, SEQ], F32R)
        dL = sb("dL", [P, 2, SEQ], F32R)
        pA = sb("pA", [P, UW])
        pB = sb("pB", [P, UW])
        inv = sb("inv", [P, SEQ])
        th = sb("th", [P, 2, HALF])
        ob = sb("ob", [P, 2, HALF])
        bank = [ctx.enter_context(nc.psum_tensor(f"ps_g{i}", [P, HALF], F32)) for i in range(4)]

        w_in = [sem("w_in0"), sem("w_in1")]
        wH_rdy = sem("wH_rdy2")
        wL_rdy = sem("wL_rdy2")
        used = sem("w_used")
        half_ps = sem("half_ps")
        ev_dve = sem("ev_dve")
        ev_act = sem("ev_act")
        pads = sem("pads")
        th_rdy = sem("th_rdy2")
        stored = [sem("stored0"), sem("stored1")]
        inv_in = sem("inv_in")
        win = sem("win")
        d_rdy = sem("d_rdy")
        dH_rdy = sem("dH_rdy")
        dL_rdy = sem("dL_rdy")
        zp_rdy = sem("zp_rdy")
        zpH_rdy = sem("zpH_rdy")
        zpL_rdy = sem("zpL_rdy")
        thp_in = [sem("thp_in0"), sem("thp_in1")]

        block = ctx.enter_context(nc.Block())

        def w_cols(c0):
            return k.w_in[:, bass.ds(c0, P)].rearrange("(a p) n -> p a n", p=P)

        @block.sync
        def _(sp):
            def load(slot, src):
                sp.dma_start(wst[:, slot, :].rearrange("p (a n) -> p a n", a=KT), src).then_inc(w_in[slot], 16)

            for n in range(2):
                load(n, w_cols(O_U + n * P))
            with sp.Fori(1, KT // 2) as i:
                for b in range(2):
                    sp.wait_ge(wL_rdy, 2 * i + (b - 1))
                    load(b, w_cols((2 * i + b) * P + O_U))
            for g in range(GROUPS):
                if g:
                    sp.wait_ge(d_rdy, 2 * g)
                sp.dma_start(inv[:], k.pool_inv[g:g + 1, :].to_broadcast([P, SEQ])).then_inc(inv_in, 16)
                n = G0 + (G_PER + 1) * g
                with sp.Fori(0, G_PER // 2) as i:
                    for b in range(2):
                        sp.wait_ge(wL_rdy, 2 * i + (n + b - 1))
                        load((n + b) % 2, w_cols((2 * i + (G_PER * g + b)) * P + O_GM))
                n += G_PER
                sp.wait_ge(wL_rdy, n - 1)
                sp.dma_start(wst[:, n % 2, 0:2 * 2 * P].rearrange("p (a n) -> p a n", a=2),
                             k.w_pool[g].rearrange("(a p) n -> p a n", p=P)).then_inc(w_in[n % 2], 16)
            for n0, off in ((GP0, O_GP), (MM0, O_MM), (MP0, O_MP)):
                with sp.Fori(0, KT // 2) as i:
                    for b in range(2):
                        sp.wait_ge(wL_rdy, 2 * i + (n0 + b - 1))
                        load(b, w_cols((2 * i + b) * P + off))
            for h in range(2):
                sp.wait_ge(stored[h], 16 * (HEADS + 2 * KT))
            with sp.Fori(0, KT // 2) as i:
                for b in range(2):
                    sp.wait_ge(wL_rdy, 2 * i + (PA0 + b - 1))
                    load(b, k.w_proj_pool[:, bass.ds((2 * i + b) * P, P)].rearrange("(a p) n -> p a n", p=P))
                    for h in range(2):
                        sp.wait_ge(ev_dve, 4 * i + (MMM + 2 * b + h - 1))
                        sp.dma_start(th[:, h, :], k.thp_d[bass.ds(2 * i + b, 1), :, h * HALF:(h + 1) * HALF]
                                     .rearrange("a p n -> p (a n)")).then_inc(thp_in[h], 16)

        @block.gpsimd
        def _(pool):
            def split(slot, n):
                pool.wait_ge(w_in[slot], (n - slot) * 8 + 16)
                if n >= 2:
                    pool.wait_ge(used, n - 1)
                nc.gpsimd.tensor_copy(wH[:, slot, :], wst[:, slot, :]).then_inc(wH_rdy, 1)
                pool.wait_ge(wH_rdy, n + 1)
                nc.gpsimd.tensor_tensor(wL[:, slot, :], wst[:, slot, :], wH[:, slot, :].bitcast(F32),
                                        ALU.subtract).then_inc(wL_rdy, 1)

            for n in range(2):
                split(n, n)
            nc.gpsimd.memset(up[:, :, 0:PAD], 0.0)
            nc.gpsimd.memset(up[:, :, PAD + SEQ:UW], 0.0).then_inc(pads, 1)
            for n in range(2, UNITS):
                split(n % 2, n)

        @block.scalar
        def _(act):
            for g in range(GROUPS):
                for q in range(G_PER):
                    for h in range(2):
                        m = GM + G_USES * g + 2 * q + h
                        act.wait_ge((half_ps, used)[h], (KT + (G_PER + 3) * g, G0 + (G_PER + 1) * g)[h] + q + 1)
                        if g or q:
                            act.wait_ge(ev_dve, m - 1 if q else m - 5)
                        nc.scalar.activation(th[:, h, :], bank[m % 4][:], ACT.Tanh, scale=0.5).then_inc(th_rdy, 1)
                        act.wait_ge(ev_dve, m + 1)
                        act.dma_start(k.sg_d[G_PER * g + q, :, h * HALF:(h + 1) * HALF], ob[:, h, :]
                                      ).then_inc(stored[h], 16)
                    if q in (1, 2):
                        j = 2 * g + q - 1
                        act.wait_ge(d_rdy, j + 1)
                        if g:
                            act.wait_ge(used, G0 + (G_PER + 1) * g)
                        nc.scalar.activation(dH[:, q - 1, :], (pA if g % 2 else pB)[:, 0:SEQ], ACT.Copy
                                             ).then_inc(dH_rdy, 1)
            with act.Fori(0, KT // 2) as i:
                for b in range(2):
                    for h in range(2):
                        act.wait_ge((half_ps, used)[h], 2 * i + ((GPH, GP0)[h] + b + 1))
                        act.wait_ge(ev_dve, 4 * i + (GPM + 2 * b + h - 1))
                        nc.scalar.activation(th[:, h, :], bank[2 * b + h][:], ACT.Tanh, scale=0.5).then_inc(th_rdy, 1)
            act.wait_ge(zp_rdy, 2 * KT)
            for seg, (dst, bg) in enumerate(((k.th_d, KT), (k.thp_d, 0))):
                for j in range(KT):
                    for h in range(2):
                        r = seg * 2 * KT + 2 * j + h
                        act.wait_ge((half_ps, used)[h], (GPH, GP0)[h] + (seg + 1) * KT + j + 1)
                        act.wait_ge(stored[h], 16 * (HEADS + seg * KT + j))
                        nc.scalar.activation(ob[:, h, :], bank[r % 4][:], ACT.Tanh, scale=0.5,
                                             bias=k.bgh[:, bg + j:bg + j + 1]).then_inc(ev_act, 1)
                        act.wait_ge(ev_act, r + 1)
                        act.dma_start(dst[j, :, h * HALF:(h + 1) * HALF], ob[:, h, :]).then_inc(stored[h], 16)
            act.wait_ge(used, PA0)
            for kt in range(KT):
                nc.scalar.activation(k.hH[:, kt, :], up[:, kt, PAD:PAD + SEQ], ACT.Copy).then_inc(zpH_rdy, 1)
            with act.Fori(0, KT // 2) as i:
                for b in range(2):
                    for h in range(2):
                        act.wait_ge(ev_dve, 4 * i + (MMM + 2 * b + h + 1))
                        act.dma_start(k.yp_d[bass.ds(2 * i + b, 1), :, h * HALF:(h + 1) * HALF]
                                      .rearrange("a p n -> p (a n)"), ob[:, h, :]).then_inc(stored[h], 16)
            for h in range(2):
                act.wait_ge(stored[h], 16 * (HEADS + 3 * KT))

        @block.vector
        def _(dve):
            dve.wait_ge(pads, 1)
            with dve.Fori(0, KT // 2) as i:
                for b in range(2):
                    for h in range(2):
                        dve.wait_ge((half_ps, used)[h], 2 * i + (b + 1))
                        nc.vector.tensor_copy(up[:, bass.ds(2 * i + b, 1), PAD + h * HALF:PAD + (h + 1) * HALF],
                                              bank[2 * b + h][:].unsqueeze(1)).then_inc(ev_dve, 1)
            steps = 0

            def pool_tile(g, j):
                nonlocal steps
                src = up[:, j, :]
                bufs = [pA, pB]
                lo, hi = 0, UW
                for lvl in range(g + 1):
                    shift = (1, 1, 2, 4)[lvl]
                    right = 0 if lvl == 0 else shift
                    lo, hi = lo + shift, hi - right
                    dst = bufs[lvl % 2]
                    if steps:
                        dve.wait_ge(win, steps)
                    nc.vector.tensor_tensor(dst[:, lo:hi], src[:, lo - shift:hi - shift],
                                            src[:, lo + right:hi + right], ALU.add).then_inc(win, 1)
                    steps += 1
                    src = dst
                cur, oth = bufs[g % 2], bufs[(g + 1) % 2]
                dve.wait_ge(win, steps)
                nc.vector.tensor_tensor(oth[:, 0:SEQ], cur[:, PAD:PAD + SEQ], inv[:], ALU.mult).then_inc(win, 1)
                steps += 1
                dve.wait_ge(win, steps)
                nc.vector.tensor_tensor(oth[:, 0:SEQ], oth[:, 0:SEQ], up[:, j, PAD:PAD + SEQ], ALU.subtract
                                        ).then_inc(d_rdy, 1)
                dve.wait_ge(d_rdy, j + 1)
                return oth

            for g in range(GROUPS):
                for q in range(G_PER):
                    for h in range(2):
                        m = GM + G_USES * g + 2 * q + h
                        gi = G_PER * g + q
                        dve.wait_ge(th_rdy, 2 * gi + h + 1)
                        if gi:
                            dve.wait_ge(stored[h], 16 * gi)
                        nc.vector.scalar_tensor_tensor(out=ob[:, h, :], in0=th[:, h, :], scalar=1.0,
                                                       in1=bank[m % 4][:], op0=ALU.add, op1=ALU.mult
                                                       ).then_inc(ev_dve, 1)
                    if q in (1, 2):
                        j = 2 * g + q - 1
                        dve.wait_ge(dH_rdy, j + 1)
                        nc.vector.tensor_tensor(dL[:, q - 1, :], (pA if g % 2 else pB)[:, 0:SEQ],
                                                dH[:, q - 1, :].bitcast(F32), ALU.subtract).then_inc(dL_rdy, 1)
                        dve.wait_ge(dL_rdy, j + 1)
                    if q < 2:
                        if q == 0:
                            dve.wait_ge(inv_in, 16 * (g + 1))
                        pool_tile(g, 2 * g + q)
                for dt in range(2):
                    for h in range(2):
                        m = GM + G_USES * g + 2 * G_PER + 2 * dt + h
                        dve.wait_ge(*((used, G0 + (G_PER + 1) * (g + 1)) if dt and h else
                                      (half_ps, KT + (G_PER + 3) * g + G_PER + 2 * dt + h + 1)))
                        nc.vector.tensor_scalar(up[:, 2 * g + dt, PAD + h * HALF:PAD + (h + 1) * HALF], bank[m % 4][:],
                                                k.vt[:, R_PS + 2 * g + dt:R_PS + 2 * g + dt + 1], None,
                                                ALU.mult).then_inc(ev_dve, 1)
            for h in range(2):
                dve.wait_ge(stored[h], 16 * HEADS)
            with dve.Fori(0, KT // 2) as i:
                for b in range(2):
                    for h in range(2):
                        a = 2 * b + h
                        dve.wait_ge(th_rdy, 4 * i + (2 * HEADS + a + 1))
                        nc.vector.scalar_tensor_tensor(out=ob[:, h, :], in0=th[:, h, :], scalar=1.0,
                                                       in1=bank[a][:], op0=ALU.add, op1=ALU.mult).then_inc(ev_dve, 1)
                        dve.wait_ge(ev_dve, 4 * i + (GPM + a + 1))
                        t = up[:, bass.ds(2 * i + b, 1), PAD + h * HALF:PAD + (h + 1) * HALF]
                        nc.vector.scalar_tensor_tensor(out=t, in0=t, scalar=0.5, in1=ob[:, h, :].unsqueeze(1),
                                                       op0=ALU.mult, op1=ALU.mult).then_inc(zp_rdy, 1)
            for kt in range(KT):
                dve.wait_ge(zpH_rdy, kt + 1)
                nc.vector.tensor_tensor(k.hL[:, kt, :], up[:, kt, PAD:PAD + SEQ], k.hH[:, kt, :].bitcast(F32),
                                        ALU.subtract).then_inc(zpL_rdy, 1)
            with dve.Fori(0, KT // 2) as i:
                for b in range(2):
                    for h in range(2):
                        a = 2 * b + h
                        dve.wait_ge((half_ps, used)[h], 2 * i + ((GPH, GP0)[h] + 3 * KT + b + 1))
                        dve.wait_ge(thp_in[h], 32 * i + 16 * (b + 1))
                        dve.wait_ge(stored[h], 32 * i + 16 * (HEADS + 2 * KT + b))
                        nc.vector.scalar_tensor_tensor(out=ob[:, h, :], in0=th[:, h, :], scalar=1.0,
                                                       in1=bank[a][:], op0=ALU.add, op1=ALU.mult).then_inc(ev_dve, 1)

        @block.tensor
        def _(pe):
            def unit(slot, n, b0, free=None, free_at=0, tiles=False):
                pe.wait_ge(wL_rdy, n + 1)
                for h in range(2):
                    if free is not None:
                        pe.wait_ge(free, free_at + h)
                    c = slice(h * HALF, (h + 1) * HALF)
                    for kt in range(KT):
                        if tiles and h == 0:
                            pe.wait_ge(zpL_rdy, kt + 1)
                        w = slice(kt * P, (kt + 1) * P)
                        last = mm3(nc, bank[b0 + h][:], wH[:, slot, w], wL[:, slot, w], k.hH[:, kt, c], k.hL[:, kt, c],
                                   kt == 0, kt == KT - 1)
                    last.then_inc((half_ps, used)[h], 1)

            def units(n0, free, free_at, first=0):
                with pe.Fori(first, KT // 2) as i:
                    for b in range(2):
                        unit(b, 2 * i + (n0 + b), 2 * b, free, 4 * i + (free_at + 2 * b))

            for n in range(2):
                unit(n, n, 2 * n)
            units(0, ev_dve, -3, first=1)
            for g in range(GROUPS):
                n, m = G0 + (G_PER + 1) * g, GM + G_USES * g
                with pe.Fori(0, G_PER // 2) as i:
                    for b in range(2):
                        unit((n + b) % 2, 2 * i + (n + b), 2 * b, ev_dve, 4 * i + (m + 2 * b - 3))
                n, m = n + G_PER, m + 2 * G_PER
                pe.wait_ge(wL_rdy, n + 1)
                pe.wait_ge(dL_rdy, 2 * g + 2)
                for dt in range(2):
                    for h in range(2):
                        pe.wait_ge(ev_dve, m + 2 * dt + h - 3)
                        for kt in range(2):
                            w = slice(kt * 2 * P + dt * P, kt * 2 * P + (dt + 1) * P)
                            c = slice(h * HALF, (h + 1) * HALF)
                            last = mm3(nc, bank[2 * dt + h][:], wH[:, n % 2, w], wL[:, n % 2, w], dH[:, kt, c],
                                       dL[:, kt, c], kt == 0, kt == 1)
                        last.then_inc(used if dt and h else half_ps, 1)
            units(GP0, ev_dve, GPM - 3)
            pe.wait_ge(ev_dve, MMM)
            for b in range(2):
                unit(b, MM0 + b, 2 * b)
            units(MM0, ev_act, -3, first=1)
            units(MP0, ev_act, 2 * KT - 3)
            pe.wait_ge(ev_act, 4 * KT)
            for b in range(2):
                unit(b, PA0 + b, 2 * b, ev_dve, MMM + 2 * b - 3, tiles=(b == 0))
            units(PA0, ev_dve, MMM - 3, first=1)


QCHUNKS = ((0, 512), (512, 1024), (1024, KEYS))
QKT = (((0, 1, 2), (3, 4), (5, 6), (7, 8, 9)),
       ((0, 1, 2), (3, 4, 5), (6, 7), (8, 9)),
       ((0, 1, 2), (3, 4, 5), (6, 7), (8, 9)),
       ((0, 1), (2, 3), (4, 5, 6), (7, 8, 9)))
M_PRO = 4
TAIL = ("R", "o", "y0", "y1", "y2", "y3", "y4", "R last", "y5", "o last", "y6", "y7",
        "h0", "h1", "h2", "h3", "h4", "h5", "h6", "h7")


def unit_products(j, kind):
    y = kind != "first"
    last = kind == "last"
    prev = ["R", "o"] * (y or j > 1)
    if j == 0:
        return [["rope"], prev, ["turn", "q"], ["absorb"]]
    if j == 1:
        return [["y0", "y1"] * y, prev + ["y2"] * y, ["q"] + ["y3"] * y, ["y4", "y5"] * y]
    if j == 2:
        return [["y6", "y7"] * y, prev + ["h0"] * y, ["turn"] * (not last) + ["q"] + ["h1"] * y,
                ["absorb"] * (not last) + ["h2"] * y]
    return [["rope"] * (not last) + ["h3"] * y, prev + ["h4", "h5"] * y, ["h6", "h7"] * y + ["q"] * (not last), []]


def body_size(kind):
    return sum(len(q) for j in range(4) for q in unit_products(j, kind))


def product_index(i, j, name, kind):
    off = 0
    for jj in range(4):
        for q in unit_products(jj, kind):
            for n in q:
                if jj == j and n == name:
                    first = M_PRO + body_size("first")
                    if kind == "first":
                        return M_PRO + off
                    if kind == "last":
                        return first + (PAIRS - 2) * body_size("mid") + off
                    return i * body_size("mid") + (first - body_size("mid") + off)
                off += 1
    raise KeyError(name)


def product_bank(j, name, kind):
    return (product_index(1, j, name, kind) if kind == "mid" else product_index(0, j, name, kind)) % 2


def stage_attention(nc, k):
    assert body_size("mid") % 2 == 0
    TAIL0 = M_PRO + body_size("first") + (PAIRS - 2) * body_size("mid") + body_size("last")
    UNITS = 4 * PAIRS

    with ExitStack() as ctx:
        def sb(name, shape, dt=F32):
            return ctx.enter_context(nc.sbuf_tensor(name, shape, dt))

        def sem(name):
            return ctx.enter_context(nc.semaphore(name))

        E = sb("E", [P, 2, QT, KEYS])
        ptH = sb("ptH", [P, 2, HALF], F32R)
        ptL = sb("ptL", [P, 2, HALF], F32R)
        qpH = sb("qpH", [P, 2, HALF], F32R)
        qpL = sb("qpL", [P, 2, HALF], F32R)
        q2 = [sb("q2a", [P, SEQ], F32R), sb("q2b", [P, SEQ], F32R)]
        cs = sb("cs", [P, 2, HALF])
        wp_st = sb("wp_st", [P, D])
        wpH = sb("wpH", [P, 2, D], F32R)
        wpL = sb("wpL", [P, 2, D], F32R)
        zH = sb("zH", [P, 2, 2, HALF], F32R)
        zL = sb("zL", [P, 2, 2, HALF], F32R)
        wq_st = sb("wq_st", [P, 2, QLT, NOPE + ROPE])
        wkv_st = sb("wkv_st", [P, 2, NOPE + VD])
        wcH = sb("wcH", [P, 2, QL], F32R)
        wcL = sb("wcL", [P, 2, QL], F32R)
        wrH = sb("wrH", [P, QLT, 2, ROPE], F32R)
        wrL = sb("wrL", [P, QLT, 2, ROPE], F32R)
        wvH = sb("wvH", [P, 2, VD], F32R)
        wvL = sb("wvL", [P, 2, VD], F32R)
        sw = sb("sw", [P, HALF])
        t1 = sb("t1", [P, HALF])
        sg = sb("sg", [P, HALF])
        opH = sb("opH", [P, HALF], F32R)
        opL = sb("opL", [P, HALF], F32R)
        mx = sb("mx", [P, 2, QT, 3])
        nm = sb("nm", [P, 2, QT])
        sums = sb("sums", [P, 2, QT])
        rinv = sb("rinv", [P, 2, QT])

        ps_s = ctx.enter_context(nc.psum_tensor("ps_s", [P, 3 * 512], F32))
        ps_pt = [ctx.enter_context(nc.psum_tensor(f"ps_pt{b}", [P, HALF], F32)) for b in range(2)]
        ps_o = ctx.enter_context(nc.psum_tensor("ps_o", [P, HALF], F32))
        ps_m = [ctx.enter_context(nc.psum_tensor(f"ps_m{b}", [P, HALF], F32)) for b in range(2)]

        wq_in = [sem("wq_in0"), sem("wq_in1")]
        wp_in = sem("wp_in")
        cs_in = sem("cs_in")
        sg_in = sem("sg_in")
        s_chunk = [sem(f"s_chunk{c}") for c in range(3)]
        mx_rdy = sem("mx_rdy")
        nm_rdy = sem("nm_rdy")
        e_rdy = sem("e_rdy")
        pt_ps = sem("pt_ps")
        ptH_rdy = sem("ptH_rdy")
        ptL_rdy = sem("ptL_rdy")
        pv = sem("pv")
        opH_rdy = sem("opH_rdy")
        opL_rdy = sem("opL_rdy")
        rinv_rdy = sem("rinv_rdy")
        m_ps = sem("m_ps")
        mH_rdy = sem("mH_rdy")
        m_free = sem("m_free")
        sw_rdy = sem("sw_rdy")
        sn_rdy = sem("sn_rdy")
        tq_rdy = sem("tq_rdy")
        q2H_rdy = sem("q2H_rdy")
        q2_rdy = sem("q2_rdy")
        wrH_rdy = sem("wrH_rdy")
        wrL_rdy = sem("wrL_rdy")
        wvH_rdy = sem("wvH_rdy")
        wvL_rdy = sem("wvL_rdy")
        wpH_rdy = sem("wpH_rdy")
        wpL_rdy = sem("wpL_rdy")
        zH_rdy = sem("zH_rdy")
        z_rdy = sem("z_rdy")

        block = ctx.enter_context(nc.Block())

        def static(v):
            return isinstance(v, int)

        def positive(eng, s, v):
            if not static(v) or v > 0:
                eng.wait_ge(s, v)

        def bodies(eng, body):
            body(0, "first")
            with eng.Fori(1, PAIRS - 1) as i:
                body(i, "mid")
            body(PAIRS - 1, "last")

        def mhi_count(i, kind, j, name):
            n = 0
            for jj in range(4):
                for q in unit_products(jj, kind):
                    for nm_ in q:
                        if nm_ in ("turn", "absorb", "q"):
                            n += 1
                        if jj == j and nm_ == name:
                            per = 8
                            return i * per + (3 + n)
            raise KeyError(name)

        def raw_rope(t):
            return t.rearrange("p k (a b c) -> p b k a c", a=2, b=2)

        def rope_half(t, b):
            return t[:, :, b * RH:(b + 1) * RH].rearrange("p k (a c) -> p k a c", a=2)

        @block.sync
        def _(sp):
            def head_weights(h, slot):
                sp.dma_start(wq_st[:, slot, :, :],
                             k.w_qb[:, bass.ds(h * (NOPE + ROPE), NOPE + ROPE)].rearrange("(a p) n -> p a n", p=P)
                             ).then_inc(wq_in[slot], 16)
                sp.dma_start(wkv_st[:, slot, :], k.w_kvb[:, bass.ds(h * (NOPE + VD), NOPE + VD)]
                             ).then_inc(wq_in[slot], 16)

            def tables(half):
                c = slice(half * HALF, (half + 1) * HALF)
                sp.dma_start(cs[:, 0, :], k.qcos_d[:, c]).then_inc(cs_in, 16)
                sp.dma_start(cs[:, 1, :], k.qsin_d[:, c]).then_inc(cs_in, 16)

            def proj_weights(h):
                sp.dma_start(wp_st[:], k.w_proj_mla[bass.ds(h * VD, VD), :]).then_inc(wp_in, 16)

            def gate_tile(h, half):
                sp.dma_start(sg[:], k.sg_d[bass.ds(h, 1), :, half * HALF:(half + 1) * HALF]
                             .rearrange("a p n -> p (a n)")).then_inc(sg_in, 16)

            head_weights(0, 0)
            head_weights(1, 1)
            tables(0)
            proj_weights(0)
            sp.wait_ge(tq_rdy, 1)
            tables(1)

            def body(i, kind):
                for j in range(4):
                    w = 4 * i + j - 2
                    if j == 0 and kind != "last":
                        sp.wait_ge(wvL_rdy, 2 * i + 1)
                        head_weights(2 * i + 2, 0)
                    if j == 2 and kind != "last":
                        sp.wait_ge(wvL_rdy, 2 * i + 2)
                        head_weights(2 * i + 3, 1)
                    if kind != "first" or j >= 2:
                        positive(sp, z_rdy, w)
                        gate_tile(2 * i + j // 2 - 1, j % 2)
                    if kind != "first" and j < 2:
                        sp.wait_ge(wpL_rdy, 2 * i - 1 + j)
                        proj_weights(2 * i - 1 + j)
                    if j == 1 and kind != "last":
                        sp.wait_ge(tq_rdy, 2 * i + 2)
                        tables(0)
                    if j == 3 and kind != "last":
                        sp.wait_ge(tq_rdy, 2 * i + 3)
                        tables(1)

            bodies(sp, body)
            sp.wait_ge(z_rdy, UNITS - 2)
            gate_tile(HEADS - 1, 0)
            sp.wait_ge(wpL_rdy, HEADS - 1)
            proj_weights(HEADS - 1)
            sp.wait_ge(z_rdy, UNITS - 1)
            gate_tile(HEADS - 1, 1)

        @block.gpsimd
        def _(pool):
            def lo(out, x, hi):
                return nc.gpsimd.tensor_tensor(out, x, hi.bitcast(F32), ALU.subtract)

            def wr_lo(h, slot):
                pool.wait_ge(wrH_rdy, h + 1)
                for b in range(2):
                    last = lo(rope_half(wrL[:, :, slot, :], b), raw_rope(wq_st[:, slot, :, NOPE:])[:, b],
                              rope_half(wrH[:, :, slot, :], b))
                last.then_inc(wrL_rdy, 1)

            def wv_lo(h, slot):
                pool.wait_ge(wvH_rdy, h + 1)
                lo(wvL[:, slot, :], wkv_st[:, slot, NOPE:], wvH[:, slot, :]).then_inc(wvL_rdy, 1)

            def wp_lo(h, slot):
                pool.wait_ge(wpH_rdy, h + 1)
                lo(wpL[:, slot, :], wp_st[:], wpH[:, slot, :]).then_inc(wpL_rdy, 1)

            def rotate(r, at):
                pool.wait_ge(cs_in, 32 * r + 32)
                pool.wait_ge(sw_rdy, r + 1)
                nc.gpsimd.tensor_tensor(sw[:], sw[:], cs[:, 1, :], ALU.mult).then_inc(sn_rdy, 1)
                pool.wait_ge(m_free, at)
                pool.wait_ge(sn_rdy, r + 1)
                nc.gpsimd.tensor_tensor(t1[:], t1[:], sw[:], ALU.add).then_inc(tq_rdy, 1)

            def z_lo(v, hp, half):
                pool.wait_ge(zH_rdy, v + 1)
                lo(zL[:, hp, half, :], sg[:], zH[:, hp, half, :]).then_inc(z_rdy, 1)

            wr_lo(0, 0)
            wr_lo(1, 1)
            wv_lo(0, 0)
            rotate(0, M_PRO)

            def body(i, kind):
                rotate(2 * i + 1, product_index(i, 0, "rope", kind) + 1)
                if kind != "first":
                    wp_lo(2 * i - 2, 0)
                if kind != "last":
                    wr_lo(2 * i + 2, 0)
                if kind != "first":
                    wp_lo(2 * i - 1, 1)
                    z_lo(4 * i - 2, 1, 0)
                wv_lo(2 * i + 1, 1)
                if kind != "first":
                    z_lo(4 * i - 1, 1, 1)
                if kind != "last":
                    wr_lo(2 * i + 3, 1)
                z_lo(4 * i, 0, 0)
                if kind != "last":
                    rotate(2 * i + 2, product_index(i, 3, "rope", kind) + 1)
                    wv_lo(2 * i + 2, 0)
                z_lo(4 * i + 1, 0, 1)

            bodies(pool, body)
            wp_lo(HEADS - 2, 0)
            z_lo(UNITS - 2, 1, 0)
            wp_lo(HEADS - 1, 1)
            z_lo(UNITS - 1, 1, 1)

        @block.scalar
        def _(act):
            def copy(out, x):
                return nc.scalar.activation(out, x, ACT.Copy)

            def wr_hi(h, slot):
                act.wait_ge(wq_in[slot], (h - slot) * 16 + 32)
                for b in range(2):
                    last = copy(rope_half(wrH[:, :, slot, :], b), raw_rope(wq_st[:, slot, :, NOPE:])[:, b])
                last.then_inc(wrH_rdy, 1)

            def wv_hi(h, slot):
                copy(wvH[:, slot, :], wkv_st[:, slot, NOPE:]).then_inc(wvH_rdy, 1)

            def wp_hi(h, slot):
                act.wait_ge(wp_in, h * 16 + 16)
                copy(wpH[:, slot, :], wp_st[:]).then_inc(wpH_rdy, 1)

            def small_hi(name, at, b, half=0, slot=0, r=None):
                if name in ("turn", "absorb", "q", "rope"):
                    act.wait_ge(m_ps, at + 1)
                if name == "turn":
                    copy(opH[:, 0:3 * P], ps_m[b][:, 0:3 * P]).then_inc(mH_rdy, 1)
                elif name == "absorb":
                    copy(wcH[:, slot, :], ps_m[b][:, 0:QL]).then_inc(mH_rdy, 1)
                elif name == "q":
                    copy(qpH[:, half, :], ps_m[b][:]).then_inc(mH_rdy, 1)
                elif name == "rope":
                    for q in range(4):
                        o = q ^ 1
                        last = copy(sw[q * RH:(q + 1) * RH, :], ps_m[b][o * RH:(o + 1) * RH, :])
                    last.then_inc(sw_rdy, 1)

            def rope_hi(r, half):
                act.wait_ge(tq_rdy, r + 1)
                c = slice(half * HALF, (half + 1) * HALF)
                copy(q2[0][0:ROPE, c], t1[0:ROPE, :])
                copy(q2[1][ROPE:P, c], t1[ROPE:P, :]).then_inc(q2H_rdy, 1)

            def z_hi(v, hp, half, at):
                act.wait_ge(m_free, at)
                copy(zH[:, hp, half, :], sg[:]).then_inc(zH_rdy, 1)

            def exponent(u, j, qt):
                act.wait_ge(nm_rdy, 4 * u + (qt + 1))
                if qt == 0:
                    positive(act, pt_ps, 10 * (u - 1))
                nc.scalar.activation(E[:, j % 2, qt, :], ps_s[:, 0:KEYS], ACT.Exp, bias=nm[:, j % 2, qt:qt + 1],
                                     accum_out=sums[:, j % 2, qt:qt + 1]).then_inc(e_rdy, 1)

            def turned_hi(v, kt):
                act.wait_ge(pt_ps, NKT * v + (kt + 1))
                positive(act, pv, NKT * v + (kt - 1))
                copy(ptH[:, kt % 2, :], ps_pt[kt % 2][:]).then_inc(ptH_rdy, 1)

            def latent_hi(v):
                act.wait_ge(pv, NKT * (v + 1))
                copy(opH[:], ps_o[:]).then_inc(opH_rdy, 1)

            wr_hi(0, 0)
            wr_hi(1, 1)
            wv_hi(0, 0)
            small_hi("turn", 0, 0)
            small_hi("absorb", 1, 1)
            small_hi("q", 2, 0)
            small_hi("rope", 3, 1)
            rope_hi(0, 0)

            def body(i, kind):
                for j in range(4):
                    u = 4 * i + j
                    v, w = u - 1, u - 2
                    has_v = kind != "first" or j > 0
                    has_w = kind != "first" or j > 1

                    def at(name, jj=j):
                        return product_index(i, jj, name, kind)

                    for qt in range(QT):
                        kts = QKT[j][qt] if has_v else ()
                        if has_v:
                            turned_hi(v, kts[0])
                        if qt == 0 and has_w:
                            latent_hi(w)
                        if has_v:
                            turned_hi(v, kts[1])
                        exponent(u, j, qt)
                        for n, name in enumerate(unit_products(j, kind)[qt]):
                            if n == 1:
                                for kt in kts[2:]:
                                    turned_hi(v, kt)
                                kts = ()
                            small_hi(name, at(name), product_bank(j, name, kind), half=(j + 1) % 2,
                                     slot=(j // 2 + 1) % 2)
                        for kt in kts[2:]:
                            turned_hi(v, kt)
                        if qt == 0 and j == 0 and kind != "first":
                            act.wait_ge(m_ps, at("rope") + 1)
                            wp_hi(2 * i - 2, 0)
                        if qt == 1 and j == 0:
                            rope_hi(2 * i + 1, 1)
                        if qt == 1 and j == 3 and kind != "last":
                            rope_hi(2 * i + 2, 0)
                        if qt == 2 and j == 0 and kind != "last":
                            wr_hi(2 * i + 2, 0)
                        if qt == 2 and j == 1:
                            if kind != "first":
                                act.wait_ge(m_ps, at("o") + 1)
                            wv_hi(2 * i + 1, 1)
                        if qt == 2 and j == 2 and kind != "last":
                            wr_hi(2 * i + 3, 1)
                        if qt == 2 and j == 3 and kind != "last":
                            act.wait_ge(m_ps, at("o") + 1)
                            wv_hi(2 * i + 2, 0)
                        if qt == 3 and j == 0 and kind != "first":
                            wp_hi(2 * i - 1, 1)
                        if qt == 3 and has_w:
                            if j == 3 and kind != "first":
                                act.wait_ge(m_ps, at("h7") + 1)
                            z_hi(w, (j // 2 + 1) % 2, j % 2, at("o") + 1)

            bodies(act, body)
            v = UNITS - 1
            for kt in range(NKT):
                turned_hi(v, kt)
                if kt == 0:
                    latent_hi(v - 1)
                    act.wait_ge(m_ps, TAIL0)
                    wp_hi(HEADS - 2, 0)
                if kt == 5:
                    z_hi(v - 1, 1, 0, TAIL0 + 2)
                    wp_hi(HEADS - 1, 1)
            latent_hi(v)
            z_hi(v, 1, 1, TAIL0 + TAIL.index("o last") + 1)

        @block.vector
        def _(dve):
            def lo(out, x, hi):
                return nc.vector.tensor_tensor(out, x, hi.bitcast(F32), ALU.subtract)

            def small(name, at, b, half=0, slot=0, hi=None, unit=None):
                ps = ps_m[b]
                if hi is not None:
                    dve.wait_ge(mH_rdy, hi)
                if name == "turn":
                    lo(opL[:, 0:3 * P], ps[:, 0:3 * P], opH[:, 0:3 * P]).then_inc(m_free, 1)
                elif name == "absorb":
                    lo(wcL[:, slot, :], ps[:, 0:QL], wcH[:, slot, :]).then_inc(m_free, 1)
                elif name == "q":
                    lo(qpL[:, half, :], ps[:], qpH[:, half, :]).then_inc(m_free, 1)
                elif name == "R":
                    dve.wait_ge(m_ps, at + 1)
                    dve.wait_ge(sg_in, 16 * (unit + 1))
                    nc.vector.tensor_tensor(sg[:], sg[:], ps[:], ALU.mult).then_inc(m_free, 1)
                elif name == "o":
                    dve.wait_ge(m_ps, at + 1)
                    dve.wait_ge(m_free, at)
                    nc.vector.scalar_tensor_tensor(out=sg[:], in0=ps[:], scalar=0.5, in1=sg[:], op0=ALU.mult,
                                                   op1=ALU.mult).then_inc(m_free, 1)
                else:
                    y_half = int(name[0] == "h")
                    t = k.yacc[:, int(name[1]), y_half * HALF:(y_half + 1) * HALF]
                    dve.wait_ge(m_ps, at + 1)
                    nc.vector.tensor_tensor(t, t, ps[:], ALU.add).then_inc(m_free, 1)

            def rope(r, at, b):
                dve.wait_ge(sw_rdy, r + 1)
                dve.wait_ge(cs_in, 32 * r + 32)
                nc.vector.tensor_tensor(t1[:], ps_m[b][:], cs[:, 0, :], ALU.mult).then_inc(m_free, 1)

            def rope_lo(r, half):
                dve.wait_ge(q2H_rdy, r + 1)
                c = slice(half * HALF, (half + 1) * HALF)
                lo(q2[0][ROPE:P, c], t1[0:ROPE, :], q2[0][0:ROPE, c])
                lo(q2[1][0:ROPE, c], t1[ROPE:P, :], q2[1][ROPE:P, c]).then_inc(q2_rdy, 1)

            def turned_lo(v, kt):
                dve.wait_ge(ptH_rdy, NKT * v + (kt + 1))
                lo(ptL[:, kt % 2, :], ps_pt[kt % 2][:], ptH[:, kt % 2, :]).then_inc(ptL_rdy, 1)

            def maximum(u, j, qt, c):
                n = 4 * u + qt
                dve.wait_ge(s_chunk[c], n + 1)
                last = nc.vector.tensor_reduce(mx[:, j % 2, qt, c:c + 1], ps_s[:, slice(*QCHUNKS[c])], AX_X, ALU.max)
                if c == 2:
                    last.then_inc(mx_rdy, 1)
                    dve.wait_ge(mx_rdy, n + 1)
                    nc.vector.tensor_reduce(nm[:, j % 2, qt:qt + 1], mx[:, j % 2, qt, :], AX_X, ALU.max, negate=True
                                            ).then_inc(nm_rdy, 1)

            def inverse_sums(v, jv):
                dve.wait_ge(e_rdy, 4 * (v + 1))
                nc.vector.reciprocal(rinv[:, jv % 2, :], sums[:, jv % 2, :]).then_inc(rinv_rdy, 1)

            def latent_lo(v):
                dve.wait_ge(opH_rdy, v + 1)
                lo(opL[:], ps_o[:], opH[:]).then_inc(opL_rdy, 1)

            nc.vector.memset(k.yacc[:], 0.0)
            small("turn", 0, 0, hi=1)
            small("absorb", 1, 1, hi=2)
            small("q", 2, 0, hi=3)
            rope(0, 3, 1)
            rope_lo(0, 0)

            def body(i, kind):
                for j in range(4):
                    u = 4 * i + j
                    v, w = u - 1, u - 2
                    has_v = kind != "first" or j > 0
                    has_w = kind != "first" or j > 1

                    def filler(name):
                        at = product_index(i, j, name, kind)
                        b = product_bank(j, name, kind)
                        if name == "rope":
                            rope(2 * i + (1 if j == 0 else 2), at, b)
                            return
                        hi = mhi_count(i, kind, j, name) if name in ("turn", "absorb", "q") else None
                        small(name, at, b, half=(j + 1) % 2, slot=(j // 2 + 1) % 2, hi=hi, unit=w)

                    for qt in range(QT):
                        kts = QKT[j][qt] if has_v else ()
                        maximum(u, j, qt, 0)
                        if qt == 0 and has_v:
                            inverse_sums(v, (j - 1) % 4)
                        if has_v:
                            turned_lo(v, kts[0])
                        maximum(u, j, qt, 1)
                        if qt == 0 and has_w:
                            latent_lo(w)
                        maximum(u, j, qt, 2)
                        if has_v:
                            turned_lo(v, kts[1])
                        for n, name in enumerate(unit_products(j, kind)[qt]):
                            if n == 1:
                                for kt in kts[2:]:
                                    turned_lo(v, kt)
                                kts = ()
                            filler(name)
                        for kt in kts[2:]:
                            turned_lo(v, kt)
                        if qt == 1 and j == 0:
                            rope_lo(2 * i + 1, 1)
                        if qt == 1 and j == 3 and kind != "last":
                            rope_lo(2 * i + 2, 0)

            bodies(dve, body)
            v = UNITS - 1
            inverse_sums(v, 3)

            def tail(n):
                small(TAIL[n].split()[0], TAIL0 + n, (TAIL0 + n) % 2, unit=v if "last" in TAIL[n] else v - 1)

            for kt in range(NKT):
                turned_lo(v, kt)
                if kt == 0:
                    latent_lo(v - 1)
                if kt in (2, 3):
                    tail(kt - 2)
                if kt >= 6:
                    tail(kt - 4)
            latent_lo(v)
            for n in range(NKT - 4, len(TAIL)):
                tail(n)

        @block.tensor
        def _(pe):
            def small(name, at, b, half=0, slot=0, unit=None, ju=None):
                if not (static(at) and at < 2):
                    pe.wait_ge(m_free, at - 1)
                ps = ps_m[b]
                if name == "turn":
                    for kt in range(QLT):
                        nc.tensor.transpose(ps[:, kt * P:(kt + 1) * P], wq_st[:, slot, kt, 0:NOPE], k.ident[:])
                    last = nc.tensor.transpose(ps[:, 2 * P:3 * P], wkv_st[:, slot, 0:NOPE], k.ident[:])
                elif name == "absorb":
                    for kt in range(QLT):
                        w = slice(kt * P, (kt + 1) * P)
                        last = mm3(nc, ps[:, w], opH[:, w], opL[:, w], opH[:, 2 * P:3 * P], opL[:, 2 * P:3 * P],
                                   True, True)
                elif name == "q":
                    for kt in range(QLT):
                        w = slice(kt * P, (kt + 1) * P)
                        c = slice(half * HALF, (half + 1) * HALF)
                        last = mm3(nc, ps[:], wcH[:, slot, w], wcL[:, slot, w], k.qnH[:, kt, c], k.qnL[:, kt, c],
                                   kt == 0, kt == QLT - 1)
                elif name == "rope":
                    for kt in range(QLT):
                        c = slice(half * HALF, (half + 1) * HALF)
                        last = mm3(nc, ps[:], wrH[:, kt, :, :].rearrange("p a b -> p (a b)"),
                                   wrL[:, kt, :, :].rearrange("p a b -> p (a b)"), k.qnH[:, kt, c], k.qnL[:, kt, c],
                                   kt == 0, kt == QLT - 1)
                elif name == "R":
                    pe.wait_ge(rinv_rdy, unit + 1)
                    for t in range(QT):
                        last = nc.tensor.transpose(ps[:, t * P:(t + 1) * P],
                                                   rinv[:, ju % 2, t:t + 1].to_broadcast([P, P]), k.ident[:])
                elif name == "o":
                    pe.wait_ge(opL_rdy, unit + 1)
                    last = mm3(nc, ps[:], wvH[:, slot, :], wvL[:, slot, :], opH[:], opL[:], True, True)
                else:
                    y_half = int(name[0] == "h")
                    w = slice(int(name[1]) * P, (int(name[1]) + 1) * P)
                    for hp in range(2):
                        last = mm3(nc, ps[:], wpH[:, hp, w], wpL[:, hp, w], zH[:, hp, y_half, :], zL[:, hp, y_half, :],
                                   hp == 0, hp == 1)
                last.then_inc(m_ps, 1)

            def scores(j, qt, c):
                half, hp = j % 2, j // 2
                lo_, hi_ = QCHUNKS[c]
                t = slice(qt * P, (qt + 1) * P)
                t2 = slice(half * HALF + qt * P, half * HALF + (qt + 1) * P)
                kc = slice(lo_, hi_)
                out = ps_s[:, kc]
                nc.tensor.matmul(out, qpH[:, half, t], k.cH[:, kc], start=True, stop=False)
                nc.tensor.matmul(out, qpH[:, half, t], k.cL[:, kc], start=False, stop=False)
                nc.tensor.matmul(out, qpL[:, half, t], k.cH[:, kc], start=False, stop=False)
                nc.tensor.matmul(out, q2[hp][:, t2], k.k2H[:, kc], start=False, stop=False)
                nc.tensor.matmul(out, q2[hp][:, t2], k.k2L[:, kc], start=False, stop=True).then_inc(s_chunk[c], 1)

            def turn_weights(v, jv, kt):
                if kt == 0:
                    pe.wait_ge(e_rdy, 4 * (v + 1))
                positive(pe, ptL_rdy, NKT * v + (kt - 1))
                for t in range(QT):
                    last = nc.tensor.transpose(ps_pt[kt % 2][:, t * P:(t + 1) * P],
                                               E[:, jv % 2, t, kt * P:(kt + 1) * P], k.ident[:])
                last.then_inc(pt_ps, 1)

            def values(v, kt):
                pe.wait_ge(ptL_rdy, NKT * v + (kt + 1))
                if kt == 0:
                    positive(pe, opL_rdy, v)
                mm3(nc, ps_o[:], k.ctokH[:, kt, :], k.ctokL[:, kt, :], ptH[:, kt % 2, :], ptL[:, kt % 2, :],
                    kt == 0, kt == NKT - 1).then_inc(pv, 1)

            pe.wait_ge(wq_in[0], 32)
            small("turn", 0, 0, slot=0)
            pe.wait_ge(m_free, 1)
            small("absorb", 1, 1)
            pe.wait_ge(m_free, 2)
            small("q", 2, 0, half=0, slot=0)
            pe.wait_ge(wrL_rdy, 2)
            small("rope", 3, 1, half=0)

            def body(i, kind):
                for j in range(4):
                    u = 4 * i + j
                    v, w = u - 1, u - 2
                    has_v = kind != "first" or j > 0
                    has_w = kind != "first" or j > 1

                    def at(name, jj=j):
                        return product_index(i, jj, name, kind)

                    def filler(name):
                        a, b = at(name), product_bank(j, name, kind)
                        if name == "turn":
                            slot = (j // 2 + 1) % 2
                            pe.wait_ge(wq_in[slot], 32 * i + (32 if j == 0 else 64))
                            small(name, a, b, slot=slot)
                        elif name == "absorb":
                            pe.wait_ge(m_free, at("turn") + 1)
                            small(name, a, b)
                        elif name == "q":
                            if j % 2:
                                pe.wait_ge(m_free, at("absorb", j - 1) + 1)
                            small(name, a, b, half=(j + 1) % 2, slot=((j + 1) // 2) % 2)
                        elif name == "rope":
                            pe.wait_ge(wrL_rdy, 2 * i + (2 if j == 0 else 4))
                            small(name, a, b, half=1 if j == 0 else 0)
                        elif name == "o":
                            pe.wait_ge(wvL_rdy, 2 * i + j // 2)
                            small(name, a, b, slot=(j // 2 + 1) % 2, unit=w)
                        elif name == "R":
                            small(name, a, b, unit=w, ju=j)
                        else:
                            if name == "y0":
                                pe.wait_ge(wpL_rdy, 2 * i)
                                pe.wait_ge(z_rdy, 4 * i - 1)
                            if name == "h0":
                                pe.wait_ge(z_rdy, 4 * i)
                            small(name, a, b)

                    for qt in range(QT):
                        n = 4 * u + qt
                        kts = QKT[j][qt] if has_v else ()
                        names = list(unit_products(j, kind)[qt])
                        positive(pe, e_rdy, n)
                        if qt == 0:
                            pe.wait_ge(m_free, at("q", j - 1) + 1 if j else 3 if kind == "first" else at("rope"))
                            if j < 2:
                                pe.wait_ge(q2_rdy, 2 * i + (j + 1))
                        scores(j, qt, 0)
                        if has_v:
                            turn_weights(v, (j - 1) % 4, kts[0])
                        scores(j, qt, 1)
                        if qt == 0 and has_w:
                            values(w, NKT - 1)
                        if qt and has_v:
                            values(v, kts[0] - 1)
                        if has_v:
                            turn_weights(v, (j - 1) % 4, kts[1])
                        scores(j, qt, 2)
                        for name in names[:1]:
                            filler(name)
                        if has_v:
                            values(v, kts[0])
                        for kt in kts[2:]:
                            turn_weights(v, (j - 1) % 4, kt)
                        for name in names[1:2]:
                            filler(name)
                        for kt in kts[2:]:
                            values(v, kt - 1)
                        for name in names[2:]:
                            filler(name)

            bodies(pe, body)
            v = UNITS - 1

            def tail(n):
                last = "last" in TAIL[n]
                small(TAIL[n].split()[0], TAIL0 + n, (TAIL0 + n) % 2, slot=1, unit=v if last else v - 1,
                      ju=3 if last else 2)

            for kt in range(NKT):
                turn_weights(v, 3, kt)
                values(v if kt else v - 1, kt - 1 if kt else NKT - 1)
                if kt in (2, 3):
                    if kt == 3:
                        pe.wait_ge(wvL_rdy, HEADS)
                    tail(kt - 2)
                if kt >= 6:
                    if kt == 6:
                        pe.wait_ge(wpL_rdy, HEADS)
                        pe.wait_ge(z_rdy, UNITS - 1)
                    tail(kt - 4)
            values(v, NKT - 1)
            for n in range(NKT - 4, len(TAIL)):
                if TAIL[n] == "h0":
                    pe.wait_ge(z_rdy, UNITS)
                tail(n)


def stage_output(nc, k):
    with ExitStack() as ctx:
        def sb(name, shape, dt=F32):
            return ctx.enter_context(nc.sbuf_tensor(name, shape, dt))

        def sem(name):
            return ctx.enter_context(nc.semaphore(name))

        yH = sb("yH", [P, KT, SEQ], F32R)
        yL = sb("yL", [P, KT, SEQ], F32R)
        woH = sb("woH", [P, KT, D], F32R)
        woL = sb("woL", [P, KT, D], F32R)
        st = sb("wo_st", [P, D])
        br = sb("br", [P, 2, SEQ])
        gate = sb("gate", [P, D])
        fg = sb("fg", [P, D])
        xr = sb("xr", [P, D])
        res = sb("res", [P, D])
        fsq = sb("fsq", [P, XT, 3])
        ps_r = [ctx.enter_context(nc.psum_tensor(f"ps_r{b}", [P, HALF], F32)) for b in range(4)]
        ps_g = [ctx.enter_context(nc.psum_tensor(f"ps_gt{b}", [P, HALF], F32)) for b in range(2)]
        ps_j = ctx.enter_context(nc.psum_tensor("ps_j", [P, 2 * HALF], F32))

        br_in = [sem("br_in0"), sem("br_in1")]
        wo_in = sem("wo_in")
        fg_in = sem("fg_in")
        xr_in = sem("xr_in")
        br_step = sem("br_step")
        y_rdy = sem("y_rdy")
        yH_rdy = sem("yH_rdy")
        yL_rdy = sem("yL_rdy")
        woH_rdy = sem("woH_rdy")
        woL_rdy = sem("woL_rdy")
        gt_ps = sem("gt_ps")
        gt_rdy = sem("gt_rdy")
        r_ps = sem("r_ps")
        r_read = sem("r_read")
        r_step = sem("r_step")
        sq_rdy = sem("sq_rdy")
        rt_rdy = sem("rt_rdy")
        ri_rdy = sem("ri_rdy")
        res_rdy = sem("res_rdy")
        out_done = sem("out_done")

        block = ctx.enter_context(nc.Block())

        @block.sync
        def _(sp):
            for kt in range(KT):
                if kt:
                    sp.wait_ge(y_rdy, kt)
                sp.dma_start(br[:, 0, :], k.th_d[kt]).then_inc(br_in[0], 16)
                sp.dma_start(br[:, 1, :], k.yp_d[kt]).then_inc(br_in[1], 16)
                if kt:
                    sp.wait_ge(woL_rdy, kt)
                sp.dma_start(st[:], k.w_out[kt * P:(kt + 1) * P, :]).then_inc(wo_in, 16)
            sp.dma_start(fg[:], k.final_g.to_broadcast([P, D])).then_inc(fg_in, 16)
            for t in range(XT):
                if t:
                    sp.wait_ge(r_step, 2 * t)
                sp.dma_start(xr[:], k.x[t * P:(t + 1) * P, :]).then_inc(xr_in, 16)
                if t:
                    sp.wait_ge(res_rdy, t)
                    sp.dma_start(k.out[(t - 1) * P:t * P, :], res[:]).then_inc(out_done, 16)
            sp.wait_ge(res_rdy, XT)
            sp.dma_start(k.out[(XT - 1) * P:XT * P, :], res[:]).then_inc(out_done, 16)
            sp.wait_ge(out_done, 16 * XT)

        @block.gpsimd
        def _(pool):
            for kt in range(KT):
                pool.wait_ge(woH_rdy, kt + 1)
                nc.gpsimd.tensor_tensor(woL[:, kt, :], st[:], woH[:, kt, :].bitcast(F32), ALU.subtract
                                        ).then_inc(woL_rdy, 1)

        @block.scalar
        def _(act):
            for kt in range(KT):
                act.wait_ge(wo_in, 16 * (kt + 1))
                nc.scalar.activation(woH[:, kt, :], st[:], ACT.Copy).then_inc(woH_rdy, 1)
                act.wait_ge(y_rdy, kt + 1)
                nc.scalar.activation(yH[:, kt, :], k.yacc[:, kt, :], ACT.Copy).then_inc(yH_rdy, 1)
            for t in range(XT):
                act.wait_ge(r_step, 2 * (t + 1))
                nc.scalar.activation(ps_j[:], res[:], ACT.Square, accum_out=fsq[:, t, 0:1]).then_inc(sq_rdy, 1)
                act.wait_ge(sq_rdy, t + 1)
                nc.scalar.activation(fsq[:, t, 1:2], fsq[:, t, 0:1], ACT.Sqrt, scale=1.0 / D, bias=k.eps[:, 0:1]
                                     ).then_inc(rt_rdy, 1)

        @block.vector
        def _(dve):
            for kt in range(KT):
                t = k.yacc[:, kt, :]
                dve.wait_ge(br_in[0], 16 * (kt + 1))
                nc.vector.scalar_tensor_tensor(out=t, in0=br[:, 0, :], scalar=1.0, in1=t, op0=ALU.add,
                                               op1=ALU.mult).then_inc(br_step, 1)
                dve.wait_ge(br_in[1], 16 * (kt + 1))
                dve.wait_ge(br_step, kt + 1)
                nc.vector.tensor_tensor(t, t, br[:, 1, :], ALU.add).then_inc(y_rdy, 1)
                dve.wait_ge(yH_rdy, kt + 1)
                nc.vector.tensor_tensor(yL[:, kt, :], t, yH[:, kt, :].bitcast(F32), ALU.subtract).then_inc(yL_rdy, 1)
            for h in range(2):
                dve.wait_ge(gt_ps, h + 1)
                nc.vector.tensor_scalar(gate[:, h * HALF:(h + 1) * HALF], ps_g[h][:], 0.5, None, ALU.mult
                                        ).then_inc(gt_rdy, 1)
            dve.wait_ge(gt_rdy, 2)
            for t in range(XT):
                if t:
                    dve.wait_ge(out_done, 16 * t)
                for h in range(2):
                    dve.wait_ge(r_ps, 2 * t + h + 1)
                    c = slice(h * HALF, (h + 1) * HALF)
                    nc.vector.tensor_tensor(res[:, c], ps_r[(2 * t + h) % 4][:], gate[:, c], ALU.mult
                                            ).then_inc(r_read, 1)
                    dve.wait_ge(r_read, 2 * t + h + 1)
                    if h == 0:
                        dve.wait_ge(xr_in, 16 * (t + 1))
                    nc.vector.tensor_tensor(res[:, c], res[:, c], xr[:, c], ALU.add).then_inc(r_step, 1)
                if t == 0:
                    dve.wait_ge(fg_in, 16)
                dve.wait_ge(rt_rdy, t + 1)
                nc.vector.reciprocal(fsq[:, t, 2:3], fsq[:, t, 1:2]).then_inc(ri_rdy, 1)
                dve.wait_ge(ri_rdy, t + 1)
                nc.vector.scalar_tensor_tensor(out=res[:], in0=res[:], scalar=fsq[:, t, 2:3], in1=fg[:],
                                               op0=ALU.mult, op1=ALU.mult).then_inc(res_rdy, 1)

        @block.tensor
        def _(pe):
            for h in range(2):
                for f in range(QT):
                    ft = h * QT + f
                    last = nc.tensor.transpose(ps_g[h][:, f * P:(f + 1) * P],
                                               k.gateT[:, ft:ft + 1].to_broadcast([P, P]), k.ident[:])
                last.then_inc(gt_ps, 1)
            for t in range(XT):
                for h in range(2):
                    n = 2 * t + h
                    if n >= 4:
                        pe.wait_ge(r_read, n - 3)
                    for kt in range(KT):
                        if n == 0:
                            pe.wait_ge(yL_rdy, kt + 1)
                            pe.wait_ge(woL_rdy, kt + 1)
                        ts, c = slice(t * P, (t + 1) * P), slice(h * HALF, (h + 1) * HALF)
                        last = mm3(nc, ps_r[n % 4][:], yH[:, kt, ts], yL[:, kt, ts], woH[:, kt, c], woL[:, kt, c],
                                   kt == 0, kt == KT - 1)
                    last.then_inc(r_ps, 1)


def build_program(nc, k):
    with ExitStack() as ctx:
        def sb(name, shape, dt=F32):
            return ctx.enter_context(nc.sbuf_tensor(name, shape, dt))

        k.ident = sb("ident", [P, P])
        k.vt = sb("vt", [P, R_END])
        k.eps = sb("eps", [P, 1])
        k.qgs = sb("qgs", [P, QLT])
        k.bgh = sb("bgh", [P, 2 * KT])
        k.gateT = sb("gateT", [P, KT])
        with ExitStack() as latents:
            def lat(name, shape, dt=F32R):
                return latents.enter_context(nc.sbuf_tensor(name, shape, dt))

            k.qnH = lat("qnH", [P, QLT, SEQ])
            k.qnL = lat("qnL", [P, QLT, SEQ])
            k.cH = lat("cH", [P, KEYS])
            k.cL = lat("cL", [P, KEYS])
            k.k2H = lat("k2H", [P, KEYS])
            k.k2L = lat("k2L", [P, KEYS])
            k.ctokH = lat("ctokH", [P, NKT, KVL])
            k.ctokL = lat("ctokL", [P, NKT, KVL])
            with ExitStack() as early:
                k.hH = early.enter_context(nc.sbuf_tensor("hH", [P, KT, SEQ], F32R))
                k.hL = early.enter_context(nc.sbuf_tensor("hL", [P, KT, SEQ], F32R))
                stage_tokens(nc, k)
                stage_gates(nc, k)
            k.yacc = ctx.enter_context(nc.sbuf_tensor("yacc", [P, KT, SEQ], F32, side="right"))
            stage_attention(nc, k)
        stage_output(nc, k)


def rope_tables():
    import numpy as np
    half = ROPE // 2
    inv = (1.0 / (np.float32(10000.0) ** (np.arange(0, half, 2, dtype=np.float32) / np.float32(half)))).astype(np.float32)
    t = np.arange(SEQ)
    ang = np.concatenate([(t // 64).astype(np.float32)[:, None] * inv, (t % 64).astype(np.float32)[:, None] * inv], axis=1)
    cos, sin = np.cos(ang).astype(np.float32), np.sin(ang).astype(np.float32)
    q_cos = np.tile(cos.T, (P // RH, 1))
    q_sin = np.concatenate([-sin.T, sin.T] * (P // ROPE), axis=0)
    return cos, sin, np.ascontiguousarray(q_cos), np.ascontiguousarray(q_sin)


def pool_counts():
    import numpy as np
    t = np.arange(SEQ)
    rows = [1.0 / (np.clip(t + w // 2, 0, SEQ) - np.clip(t - w // 2, 0, SEQ)).astype(np.float32) for w in WINDOWS]
    return np.stack(rows).astype(np.float32)


def kernel(x, c, ctx, c_ctx, ada_w, ada_b, norm_g, w_in, b_gate, w_pool, pool_scale, q_norm_g, w_qb,
           kv_norm_g, w_kvb, w_proj_pool, w_proj_mla, w_out, final_g):
    import numpy as np
    import concourse.bacc as bacc
    from concourse.bass_utils import run_bass_kernel_spmd

    nc = bacc.Bacc("TRN2", target_bir_lowering=False, num_devices=1)
    cos, sin, q_cos, q_sin = rope_tables()
    arrays = {
        "x": np.asarray(x).reshape(SEQ, D), "ctx": np.asarray(ctx).reshape(CTX, D),
        "c": np.asarray(c).reshape(KT, P), "c_ctx": np.asarray(c_ctx).reshape(KT, P),
        "ada_w": np.asarray(ada_w)[0], "ada_b": np.asarray(ada_b).reshape(3 * KT, P),
        "norm_g": np.asarray(norm_g).reshape(KT, P), "w_in": np.asarray(w_in)[0],
        "b_gate": np.asarray(b_gate).reshape(2 * KT, P), "w_pool": np.asarray(w_pool)[0],
        "pool_scale": np.asarray(pool_scale).reshape(KT, P), "q_norm_g": np.asarray(q_norm_g).reshape(QLT, P),
        "w_qb": np.asarray(w_qb)[0], "kv_norm_g": np.asarray(kv_norm_g).reshape(1, KVL),
        "w_kvb": np.asarray(w_kvb)[0], "w_proj_pool": np.asarray(w_proj_pool)[0],
        "w_proj_mla": np.asarray(w_proj_mla)[0], "w_out": np.asarray(w_out)[0],
        "final_g": np.asarray(final_g).reshape(1, D),
        "ident_d": np.eye(P, dtype=np.float32), "kcos_d": cos, "ksin_d": sin, "qcos_d": q_cos, "qsin_d": q_sin,
        "pool_inv": pool_counts(),
    }
    arrays = {n: np.ascontiguousarray(a) for n, a in arrays.items()}
    k = Chip()
    for n, a in arrays.items():
        k.__dict__[n] = nc.dram_tensor("in_" + n, a.shape, F32, kind="ExternalInput").ap()
    k.out = nc.dram_tensor("out", (SEQ, D), F32, kind="ExternalOutput").ap()
    k.sg_d = nc.dram_tensor("sg_scratch", (HEADS, P, SEQ), F32, kind="Internal").ap()
    k.yp_d = nc.dram_tensor("yp_scratch", (KT, P, SEQ), F32, kind="Internal").ap()
    k.thp_d = nc.dram_tensor("thp_scratch", (KT, P, SEQ), F32, kind="Internal").ap()
    k.th_d = nc.dram_tensor("th_scratch", (KT, P, SEQ), F32, kind="Internal").ap()
    build_program(nc, k)
    result = run_bass_kernel_spmd(nc, [{"in_" + n: a for n, a in arrays.items()}], core_ids=[0]).results[0]["out"]
    return result.reshape(1, SEQ, D)
```

```python
from contextlib import ExitStack

import concourse.bass as bass
from concourse import mybir

F32 = mybir.dt.float32
F32R = mybir.dt.float32r
BF16 = mybir.dt.bfloat16
ACT = mybir.ActivationFunctionType
ALU = mybir.AluOpType
AX_X = mybir.AxisListType.X

P = 128
D = 1024
KT = D // P
SEQ = 1024
CTX = 256
XT = SEQ // P
CT = CTX // P
KEYS = SEQ + CTX
NKT = KEYS // P
HALF = 512
NHALF = SEQ // HALF
QT = HALF // P
HEADS = 16
PAIRS = HEADS // 2
NOPE = 128
ROPE = 64
RH = ROPE // 2
VD = 128
QL = 256
QLT = QL // P
KVL = 128
LORA = QL + KVL + ROPE
MLA = HEADS * VD
WINDOWS = (2, 4, 8, 16)
GROUPS = len(WINDOWS)
PAD = max(WINDOWS) // 2
UW = SEQ + 2 * PAD
EPS = 1e-6
SCALE = float(NOPE + ROPE) ** -0.5

O_U = 0
O_GP = O_U + D
O_QA = O_GP + D
O_KV = O_QA + QL
O_GM = O_KV + KVL + ROPE
O_MP = O_GM + MLA
O_MM = O_MP + D

R_ADAB, R_NG, R_BG, R_PS, R_QG, R_C, R_CC, R_END = 0, 24, 32, 48, 56, 58, 66, 74


class Chip:
    pass


def mm3(nc, out, ah, al, bh, bl, first, last):
    nc.tensor.matmul(out, ah, bh, start=first, stop=False)
    nc.tensor.matmul(out, ah, bl, start=False, stop=False)
    return nc.tensor.matmul(out, al, bh, start=False, stop=last)


def loaded_as(nc, ctx, raw_name, name, shape):
    with nc.sbuf_tensor(raw_name, shape, F32) as raw:
        pass
    return raw, ctx.enter_context(nc.sbuf_tensor(name, shape, F32R))


def unit_half(nc, k, out, slot, h):
    c = slice(h * HALF, (h + 1) * HALF)
    for kt in range(KT):
        w = slice(kt * P, (kt + 1) * P)
        last = mm3(nc, out[:], k.wH[:, slot, w], k.wL[:, slot, w], k.hH[:, kt, c], k.hL[:, kt, c], kt == 0,
                   kt == KT - 1)
    return last


def split_weights(nc, k, slot, n):
    nc.gpsimd.wait_ge(k.w_in_sem[slot], (n - slot) * 8 + 16)
    nc.gpsimd.tensor_copy(k.wH[:, slot, :], k.wst[:, slot, :]).then_inc(k.wH_rdy, 1)
    nc.gpsimd.wait_ge(k.wH_rdy, n + 1)
    nc.gpsimd.tensor_tensor(k.wL[:, slot, :], k.wst[:, slot, :], k.wH[:, slot, :].bitcast(F32),
                            ALU.subtract).then_inc(k.wL_rdy, 1)


def stage_tokens(nc, k):
    GT = [(0, QT), (QT, QT), (XT, CT)]
    NG = len(GT)
    XB = 3
    XS = 6
    AS = 4
    assert XT + CT - XS == GT[0][1]
    with ExitStack() as ctx:
        def sb(name, shape, dt=F32):
            return ctx.enter_context(nc.sbuf_tensor(name, shape, dt))

        def sem(name):
            return ctx.enter_context(nc.semaphore(name))

        with ExitStack() as place:
            k.wH, k.wL = (place.enter_context(nc.sbuf_tensor(n, [P, 2, D], F32R)) for n in ("wH", "wL"))
        xs = sb("xs", [P, XS, D])
        vecs = sb("vecs", [R_END, P])
        junk = sb("junk", [P, D], BF16)
        wlH = sb("wlH", [P, KT, LORA], F32R)
        wl_raw, wlL = loaded_as(nc, ctx, "wl_raw", "wlL", [P, KT, LORA])
        vec4, hcH = loaded_as(nc, ctx, "vec4", "hcH", [P, KT, CTX])
        hcL = sb("hcL", [P, KT, CTX], F32R)
        htmp = sb("htmp", [P, 2, HALF])
        kcos = sb("kcos", [P, XT, RH])
        ksin = sb("ksin", [P, XT, RH])
        kvg = sb("kvg", [P, KVL])
        condT = sb("condT", [P, 2 * KT])
        cond = k.cond
        cond4 = sb("cond4", [P, KT, 4], F32R)
        modp = sb("modp", [P, 2 * KT, 2])
        mod = sb("mod", [P, 2 * KT, 2])
        gain = sb("gain", [P, KT, 2])
        ssq = sb("ssq", [P, XT + CT])
        rst = sb("rst", [P, XT + CT])
        rstd = sb("rstd", [P, XT + CT])
        lms = sb("lms", [P, XT + CT, 2])
        lsd = sb("lsd", [P, XT + CT, 2])
        lrs = sb("lrs", [P, XT + CT, 2])
        qn = sb("qn", [P, 2, QL])
        cn = sb("cn", [P, 2, KVL])
        rp1 = sb("rp1", [P, 2, ROPE])
        rp2 = sb("rp2", [P, 2, ROPE])
        kr = sb("kr", [P, 2, ROPE])
        krH = sb("krH", [P, 2, 2, ROPE], F32R)
        krL = sb("krL", [P, 2, 2, ROPE], F32R)

        def pb(name):
            return ctx.enter_context(nc.psum_tensor(name, [P, 512], F32))

        ps_x, ps_p = k.bank[0:2], k.bank[2:4]
        ps_ada = pb("ps_ada")
        ps_t = pb("ps_t")
        ps_u = pb("ps_u")
        ps_v = pb("ps_v")
        ps_x = ps_x + [ps_v]
        ps_row = [ps_p[0], ps_p[1], ps_t, ps_u]

        vec_in = sem("vec_in")
        tab_in = sem("tab_in")
        ada_in = [sem(f"ada_in{j}") for j in range(AS)]
        x_in = [sem(f"x_in{j}") for j in range(XS)]
        wl_in = sem("wl_in")
        vt_ps = sem("vt_ps")
        vt_rdy = sem("vt_rdy")
        th_rdy = sem("th_rdy")
        cond_rdy = sem("cond_rdy")
        ada_used = sem("ada_used")
        cond4H_rdy = sem("cond4H_rdy")
        cond4_rdy = sem("cond4_rdy")
        adaH_rdy = sem("adaH_rdy")
        adaL_rdy = sem("adaL_rdy")
        row_act = sem("row_act")
        row_dve = sem("row_dve")
        ada_ps = sem("ada_ps")
        modp_rdy = sem("modp_rdy")
        mod_rdy = sem("mod_rdy")
        gain_rdy = sem("gain_rdy")
        ssq_rdy = sem("ssq_rdy")
        rst_rdy = sem("rst_rdy")
        rstd_rdy = sem("rstd_rdy")
        xn_rdy = sem("xn_rdy")
        x_ps = sem("x_ps")
        hH_rdy = sem("hH_rdy")
        ht_rdy = sem("ht_rdy")
        hL_rdy = sem("hL_rdy")
        wlH_rdy = sem("wlH_rdy")
        wlL_rdy = sem("wlL_rdy")
        p_ps = sem("p_ps")
        lms_rdy = sem("lms_rdy")
        lsd_rdy = sem("lsd_rdy")
        lrs_rdy = sem("lrs_rdy")
        rope_step = sem("rope_step")
        lat_rdy = sem("lat_rdy")
        latH_rdy = sem("latH_rdy")
        latL_rdy = sem("latL_rdy")
        t_ps = sem("t_ps")
        tH_rdy = sem("tH_rdy")
        tL_rdy = sem("tL_rdy")

        block = ctx.enter_context(nc.Block())

        def x_tile(t):
            return k.x[t * P:(t + 1) * P, :] if t < XT else k.ctx[(t - XT) * P:(t - XT + 1) * P, :]

        def hslice(g, ft):
            t0, n = GT[g]
            if t0 < XT:
                return k.hH[:, ft, t0 * P:(t0 + n) * P], k.hL[:, ft, t0 * P:(t0 + n) * P], n * P
            return hcH[:, ft, :], hcL[:, ft, :], n * P

        def ada_slot(t, kt):
            s = kt % AS
            return t[:, 2 * s:2 * s + 2, :].rearrange("p a b -> p (a b)")

        @block.sync
        def _(sp):
            rows = [(k.c, R_C), (k.c_ctx, R_CC), (k.ada_b, R_ADAB), (k.norm_g, R_NG), (k.b_gate, R_BG),
                    (k.pool_scale, R_PS), (k.q_norm_g, R_QG)]

            def ada_rows(kt):
                if kt >= AS:
                    sp.wait_ge(ada_used, kt - AS + 1)
                sp.dma_start(ada_slot(k.h_raw, kt), k.ada_w[kt * P:(kt + 1) * P, 0:2 * D]).then_inc(ada_in[kt % AS], 16)

            def tokens(t):
                sp.dma_start(xs[:, t % XS, :], x_tile(t)).then_inc(x_in[t % XS], 16)

            ada_rows(0)
            sp.dma_start(k.ident[:], k.ident_d).then_inc(vec_in, 16)
            for v, r in rows:
                sp.dma_start(vecs[r:r + v.shape[0], :], v).then_inc(vec_in, 16)
            ada_rows(1)
            for t in (0, 1):
                tokens(t)
            ada_rows(2)
            for t in (2, 3):
                tokens(t)
            for kt in range(3, KT):
                ada_rows(kt)
            sp.dma_start(wl_raw[:], k.w_in[:, O_QA:O_QA + LORA].rearrange("(a p) n -> p a n", p=P)).then_inc(wl_in, 16)
            for t in range(QT, XS):
                tokens(t)
            sp.dma_start(kcos[:], k.kcos_d.rearrange("(t p) d -> p t d", p=P)).then_inc(tab_in, 16)
            sp.dma_start(ksin[:], k.ksin_d.rearrange("(t p) d -> p t d", p=P)).then_inc(tab_in, 16)
            sp.dma_start(kvg[:], k.kv_norm_g.to_broadcast([P, KVL])).then_inc(tab_in, 16)
            sp.wait_ge(x_ps, KT)
            for t in range(XS, XT + CT):
                tokens(t)
            for n in range(2):
                sp.dma_start(k.wst[:, n, :].rearrange("p (a n) -> p a n", a=KT),
                             k.w_in[:, O_U + n * P:O_U + (n + 1) * P].rearrange("(a p) n -> p a n", p=P)
                             ).then_inc(k.w_in_sem[n], 16)

        @block.scalar
        def _(act):
            def ada_hi(kt):
                act.wait_ge(ada_in[kt % AS], 16 * (kt // AS + 1))
                nc.scalar.activation(ada_slot(k.hH, kt), ada_slot(k.h_raw, kt), ACT.Copy).then_inc(adaH_rdy, 1)

            def square(t):
                act.wait_ge(x_in[t % XS], 16 * (t // XS + 1))
                if t:
                    act.wait_ge(ssq_rdy, t)
                nc.scalar.activation(junk[:], xs[:, t % XS, :], ACT.Square, accum_out=ssq[:, t:t + 1]
                                     ).then_inc(ssq_rdy, 1)

            def root(g):
                t0, n = GT[g]
                act.wait_ge(ssq_rdy, t0 + n)
                nc.scalar.activation(rst[:, t0:t0 + n], ssq[:, t0:t0 + n], ACT.Sqrt, scale=1.0 / D,
                                     bias=k.eps[:, 0:1]).then_inc(rst_rdy, 1)

            def token_stats(g):
                t0, n = GT[g]
                for t in range(t0, t0 + n):
                    square(t)
                root(g)

            def modulate(g):
                if g == 0:
                    act.wait_ge(gain_rdy, 1)
                    act.wait_ge(wl_in, 16)
                for ft in range(KT):
                    act.wait_ge(x_ps, KT * g + ft + 1)
                    hi, _, n = hslice(g, ft)
                    j = int(g == NG - 1)
                    nc.scalar.activation(hi, ps_x[(KT * g + ft) % XB][:, 0:n], ACT.Identity, scale=gain[:, ft, j:j + 1],
                                         bias=mod[:, ft, j:j + 1]).then_inc(hH_rdy, 1)
                    if g == 0:
                        nc.scalar.activation(wlH[:, ft, :], wl_raw[:, ft, :], ACT.Copy).then_inc(wlH_rdy, 1)

            def latent_stats(t):
                act.wait_ge(p_ps, t + 1)
                ps = ps_p[t % 2]
                n = 2 * t if t < XT else 2 * XT + (t - XT)
                if t < XT:
                    act.wait_ge(lms_rdy, n) if n else None
                    nc.scalar.activation(junk[:, 0:QL], ps[:, 0:QL], ACT.Square, scale=QL ** -0.5,
                                         accum_out=lms[:, t, 0:1]).then_inc(lms_rdy, 1)
                    n += 1
                    c0 = QL
                else:
                    c0 = 0
                act.wait_ge(lms_rdy, n)
                nc.scalar.activation(junk[:, 0:KVL], ps[:, c0:c0 + KVL], ACT.Square, scale=KVL ** -0.5,
                                     accum_out=lms[:, t, 1:2]).then_inc(lms_rdy, 1)
                act.wait_ge(lms_rdy, n + 1)
                a = 0 if t < XT else 1
                nc.scalar.activation(lsd[:, t, a:2], lms[:, t, a:2], ACT.Sqrt, bias=k.eps[:, 0:1]).then_inc(lsd_rdy, 1)

            def latent_hi(t):
                act.wait_ge(lat_rdy, t + 1)
                if t >= 2:
                    act.wait_ge(t_ps, t - 1)
                nc.scalar.activation(k.ctokH[:, t, :], cn[:, t % 2, :], ACT.Copy)
                nc.scalar.activation(krH[:, t % 2, :, :], kr[:, t % 2, :].unsqueeze(1).to_broadcast([P, 2, ROPE]),
                                     ACT.Copy).then_inc(latH_rdy, 1)

            def latent_T_hi(t):
                act.wait_ge(t_ps, t + 1)
                c = slice(t * P, (t + 1) * P)
                if t < XT:
                    for i in range(QLT):
                        nc.scalar.activation(k.qnH[:, i, c], ps_t[:, i * P:(i + 1) * P], ACT.Copy,
                                             scale=k.qgs[:, i:i + 1])
                nc.scalar.activation(k.k2H[:, c], ps_t[:, 3 * P:4 * P], ACT.Copy)
                nc.scalar.activation(k.cH[:, c], ps_t[:, 2 * P:3 * P], ACT.Copy).then_inc(tH_rdy, 1)

            ada_hi(0)
            act.wait_ge(vt_rdy, 1)
            nc.scalar.activation(condT[:], k.vt[:, R_C:R_END], ACT.Tanh, scale=0.5).then_inc(th_rdy, 1)
            act.wait_ge(cond_rdy, 1)
            nc.scalar.activation(cond4[:, :, 0:2], cond[:], ACT.Copy).then_inc(cond4H_rdy, 1)
            ada_hi(1)
            for t in (0, 1):
                square(t)
            ada_hi(2)
            for t in (2, 3):
                square(t)
            root(0)
            for kt in range(3, KT):
                ada_hi(kt)
            act.wait_ge(ada_used, KT)
            for c in range(2):
                last = nc.scalar.activation(vec4[0:4, :, :].rearrange("p a b -> p (a b)")[:, c * HALF:(c + 1) * HALF],
                                            ps_row[c][0:4, :], ACT.Copy)
            last.then_inc(row_act, 1)
            modulate(0)
            token_stats(1)
            for t in range(XT + CT):
                if t == 2:
                    modulate(1)
                    token_stats(2)
                if t == 5:
                    modulate(2)
                latent_stats(t)
                if t:
                    latent_T_hi(t - 1)
                latent_hi(t)
            latent_T_hi(XT + CT - 1)

        @block.vector
        def _(dve):
            nc.vector.memset(k.eps[:], EPS)
            dve.wait_ge(vt_ps, 1)
            nc.vector.tensor_copy(k.vt[:, 0:R_END], ps_v[:, 0:R_END]).then_inc(vt_rdy, 1)
            dve.wait_ge(th_rdy, 1)
            nc.vector.scalar_tensor_tensor(out=cond[:].rearrange("p a j -> p j a"),
                                           in0=condT[:].rearrange("p (j a) -> p j a", j=2), scalar=1.0,
                                           in1=k.vt[:, R_C:R_END].rearrange("p (j a) -> p j a", j=2),
                                           op0=ALU.add, op1=ALU.mult).then_inc(cond_rdy, 1)
            dve.wait_ge(cond4H_rdy, 1)
            nc.vector.tensor_tensor(cond4[:, :, 2:4], cond[:], cond4[:, :, 0:2].bitcast(F32), ALU.subtract
                                    ).then_inc(cond4_rdy, 1)
            nc.vector.tensor_scalar(k.qgs[:], k.vt[:, R_QG:R_QG + QLT], SCALE, None, ALU.mult)
            nc.vector.tensor_scalar(k.bgh[:], k.vt[:, R_BG:R_BG + 2 * KT], 0.5, None, ALU.mult)

            def normalise(g):
                t0, n = GT[g]
                dve.wait_ge(rst_rdy, g + 1)
                nc.vector.reciprocal(rstd[:, t0:t0 + n], rst[:, t0:t0 + n]).then_inc(rstd_rdy, 1)
                dve.wait_ge(rstd_rdy, g + 1)
                for j in range(n):
                    nc.vector.tensor_scalar(xs[:, (t0 + j) % XS, :], xs[:, (t0 + j) % XS, :], rstd[:, t0 + j:t0 + j + 1], None,
                                            ALU.mult).then_inc(xn_rdy, 1)

            def modulate(g):
                for ft in range(KT):
                    i = KT * g + ft
                    dve.wait_ge(x_ps, i + 1)
                    dve.wait_ge(hH_rdy, i + 1)
                    if i >= 2:
                        dve.wait_ge(hL_rdy, i - 1)
                    _, _, n = hslice(g, ft)
                    j = int(g == NG - 1)
                    nc.vector.tensor_scalar(htmp[:, ft % 2, 0:n], ps_x[i % XB][:, 0:n], gain[:, ft, j:j + 1],
                                            mod[:, ft, j:j + 1], ALU.mult, ALU.add).then_inc(ht_rdy, 1)
                    if g == 0:
                        dve.wait_ge(wlH_rdy, ft + 1)
                        nc.vector.tensor_tensor(wlL[:, ft, :], wl_raw[:, ft, :], wlH[:, ft, :].bitcast(F32),
                                                ALU.subtract).then_inc(wlL_rdy, 1)

            def latents(t):
                s = t % 2
                a = 0 if t < XT else 1
                ps = ps_p[s]
                c0 = QL if t < XT else 0
                dve.wait_ge(lsd_rdy, t + 1)
                nc.vector.reciprocal(lrs[:, t, a:2], lsd[:, t, a:2]).then_inc(lrs_rdy, 1)
                if t >= 2:
                    dve.wait_ge(t_ps, t - 1)
                dve.wait_ge(lrs_rdy, t + 1)
                if t < XT:
                    nc.vector.tensor_scalar(qn[:, s, :], ps[:, 0:QL], lrs[:, t, 0:1], None, ALU.mult)
                if t == 0:
                    dve.wait_ge(tab_in, 48)
                nc.vector.scalar_tensor_tensor(out=cn[:, s, :], in0=ps[:, c0:c0 + KVL], scalar=lrs[:, t, 1:2],
                                               in1=kvg[:], op0=ALU.mult, op1=ALU.mult)
                raw = ps[:, c0 + KVL:c0 + KVL + ROPE].rearrange("p (a b c) -> p b a c", a=2, b=2)

                def half(tile, b):
                    return tile[:, s, b * RH:(b + 1) * RH].rearrange("p (a c) -> p a c", a=2)

                if t < XT:
                    cs = kcos[:, t, :].rearrange("p (a c) -> p a c", a=2)
                    sn = ksin[:, t, :].rearrange("p (a c) -> p a c", a=2)
                    for b in range(2):
                        nc.vector.tensor_tensor(half(rp1, b), raw[:, b], cs, ALU.mult)
                        last = nc.vector.tensor_tensor(half(rp2, b), raw[:, 1 - b], sn, ALU.mult)
                    last.then_inc(rope_step, 1)
                    dve.wait_ge(rope_step, t + 1)
                    nc.vector.tensor_tensor(kr[:, s, 0:RH], rp1[:, s, 0:RH], rp2[:, s, 0:RH], ALU.subtract)
                    nc.vector.tensor_tensor(kr[:, s, RH:ROPE], rp1[:, s, RH:ROPE], rp2[:, s, RH:ROPE],
                                            ALU.add).then_inc(lat_rdy, 1)
                else:
                    nc.vector.tensor_copy(half(kr, 0), raw[:, 0])
                    nc.vector.tensor_copy(half(kr, 1), raw[:, 1]).then_inc(lat_rdy, 1)

            def latents_lo(t):
                s = t % 2
                dve.wait_ge(latH_rdy, t + 1)
                nc.vector.tensor_tensor(k.ctokL[:, t, :], cn[:, s, :], k.ctokH[:, t, :].bitcast(F32), ALU.subtract)
                nc.vector.tensor_tensor(krL[:, s, :, :], kr[:, s, :].unsqueeze(1).to_broadcast([P, 2, ROPE]),
                                        krH[:, s, :, :].bitcast(F32), ALU.subtract).then_inc(latL_rdy, 1)

            def latents_T_lo(t):
                c = slice(t * P, (t + 1) * P)
                dve.wait_ge(tH_rdy, t + 1)
                if t < XT:
                    for i in range(QLT):
                        nc.vector.scalar_tensor_tensor(out=k.qnL[:, i, c], in0=ps_t[:, i * P:(i + 1) * P],
                                                       scalar=k.qgs[:, i:i + 1], in1=k.qnH[:, i, c].bitcast(F32),
                                                       op0=ALU.mult, op1=ALU.subtract)
                nc.vector.tensor_copy(k.k2L[:, c], ps_u[:, 0:P])
                nc.vector.tensor_tensor(k.cL[:, c], ps_t[:, 2 * P:3 * P], k.cH[:, c].bitcast(F32),
                                        ALU.subtract).then_inc(tL_rdy, 1)

            for kt in range(KT):
                if kt == 3:
                    normalise(0)
                dve.wait_ge(adaH_rdy, kt + 1)
                nc.vector.tensor_tensor(ada_slot(k.hL, kt), ada_slot(k.h_raw, kt), ada_slot(k.hH, kt).bitcast(F32),
                                        ALU.subtract).then_inc(adaL_rdy, 1)
            dve.wait_ge(ada_used, KT)
            for c in range(2, 4):
                last = nc.vector.tensor_copy(vec4[0:4, :, :].rearrange("p a b -> p (a b)")[:, c * HALF:(c + 1) * HALF],
                                             ps_row[c][0:4, :])
            last.then_inc(row_dve, 1)
            dve.wait_ge(ada_ps, 1)
            b = k.vt[:, R_ADAB:R_ADAB + 2 * KT].unsqueeze(2).to_broadcast([P, 2 * KT, 2])
            parts = ps_ada[:, 0:8 * KT].rearrange("p (a h j) -> p a h j", h=2, j=2)
            nc.vector.tensor_copy(modp[:], parts[:, :, 1]).then_inc(modp_rdy, 1)
            dve.wait_ge(modp_rdy, 1)
            nc.vector.tensor_tensor(modp[:], modp[:], parts[:, :, 0], ALU.add).then_inc(modp_rdy, 1)
            dve.wait_ge(modp_rdy, 2)
            nc.vector.scalar_tensor_tensor(out=mod[:], in0=modp[:],
                                           scalar=0.5, in1=b, op0=ALU.mult, op1=ALU.add).then_inc(mod_rdy, 1)
            dve.wait_ge(mod_rdy, 1)
            nc.vector.scalar_tensor_tensor(out=gain[:], in0=mod[:, KT:2 * KT, :], scalar=1.0,
                                           in1=k.vt[:, R_NG:R_NG + KT].unsqueeze(2).to_broadcast([P, KT, 2]),
                                           op0=ALU.add, op1=ALU.mult).then_inc(gain_rdy, 1)
            dve.wait_ge(gain_rdy, 1)
            modulate(0)
            normalise(1)
            for t in range(XT + CT):
                if t == 2:
                    modulate(1)
                    normalise(2)
                if t == 5:
                    modulate(2)
                latents(t)
                if t:
                    latents_T_lo(t - 1)
                latents_lo(t)
            latents_T_lo(XT + CT - 1)

        @block.gpsimd
        def _(pool):
            def modulated_lo(g):
                for ft in range(KT):
                    i = KT * g + ft
                    pool.wait_ge(ht_rdy, i + 1)
                    hi, lo, n = hslice(g, ft)
                    nc.gpsimd.tensor_tensor(lo, htmp[:, ft % 2, 0:n], hi.bitcast(F32), ALU.subtract
                                            ).then_inc(hL_rdy, 1)

            for g in range(NG):
                modulated_lo(g)
            pool.wait_ge(x_ps, NG * KT)
            for n in range(2):
                split_weights(nc, k, n, n)

        @block.tensor
        def _(pe):
            pe.wait_ge(vec_in, 16 * 8)
            nc.tensor.transpose(ps_v[:, 0:R_END], vecs[:], k.ident[0:R_END, 0:R_END]).then_inc(vt_ps, 1)
            pe.wait_ge(cond4_rdy, 1)
            for kt in range(KT):
                pe.wait_ge(adaL_rdy, kt + 1)
                for c in range(4):
                    cc = slice(c * HALF, (c + 1) * HALF)
                    nc.tensor.matmul(ps_row[c][0:4, :], cond4[:, kt, :], ada_slot(k.hH, kt)[:, cc], start=(kt == 0),
                                     stop=False)
                    last = nc.tensor.matmul(ps_row[c][0:4, :], cond4[:, kt, :], ada_slot(k.hL, kt)[:, cc],
                                            start=False, stop=(kt == KT - 1))
                last.then_inc(ada_used, 1)
            def transposes(g, ft):
                t0, n = GT[g]
                if ft == 0:
                    pe.wait_ge(xn_rdy, t0 + n)
                i = KT * g + ft
                if i >= XB:
                    pe.wait_ge(ht_rdy, i - XB + 1)
                for t in range(t0, t0 + n):
                    last = nc.tensor.transpose(ps_x[i % XB][:, (t - t0) * P:(t - t0 + 1) * P],
                                               xs[:, t % XS, ft * P:(ft + 1) * P], k.ident[:])
                last.then_inc(x_ps, 1)

            def project(t, g=None):
                w = LORA if t < XT else LORA - QL
                hi, lo = (k.hH, k.hL) if t < XT else (hcH, hcL)
                c = slice(t * P, (t + 1) * P) if t < XT else slice((t - XT) * P, (t - XT + 1) * P)
                if t >= 2:
                    pe.wait_ge(lat_rdy, t - 1)
                for kt in range(KT):
                    if t == 0:
                        pe.wait_ge(wlL_rdy, kt + 1)
                        pe.wait_ge(hL_rdy, kt + 1)
                    last = mm3(nc, ps_p[t % 2][:, 0:w], hi[:, kt, c], lo[:, kt, c], wlH[:, kt, LORA - w:],
                               wlL[:, kt, LORA - w:], kt == 0, kt == KT - 1)
                    if kt == KT - 1:
                        last.then_inc(p_ps, 1)
                    if g is not None:
                        transposes(g, kt)

            def turn(t):
                s = t % 2
                pe.wait_ge(latL_rdy, t + 1)
                if t:
                    pe.wait_ge(tL_rdy, t)
                if t < XT:
                    for i in range(QLT):
                        nc.tensor.transpose(ps_t[:, i * P:(i + 1) * P], qn[:, s, i * P:(i + 1) * P], k.ident[:])
                nc.tensor.transpose(ps_t[:, 2 * P:3 * P], cn[:, s, :], k.ident[:])
                nc.tensor.transpose(ps_t[:, 3 * P:4 * P], krH[:, s, :, :].rearrange("p a b -> p (a b)").bitcast(F32),
                                    k.ident[:])
                nc.tensor.transpose(ps_u[:, 0:P], krL[:, s, :, :].rearrange("p a b -> p (a b)").bitcast(F32),
                                    k.ident[:]).then_inc(t_ps, 1)

            for ft in range(XB):
                transposes(0, ft)
            pe.wait_ge(row_act, 1)
            pe.wait_ge(row_dve, 1)
            for o in range(2 * KT):
                last = nc.tensor.transpose(ps_ada[:, 4 * o:4 * o + 4],
                                           vec4[0:4, :, :].rearrange("p a b -> p (a b)")[:, o * P:(o + 1) * P],
                                           k.ident[0:4, 0:4])
            last.then_inc(ada_ps, 1)
            for ft in range(XB, KT):
                transposes(0, ft)
            for t in range(XT + CT):
                if t == QT:
                    pe.wait_ge(hL_rdy, 2 * KT)
                if t == XT:
                    pe.wait_ge(hL_rdy, 3 * KT)
                project(t, {2: 1, 5: 2}.get(t))
                if t:
                    turn(t - 1)
            pe.wait_ge(ht_rdy, NG * KT)
            pe.wait_ge(k.wL_rdy, 1)
            for h in range(2):
                unit_half(nc, k, ps_x[h], 0, h).then_inc((k.half_ps, k.used)[h], 1)
            turn(XT + CT - 1)


EARLY_3 = (("wq_st", [P, 2, QLT, NOPE + ROPE]), ("wkv_st", [P, 2, NOPE + VD]), ("cs", [P, 2, HALF]))


def load_head(nc, k, h, slot):
    nc.sync.dma_start(k.wq_st[:, slot, :, :],
                      k.w_qb[:, bass.ds(h * (NOPE + ROPE), NOPE + ROPE)].rearrange("(a p) n -> p a n", p=P)
                      ).then_inc(k.wq_in[slot], 16)
    nc.sync.dma_start(k.wkv_st[:, slot, :], k.w_kvb[:, bass.ds(h * (NOPE + VD), NOPE + VD)]
                      ).then_inc(k.wq_in[slot], 16)


def load_rope(nc, k, half):
    c = slice(half * HALF, (half + 1) * HALF)
    nc.sync.dma_start(k.cs[:, 0, :], k.qcos_d[:, c]).then_inc(k.cs_in, 16)
    nc.sync.dma_start(k.cs[:, 1, :], k.qsin_d[:, c]).then_inc(k.cs_in, 16)


def stage_gates(nc, k):
    G_PER = HEADS // GROUPS
    G0 = KT
    GP0 = G0 + GROUPS * (G_PER + 1)
    MM0, MP0, PA0 = GP0 + KT, GP0 + 2 * KT, GP0 + 3 * KT
    UNITS = PA0 + KT
    GM = 2 * KT
    G_USES = 2 * G_PER + 4
    GPM = GM + GROUPS * G_USES
    MMM = GPM + 2 * KT
    GPH = KT + GROUPS * (G_PER + 3)
    assert UNITS % 2 == 0 and GM % 4 == 0 and G_USES % 4 == 0

    with ExitStack() as ctx:
        def sb(name, shape, dt=F32):
            return ctx.enter_context(nc.sbuf_tensor(name, shape, dt))

        def sem(name):
            return ctx.enter_context(nc.semaphore(name))

        wst, w_in = k.wst, k.w_in_sem
        wH, wL = k.wH, k.wL
        for name in ("wH", "wL"):
            sb(name + "_place", [P, 2, D])
        with ExitStack() as place:
            k.wq_st, k.wkv_st, k.cs = (place.enter_context(nc.sbuf_tensor(name, shape, F32)) for name, shape in EARLY_3)
        pA = sb("pA", [P, UW])
        pB = sb("pB", [P, UW])
        inv = sb("inv", [P, SEQ])
        up = sb("up", [P, KT, UW])
        dH = sb("dH", [P, 2, SEQ], F32R)
        dL = sb("dL", [P, 2, SEQ], F32R)
        th = sb("th", [P, 2, HALF])
        ob = sb("ob", [P, 2, HALF])
        ones = sb("ones", [P, 1])
        bank = k.bank
        ps_gate = ctx.enter_context(nc.psum_tensor("ps_gate", [P, KT], F32))

        wL_rdy = k.wL_rdy
        used = k.used
        half_ps = k.half_ps
        ev_dve = sem("ev_dve")
        ev_act = sem("ev_act")
        pads = sem("pads")
        ones_rdy = sem("ones_rdy")
        gate_in = [sem("gate_in0"), sem("gate_in1")]
        gate_sum = sem("gate_sum")
        gate_ps = sem("gate_ps")
        gate_rdy = sem("gate_rdy")
        th_rdy = sem("th_rdy2")
        stored = k.stored
        inv_in = sem("inv_in")
        win = sem("win")
        d_rdy = sem("d_rdy")
        dH_rdy = sem("dH_rdy")
        dL_rdy = sem("dL_rdy")
        zp_rdy = sem("zp_rdy")
        zpH_rdy = sem("zpH_rdy")
        zpL_rdy = sem("zpL_rdy")
        thp_in = [sem("thp_in0"), sem("thp_in1")]

        block = ctx.enter_context(nc.Block())

        def w_cols(c0):
            return k.w_in[:, bass.ds(c0, P)].rearrange("(a p) n -> p a n", p=P)

        @block.sync
        def _(sp):
            def load(slot, src):
                sp.dma_start(wst[:, slot, :].rearrange("p (a n) -> p a n", a=KT), src).then_inc(w_in[slot], 16)

            with sp.Fori(1, KT // 2) as i:
                for b in range(2):
                    sp.wait_ge(wL_rdy, 2 * i + (b - 1))
                    load(b, w_cols((2 * i + b) * P + O_U))
            for g in range(GROUPS):
                if g:
                    sp.wait_ge(d_rdy, 2 * g)
                sp.dma_start(inv[:], k.pool_inv[g:g + 1, :].to_broadcast([P, SEQ])).then_inc(inv_in, 16)
                n = G0 + (G_PER + 1) * g
                with sp.Fori(0, G_PER // 2) as i:
                    for b in range(2):
                        sp.wait_ge(wL_rdy, 2 * i + (n + b - 1))
                        load((n + b) % 2, w_cols((2 * i + (G_PER * g + b)) * P + O_GM))
                n += G_PER
                sp.wait_ge(wL_rdy, n - 1)
                sp.dma_start(wst[:, n % 2, 0:2 * 2 * P].rearrange("p (a n) -> p a n", a=2),
                             k.w_pool[g].rearrange("(a p) n -> p a n", p=P)).then_inc(w_in[n % 2], 16)

            def pair(i, n0, off):
                for b in range(2):
                    sp.wait_ge(wL_rdy, 2 * i + (n0 + b - 1))
                    load(b, w_cols((2 * i + b) * P + off))

            for n0, off in ((GP0, O_GP), (MM0, O_MM)):
                with sp.Fori(0, KT // 2) as i:
                    pair(i, n0, off)
            sp.wait_ge(dL_rdy, KT)
            for kt in range(2):
                sp.dma_start((pA, pB)[kt][:, 0:D], k.ada_w[kt * P:(kt + 1) * P, 2 * D:3 * D]).then_inc(gate_in[kt], 16)
            with sp.Fori(0, KT // 2 - 1) as i:
                pair(i, MP0, O_MP)
                for b in range(2):
                    sp.wait_ge(gate_sum, 2 * i + (b + 1))
                    sp.dma_start((pA, pB)[b][:, 0:D], k.ada_w[bass.ds((2 * i + (b + 2)) * P, P), 2 * D:3 * D]
                                 ).then_inc(gate_in[b], 16)
            pair(KT // 2 - 1, MP0, O_MP)

            def proj_weights(slot, j):
                load(slot, k.w_proj_pool[:, bass.ds(j * P, P)].rearrange("(a p) n -> p a n", p=P))

            def pool_tanh(i, b):
                for h in range(2):
                    sp.wait_ge(ev_dve, 4 * i + (MMM + 2 * b + h - 1))
                    sp.dma_start(th[:, h, :], k.thp_d[bass.ds(2 * i + b, 1), :, h * HALF:(h + 1) * HALF]
                                 .rearrange("a p n -> p (a n)")).then_inc(thp_in[h], 16)

            for b in range(2):
                sp.wait_ge(wL_rdy, PA0 + b - 1)
                proj_weights(b, b)
            for h in range(2):
                sp.wait_ge(stored[h], 16 * (HEADS + 2 * KT))
            with sp.Fori(0, KT // 2 - 1) as i:
                for b in range(2):
                    pool_tanh(i, b)
                    sp.wait_ge(wL_rdy, 2 * i + (PA0 + b + 1))
                    proj_weights(b, 2 * i + (b + 2))
            for b in range(2):
                pool_tanh(KT // 2 - 1, b)
            sp.wait_ge(gate_ps, 1)
            for h in range(2):
                load_head(nc, k, h, h)
            load_rope(nc, k, 0)

        @block.gpsimd
        def _(pool):
            nc.gpsimd.memset(up[:, :, 0:PAD], 0.0)
            nc.gpsimd.memset(up[:, :, PAD + SEQ:UW], 0.0).then_inc(pads, 1)
            for n in range(2, UNITS):
                pool.wait_ge(used, n - 1)
                split_weights(nc, k, n % 2, n)

        @block.scalar
        def _(act):
            for g in range(GROUPS):
                for q in range(G_PER):
                    for h in range(2):
                        m = GM + G_USES * g + 2 * q + h
                        act.wait_ge((half_ps, used)[h], (KT + (G_PER + 3) * g, G0 + (G_PER + 1) * g)[h] + q + 1)
                        if g or q:
                            act.wait_ge(ev_dve, m - 1 if q else m - 5)
                        nc.scalar.activation(th[:, h, :], bank[m % 4][:], ACT.Tanh, scale=0.5).then_inc(th_rdy, 1)
                        act.wait_ge(ev_dve, m + 1)
                        act.dma_start(k.sg_d[G_PER * g + q, :, h * HALF:(h + 1) * HALF], ob[:, h, :]
                                      ).then_inc(stored[h], 16)
                    if q in (1, 2):
                        j = 2 * g + q - 1
                        act.wait_ge(d_rdy, j + 1)
                        if g:
                            act.wait_ge(used, G0 + (G_PER + 1) * g)
                        nc.scalar.activation(dH[:, q - 1, :], (pA if g % 2 else pB)[:, 0:SEQ], ACT.Copy
                                             ).then_inc(dH_rdy, 1)
            with act.Fori(0, KT // 2) as i:
                for b in range(2):
                    for h in range(2):
                        act.wait_ge((half_ps, used)[h], 2 * i + ((GPH, GP0)[h] + b + 1))
                        act.wait_ge(ev_dve, 4 * i + (GPM + 2 * b + h - 1))
                        nc.scalar.activation(th[:, h, :], bank[2 * b + h][:], ACT.Tanh, scale=0.5).then_inc(th_rdy, 1)
            act.wait_ge(zp_rdy, 2 * KT)
            for seg, (dst, bg) in enumerate(((k.th_d, KT), (k.thp_d, 0))):
                for j in range(KT):
                    for h in range(2):
                        r = seg * 2 * KT + 2 * j + h
                        act.wait_ge((half_ps, used)[h], (GPH, GP0)[h] + (seg + 1) * KT + j + 1)
                        act.wait_ge(stored[h], 16 * (HEADS + seg * KT + j))
                        nc.scalar.activation(ob[:, h, :], bank[r % 4][:], ACT.Tanh, scale=0.5,
                                             bias=k.bgh[:, bg + j:bg + j + 1]).then_inc(ev_act, 1)
                        act.wait_ge(ev_act, r + 1)
                        act.dma_start(dst[j, :, h * HALF:(h + 1) * HALF], ob[:, h, :]).then_inc(stored[h], 16)
            act.wait_ge(used, PA0)
            for kt in range(KT):
                nc.scalar.activation(k.hH[:, kt, :], up[:, kt, PAD:PAD + SEQ], ACT.Copy).then_inc(zpH_rdy, 1)
            with act.Fori(0, KT // 2) as i:
                for b in range(2):
                    for h in range(2):
                        act.wait_ge(ev_dve, 4 * i + (MMM + 2 * b + h + 1))
                        act.dma_start(k.yp_d[bass.ds(2 * i + b, 1), :, h * HALF:(h + 1) * HALF]
                                      .rearrange("a p n -> p (a n)"), ob[:, h, :]).then_inc(stored[h], 16)

        @block.vector
        def _(dve):
            nc.vector.memset(ones[:], 1.0).then_inc(ones_rdy, 1)
            dve.wait_ge(pads, 1)
            with dve.Fori(0, KT // 2) as i:
                for b in range(2):
                    for h in range(2):
                        dve.wait_ge((half_ps, used)[h], 2 * i + (b + 1))
                        nc.vector.tensor_copy(up[:, bass.ds(2 * i + b, 1), PAD + h * HALF:PAD + (h + 1) * HALF],
                                              bank[2 * b + h][:].unsqueeze(1)).then_inc(ev_dve, 1)
            steps = 0

            def pool_tile(g, j):
                nonlocal steps
                src = up[:, j, :]
                bufs = [pA, pB]
                lo, hi = 0, UW
                for lvl in range(g + 1):
                    shift = (1, 1, 2, 4)[lvl]
                    right = 0 if lvl == 0 else shift
                    lo, hi = lo + shift, hi - right
                    dst = bufs[lvl % 2]
                    if steps:
                        dve.wait_ge(win, steps)
                    nc.vector.tensor_tensor(dst[:, lo:hi], src[:, lo - shift:hi - shift],
                                            src[:, lo + right:hi + right], ALU.add).then_inc(win, 1)
                    steps += 1
                    src = dst
                cur, oth = bufs[g % 2], bufs[(g + 1) % 2]
                dve.wait_ge(win, steps)
                nc.vector.tensor_tensor(oth[:, 0:SEQ], cur[:, PAD:PAD + SEQ], inv[:], ALU.mult).then_inc(win, 1)
                steps += 1
                dve.wait_ge(win, steps)
                nc.vector.tensor_tensor(oth[:, 0:SEQ], oth[:, 0:SEQ], up[:, j, PAD:PAD + SEQ], ALU.subtract
                                        ).then_inc(d_rdy, 1)
                dve.wait_ge(d_rdy, j + 1)
                return oth

            for g in range(GROUPS):
                for q in range(G_PER):
                    for h in range(2):
                        m = GM + G_USES * g + 2 * q + h
                        gi = G_PER * g + q
                        dve.wait_ge(th_rdy, 2 * gi + h + 1)
                        if gi:
                            dve.wait_ge(stored[h], 16 * gi)
                        nc.vector.scalar_tensor_tensor(out=ob[:, h, :], in0=th[:, h, :], scalar=1.0,
                                                       in1=bank[m % 4][:], op0=ALU.add, op1=ALU.mult
                                                       ).then_inc(ev_dve, 1)
                    if q in (1, 2):
                        j = 2 * g + q - 1
                        dve.wait_ge(dH_rdy, j + 1)
                        nc.vector.tensor_tensor(dL[:, q - 1, :], (pA if g % 2 else pB)[:, 0:SEQ],
                                                dH[:, q - 1, :].bitcast(F32), ALU.subtract).then_inc(dL_rdy, 1)
                        dve.wait_ge(dL_rdy, j + 1)
                    if q < 2:
                        if q == 0:
                            dve.wait_ge(inv_in, 16 * (g + 1))
                        pool_tile(g, 2 * g + q)
                for dt in range(2):
                    for h in range(2):
                        m = GM + G_USES * g + 2 * G_PER + 2 * dt + h
                        dve.wait_ge(*((used, G0 + (G_PER + 1) * (g + 1)) if dt and h else
                                      (half_ps, KT + (G_PER + 3) * g + G_PER + 2 * dt + h + 1)))
                        nc.vector.tensor_scalar(up[:, 2 * g + dt, PAD + h * HALF:PAD + (h + 1) * HALF], bank[m % 4][:],
                                                k.vt[:, R_PS + 2 * g + dt:R_PS + 2 * g + dt + 1], None,
                                                ALU.mult).then_inc(ev_dve, 1)
            for h in range(2):
                dve.wait_ge(stored[h], 16 * HEADS)
            with dve.Fori(0, KT // 2) as i:
                for b in range(2):
                    for h in range(2):
                        a = 2 * b + h
                        dve.wait_ge(th_rdy, 4 * i + (2 * HEADS + a + 1))
                        nc.vector.scalar_tensor_tensor(out=ob[:, h, :], in0=th[:, h, :], scalar=1.0,
                                                       in1=bank[a][:], op0=ALU.add, op1=ALU.mult).then_inc(ev_dve, 1)
                        dve.wait_ge(ev_dve, 4 * i + (GPM + a + 1))
                        t = up[:, bass.ds(2 * i + b, 1), PAD + h * HALF:PAD + (h + 1) * HALF]
                        nc.vector.scalar_tensor_tensor(out=t, in0=t, scalar=0.5, in1=ob[:, h, :].unsqueeze(1),
                                                       op0=ALU.mult, op1=ALU.mult).then_inc(zp_rdy, 1)
            for kt in range(KT):
                dve.wait_ge(gate_in[kt % 2], 16 * (kt // 2 + 1))
                row, c = (pA, pB)[kt % 2][:, 0:D], k.cond[:, kt, 0:1]
                if kt:
                    dve.wait_ge(gate_sum, kt)
                    nc.vector.scalar_tensor_tensor(out=inv[:], in0=row, scalar=c, in1=inv[:], op0=ALU.mult,
                                                   op1=ALU.add).then_inc(gate_sum, 1)
                else:
                    nc.vector.tensor_scalar(inv[:], row, c, None, ALU.mult).then_inc(gate_sum, 1)
            for kt in range(KT):
                dve.wait_ge(zpH_rdy, kt + 1)
                nc.vector.tensor_tensor(k.hL[:, kt, :], up[:, kt, PAD:PAD + SEQ], k.hH[:, kt, :].bitcast(F32),
                                        ALU.subtract).then_inc(zpL_rdy, 1)
            dve.wait_ge(gate_ps, 1)
            nc.vector.scalar_tensor_tensor(out=k.gateT[:], in0=ps_gate[:],
                                           scalar=0.5, in1=k.vt[:, R_ADAB + 2 * KT:R_ADAB + 3 * KT],
                                           op0=ALU.mult, op1=ALU.add).then_inc(gate_rdy, 1)
            with dve.Fori(0, KT // 2) as i:
                for b in range(2):
                    for h in range(2):
                        a = 2 * b + h
                        dve.wait_ge((half_ps, used)[h], 2 * i + ((GPH, GP0)[h] + 3 * KT + b + 1))
                        dve.wait_ge(thp_in[h], 32 * i + 16 * (b + 1))
                        dve.wait_ge(stored[h], 32 * i + 16 * (HEADS + 2 * KT + b))
                        nc.vector.scalar_tensor_tensor(out=ob[:, h, :], in0=th[:, h, :], scalar=1.0,
                                                       in1=bank[a][:], op0=ALU.add, op1=ALU.mult).then_inc(ev_dve, 1)

        @block.tensor
        def _(pe):
            def unit(slot, n, b0, free=None, free_at=0):
                pe.wait_ge(wL_rdy, n + 1)
                for h in range(2):
                    if free is not None:
                        pe.wait_ge(free, free_at + h)
                    unit_half(nc, k, bank[b0 + h], slot, h).then_inc((half_ps, used)[h], 1)

            def units(n0, free, free_at, first=0):
                with pe.Fori(first, KT // 2) as i:
                    for b in range(2):
                        unit(b, 2 * i + (n0 + b), 2 * b, free, 4 * i + (free_at + 2 * b))

            unit(1, 1, 2)
            units(0, ev_dve, -3, first=1)
            for g in range(GROUPS):
                n, m = G0 + (G_PER + 1) * g, GM + G_USES * g
                with pe.Fori(0, G_PER // 2) as i:
                    for b in range(2):
                        unit((n + b) % 2, 2 * i + (n + b), 2 * b, ev_dve, 4 * i + (m + 2 * b - 3))
                n, m = n + G_PER, m + 2 * G_PER
                pe.wait_ge(wL_rdy, n + 1)
                pe.wait_ge(dL_rdy, 2 * g + 2)
                for dt in range(2):
                    for h in range(2):
                        pe.wait_ge(ev_dve, m + 2 * dt + h - 3)
                        for kt in range(2):
                            w = slice(kt * 2 * P + dt * P, kt * 2 * P + (dt + 1) * P)
                            c = slice(h * HALF, (h + 1) * HALF)
                            last = mm3(nc, bank[2 * dt + h][:], wH[:, n % 2, w], wL[:, n % 2, w], dH[:, kt, c],
                                       dL[:, kt, c], kt == 0, kt == 1)
                        last.then_inc(used if dt and h else half_ps, 1)
            units(GP0, ev_dve, GPM - 3)
            pe.wait_ge(ev_dve, MMM)
            for b in range(2):
                unit(b, MM0 + b, 2 * b)
            units(MM0, ev_act, -3, first=1)
            units(MP0, ev_act, 2 * KT - 3)
            pe.wait_ge(ev_act, 4 * KT)
            pe.wait_ge(ones_rdy, 1)
            pe.wait_ge(gate_sum, KT)
            for o in range(KT):
                last = nc.tensor.matmul(ps_gate[:, o:o + 1], inv[:, o * P:(o + 1) * P], ones[:], start=True, stop=True)
            last.then_inc(gate_ps, 1)
            pe.wait_ge(wL_rdy, PA0 + 1)
            for kt in range(KT):
                pe.wait_ge(zpL_rdy, kt + 1)
                for h in range(2):
                    w, c = slice(kt * P, (kt + 1) * P), slice(h * HALF, (h + 1) * HALF)
                    last = mm3(nc, bank[h][:], wH[:, 0, w], wL[:, 0, w], k.hH[:, kt, c], k.hL[:, kt, c],
                               kt == 0, kt == KT - 1)
                    if kt == KT - 1:
                        last.then_inc((half_ps, used)[h], 1)
            unit(1, PA0 + 1, 2)
            units(PA0, ev_dve, MMM - 3, first=1)


QCHUNKS = ((0, 512), (512, 1024), (1024, KEYS))
QKT = (((0, 1, 2), (3, 4), (5, 6), (7, 8, 9)),
       ((0, 1, 2), (3, 4, 5), (6, 7), (8, 9)),
       ((0, 1, 2), (3, 4, 5), (6, 7), (8, 9)),
       ((0, 1), (2, 3), (4, 5, 6), (7, 8, 9)))
M_PRO = 4
TAIL = ("R", "o", "y0", "y1", "y2", "y3", "y4", "R last", "y5", "o last", "y6", "y7",
        "h0", "h1", "h2", "h3", "h4", "h5", "h6", "h7")


def unit_products(j, kind):
    y = kind != "first"
    last = kind == "last"
    prev = ["R", "o"] * (y or j > 1)
    if j == 0:
        return [["rope"], prev, ["turn", "q"], ["absorb"]]
    if j == 1:
        return [["y0", "y1"] * y, prev + ["y2"] * y, ["y3"] * y + ["q"], ["y4", "y5"] * y]
    if j == 2:
        return [["y6", "y7"] * y, prev + ["h0"] * y, ["h1"] * y + ["turn"] * (not last) + ["q"],
                ["absorb"] * (not last) + ["h2"] * y]
    return [["rope"] * (not last) + ["h3"] * y, prev + ["h4", "h5"] * y, ["h6", "h7"] * y + ["q"] * (not last), []]


WO_EARLY = QT * KEYS // D - 1
SPLIT_EARLY = 2 * QT * KEYS // D - KT


def body_size(kind):
    return sum(len(q) for j in range(4) for q in unit_products(j, kind))


def product_index(i, j, name, kind):
    off = 0
    for jj in range(4):
        for q in unit_products(jj, kind):
            for n in q:
                if jj == j and n == name:
                    first = M_PRO + body_size("first")
                    if kind == "first":
                        return M_PRO + off
                    if kind == "last":
                        return first + (PAIRS - 2) * body_size("mid") + off
                    return i * body_size("mid") + (first - body_size("mid") + off)
                off += 1
    raise KeyError(name)


def product_bank(j, name, kind):
    return (product_index(1, j, name, kind) if kind == "mid" else product_index(0, j, name, kind)) % 2


def stage_attention(nc, k):
    assert body_size("mid") % 2 == 0
    TAIL0 = M_PRO + body_size("first") + (PAIRS - 2) * body_size("mid") + body_size("last")
    UNITS = 4 * PAIRS

    with ExitStack() as ctx:
        def sb(name, shape, dt=F32):
            return ctx.enter_context(nc.sbuf_tensor(name, shape, dt))

        def sem(name):
            return ctx.enter_context(nc.semaphore(name))

        with ExitStack() as place:
            k.wo_raw, k.woL = loaded_as(nc, place, "wo_raw", "woL", [P, KT, D])
            k.woH = place.enter_context(nc.sbuf_tensor("woH", [P, KT, D], F32R))
        E = sb("E", [P, 2, QT, KEYS])
        zH = sb("zH", [P, 2, 2, HALF], F32R)
        zL = sb("zL", [P, 2, 2, HALF], F32R)
        wpH = sb("wpH", [P, 2, D], F32R)
        wpL = sb("wpL", [P, 2, D], F32R)
        wp_st = sb("wp_st", [P, D])
        ptH = sb("ptH", [P, 2, HALF], F32R)
        ptL = sb("ptL", [P, 2, HALF], F32R)
        sg = sb("sg", [P, HALF])
        sw = sb("sw", [P, HALF])
        assert 2 * QT * KEYS + 8 * HALF + 5 * D + 4 * HALF + 2 * HALF == 2 * KT * SEQ + 3 * 2 * D
        wq_st, wkv_st, cs = k.wq_st, k.wkv_st, k.cs
        for name, shape in EARLY_3:
            sb(name + "_place", shape)
        qpH = sb("qpH", [P, 2, HALF], F32R)
        qpL = sb("qpL", [P, 2, HALF], F32R)
        q2 = [sb("q2a", [P, SEQ], F32R), sb("q2b", [P, SEQ], F32R)]
        wcH = sb("wcH", [P, 2, QL], F32R)
        wcL = sb("wcL", [P, 2, QL], F32R)
        wrH = sb("wrH", [P, QLT, 2, ROPE], F32R)
        wrL = sb("wrL", [P, QLT, 2, ROPE], F32R)
        wvH = sb("wvH", [P, 2, VD], F32R)
        wvL = sb("wvL", [P, 2, VD], F32R)
        t1 = sb("t1", [P, HALF])
        opH = sb("opH", [P, HALF], F32R)
        opL = sb("opL", [P, HALF], F32R)
        mx = sb("mx", [P, 2, QT, 3])
        nm = sb("nm", [P, 2, QT])
        sums = sb("sums", [P, 2, QT])
        rinv = sb("rinv", [P, 2, QT])

        ps_s = ctx.enter_context(nc.psum_tensor("ps_s", [P, 3 * 512], F32))
        ps_pt = [ctx.enter_context(nc.psum_tensor(f"ps_pt{b}", [P, HALF], F32)) for b in range(2)]
        ps_o = ctx.enter_context(nc.psum_tensor("ps_o", [P, HALF], F32))
        ps_m = [ctx.enter_context(nc.psum_tensor(f"ps_m{b}", [P, HALF], F32)) for b in range(2)]

        wq_in, cs_in = k.wq_in, k.cs_in
        wp_in = sem("wp_in")
        sg_in = sem("sg_in")
        s_chunk = [sem(f"s_chunk{c}") for c in range(3)]
        mx_rdy = sem("mx_rdy")
        nm_rdy = sem("nm_rdy")
        e_rdy = sem("e_rdy")
        pt_ps = sem("pt_ps")
        ptH_rdy = sem("ptH_rdy")
        ptL_rdy = sem("ptL_rdy")
        pv = sem("pv")
        opH_rdy = sem("opH_rdy")
        opL_rdy = sem("opL_rdy")
        rinv_rdy = sem("rinv_rdy")
        m_ps = sem("m_ps")
        mH_rdy = sem("mH_rdy")
        m_free = sem("m_free")
        sw_rdy = sem("sw_rdy")
        sn_rdy = sem("sn_rdy")
        tq_rdy = sem("tq_rdy")
        q2H_rdy = sem("q2H_rdy")
        q2_rdy = sem("q2_rdy")
        wrH_rdy = sem("wrH_rdy")
        wrL_rdy = sem("wrL_rdy")
        wvH_rdy = sem("wvH_rdy")
        wvL_rdy = sem("wvL_rdy")
        wpH_rdy = sem("wpH_rdy")
        wpL_rdy = sem("wpL_rdy")
        zH_rdy = sem("zH_rdy")
        z_rdy = sem("z_rdy")
        ym_rdy = sem("ym_rdy")
        th_in_sem = [sem("th_in0"), sem("th_in1")]
        yp0_in = sem("yp0_in")
        y0_rdy = sem("y0_rdy")

        block = ctx.enter_context(nc.Block())

        def static(v):
            return isinstance(v, int)

        def positive(eng, s, v):
            if not static(v) or v > 0:
                eng.wait_ge(s, v)

        def bodies(eng, body):
            body(0, "first")
            with eng.Fori(1, PAIRS - 1) as i:
                body(i, "mid")
            body(PAIRS - 1, "last")

        def mhi_count(i, kind, j, name):
            n = 0
            for jj in range(4):
                for q in unit_products(jj, kind):
                    for nm_ in q:
                        if nm_ in ("turn", "absorb", "q"):
                            n += 1
                        if jj == j and nm_ == name:
                            per = 8
                            return i * per + (3 + n)
            raise KeyError(name)

        def raw_rope(t):
            return t.rearrange("p k (a b c) -> p b k a c", a=2, b=2)

        def rope_half(t, b):
            return t[:, :, b * RH:(b + 1) * RH].rearrange("p k (a c) -> p k a c", a=2)

        @block.sync
        def _(sp):
            def head_weights(h, slot):
                load_head(nc, k, h, slot)

            def tables(half):
                load_rope(nc, k, half)

            def proj_weights(h):
                sp.dma_start(wp_st[:], k.w_proj_mla[bass.ds(h * VD, VD), :]).then_inc(wp_in, 16)

            def gate_tile(h, half):
                sp.dma_start(sg[:], k.sg_d[bass.ds(h, 1), :, half * HALF:(half + 1) * HALF]
                             .rearrange("a p n -> p (a n)")).then_inc(sg_in, 16)

            proj_weights(0)
            for h in range(2):
                sp.wait_ge(k.stored[h], 16 * (HEADS + 3 * KT))
            sp.wait_ge(tq_rdy, 1)
            tables(1)

            def body(i, kind):
                for j in range(4):
                    w = 4 * i + j - 2
                    if j == 0 and kind != "last":
                        sp.wait_ge(wvL_rdy, 2 * i + 1)
                        head_weights(2 * i + 2, 0)
                    if j == 2 and kind != "last":
                        sp.wait_ge(wvL_rdy, 2 * i + 2)
                        head_weights(2 * i + 3, 1)
                    if kind != "first" or j >= 2:
                        positive(sp, z_rdy, w)
                        gate_tile(2 * i + j // 2 - 1, j % 2)
                    if kind != "first" and j < 2:
                        sp.wait_ge(wpL_rdy, 2 * i - 1 + j)
                        proj_weights(2 * i - 1 + j)
                    if j == 1 and kind != "last":
                        sp.wait_ge(tq_rdy, 2 * i + 2)
                        tables(0)
                    if j == 3 and kind != "last":
                        sp.wait_ge(tq_rdy, 2 * i + 3)
                        tables(1)

            bodies(sp, body)
            sp.wait_ge(wpL_rdy, HEADS - 1)
            proj_weights(HEADS - 1)
            sp.wait_ge(z_rdy, UNITS - 2)
            gate_tile(HEADS - 1, 0)
            sp.wait_ge(s_chunk[2], QT * UNITS)
            for b in range(2):
                f = slice(b * KT // 2, (b + 1) * KT // 2)
                sp.dma_start(k.th_in[:, f, :], k.th_d[f].rearrange("a p n -> p a n")).then_inc(th_in_sem[b], 16)
            sp.wait_ge(z_rdy, UNITS - 1)
            gate_tile(HEADS - 1, 1)
            sp.wait_ge(pt_ps, NKT * (UNITS - 1))
            sp.dma_start(k.wo_raw[:, 0:WO_EARLY, :], k.w_out[0:WO_EARLY * P, :].rearrange("(a p) n -> p a n", p=P)
                         ).then_inc(k.wo_in_sem, 16)
            sp.dma_start(k.wo_raw[:, WO_EARLY, :], k.yp_d[0]).then_inc(yp0_in, 16)

        @block.gpsimd
        def _(pool):
            def lo(out, x, hi):
                return nc.gpsimd.tensor_tensor(out, x, hi.bitcast(F32), ALU.subtract)

            def wr_lo(h, slot):
                pool.wait_ge(wrH_rdy, h + 1)
                for b in range(2):
                    last = lo(rope_half(wrL[:, :, slot, :], b), raw_rope(wq_st[:, slot, :, NOPE:])[:, b],
                              rope_half(wrH[:, :, slot, :], b))
                last.then_inc(wrL_rdy, 1)

            def wv_lo(h, slot):
                pool.wait_ge(wvH_rdy, h + 1)
                lo(wvL[:, slot, :], wkv_st[:, slot, NOPE:], wvH[:, slot, :]).then_inc(wvL_rdy, 1)

            def wp_lo(h, slot):
                pool.wait_ge(wpH_rdy, h + 1)
                lo(wpL[:, slot, :], wp_st[:], wpH[:, slot, :]).then_inc(wpL_rdy, 1)

            def rotate(r, at):
                pool.wait_ge(cs_in, 32 * r + 32)
                pool.wait_ge(sw_rdy, r + 1)
                nc.gpsimd.tensor_tensor(sw[:], sw[:], cs[:, 1, :], ALU.mult).then_inc(sn_rdy, 1)
                pool.wait_ge(m_free, at)
                pool.wait_ge(sn_rdy, r + 1)
                nc.gpsimd.tensor_tensor(t1[:], t1[:], sw[:], ALU.add).then_inc(tq_rdy, 1)

            def z_lo(v, hp, half):
                pool.wait_ge(zH_rdy, v + 1)
                lo(zL[:, hp, half, :], sg[:], zH[:, hp, half, :]).then_inc(z_rdy, 1)

            wr_lo(0, 0)
            wr_lo(1, 1)
            rotate(0, 2)
            wv_lo(0, 0)

            def body(i, kind):
                rotate(2 * i + 1, product_index(i, 0, "rope", kind) + 1)
                if kind != "first":
                    wp_lo(2 * i - 2, 0)
                    wp_lo(2 * i - 1, 1)
                if kind != "last":
                    wr_lo(2 * i + 2, 0)
                if kind != "first":
                    z_lo(4 * i - 2, 1, 0)
                wv_lo(2 * i + 1, 1)
                if kind != "first":
                    z_lo(4 * i - 1, 1, 1)
                if kind != "last":
                    wr_lo(2 * i + 3, 1)
                z_lo(4 * i, 0, 0)
                if kind != "last":
                    rotate(2 * i + 2, product_index(i, 3, "rope", kind) + 1)
                    wv_lo(2 * i + 2, 0)
                if kind == "last":
                    wp_lo(HEADS - 2, 0)
                z_lo(4 * i + 1, 0, 1)

            bodies(pool, body)
            wp_lo(HEADS - 1, 1)
            z_lo(UNITS - 2, 1, 0)
            z_lo(UNITS - 1, 1, 1)
            pool.wait_ge(yp0_in, 16)
            pool.wait_ge(ym_rdy, KT + 1)
            nc.gpsimd.tensor_tensor(k.yacc[:, 0, :], k.yacc[:, 0, :], k.wo_raw[:, WO_EARLY, :], ALU.add
                                    ).then_inc(y0_rdy, 1)
            for kt in range(SPLIT_EARLY):
                pool.wait_ge(k.woH_rdy, kt + 1)
                lo(k.woL[:, kt, :], k.wo_raw[:, kt, :], k.woH[:, kt, :]).then_inc(k.woL_rdy, 1)

        @block.scalar
        def _(act):
            def copy(out, x):
                return nc.scalar.activation(out, x, ACT.Copy)

            def wr_hi(h, slot):
                act.wait_ge(wq_in[slot], (h - slot) * 16 + 32)
                for b in range(2):
                    last = copy(rope_half(wrH[:, :, slot, :], b), raw_rope(wq_st[:, slot, :, NOPE:])[:, b])
                last.then_inc(wrH_rdy, 1)

            def wv_hi(h, slot):
                copy(wvH[:, slot, :], wkv_st[:, slot, NOPE:]).then_inc(wvH_rdy, 1)

            def wp_hi(h, slot):
                act.wait_ge(wp_in, h * 16 + 16)
                copy(wpH[:, slot, :], wp_st[:]).then_inc(wpH_rdy, 1)

            def small_hi(name, at, b, half=0, slot=0, r=None):
                if name in ("turn", "absorb", "q", "rope"):
                    act.wait_ge(m_ps, at + 1)
                if name == "turn":
                    copy(opH[:, 0:3 * P], ps_m[b][:, 0:3 * P]).then_inc(mH_rdy, 1)
                elif name == "absorb":
                    copy(wcH[:, slot, :], ps_m[b][:, 0:QL]).then_inc(mH_rdy, 1)
                elif name == "q":
                    copy(qpH[:, half, :], ps_m[b][:]).then_inc(mH_rdy, 1)
                elif name == "rope":
                    for q in range(4):
                        o = q ^ 1
                        last = copy(sw[q * RH:(q + 1) * RH, :], ps_m[b][o * RH:(o + 1) * RH, :])
                    last.then_inc(sw_rdy, 1)

            def rope_hi(r, half):
                act.wait_ge(tq_rdy, r + 1)
                c = slice(half * HALF, (half + 1) * HALF)
                copy(q2[0][0:ROPE, c], t1[0:ROPE, :])
                copy(q2[1][ROPE:P, c], t1[ROPE:P, :]).then_inc(q2H_rdy, 1)

            def z_hi(v, hp, half, at):
                act.wait_ge(m_free, at)
                copy(zH[:, hp, half, :], sg[:]).then_inc(zH_rdy, 1)

            def exponent(u, j, qt):
                act.wait_ge(nm_rdy, 4 * u + (qt + 1))
                if qt == 0:
                    positive(act, pt_ps, 10 * (u - 1))
                nc.scalar.activation(E[:, j % 2, qt, :], ps_s[:, 0:KEYS], ACT.Exp, bias=nm[:, j % 2, qt:qt + 1],
                                     accum_out=sums[:, j % 2, qt:qt + 1]).then_inc(e_rdy, 1)

            def turned_hi(v, kt):
                act.wait_ge(pt_ps, NKT * v + (kt + 1))
                positive(act, pv, NKT * v + (kt - 1))
                copy(ptH[:, kt % 2, :], ps_pt[kt % 2][:]).then_inc(ptH_rdy, 1)

            def latent_hi(v):
                act.wait_ge(pv, NKT * (v + 1))
                copy(opH[:], ps_o[:]).then_inc(opH_rdy, 1)

            wr_hi(0, 0)
            wr_hi(1, 1)
            small_hi("turn", 0, 0)
            small_hi("rope", 1, 1)
            small_hi("absorb", 2, 0)
            wv_hi(0, 0)
            small_hi("q", 3, 1)
            rope_hi(0, 0)

            def body(i, kind):
                for j in range(4):
                    u = 4 * i + j
                    v, w = u - 1, u - 2
                    has_v = kind != "first" or j > 0
                    has_w = kind != "first" or j > 1

                    def at(name, jj=j):
                        return product_index(i, jj, name, kind)

                    for qt in range(QT):
                        kts = QKT[j][qt] if has_v else ()
                        if has_v:
                            turned_hi(v, kts[0])
                        if qt == 0 and has_w:
                            latent_hi(w)
                        if has_v:
                            turned_hi(v, kts[1])
                        exponent(u, j, qt)
                        for n, name in enumerate(unit_products(j, kind)[qt]):
                            if n == 1:
                                for kt in kts[2:]:
                                    turned_hi(v, kt)
                                kts = ()
                            small_hi(name, at(name), product_bank(j, name, kind), half=(j + 1) % 2,
                                     slot=(j // 2 + 1) % 2)
                        for kt in kts[2:]:
                            turned_hi(v, kt)
                        if qt == 0 and j == 0 and kind != "first":
                            act.wait_ge(m_ps, at("rope") + 1)
                            wp_hi(2 * i - 2, 0)
                        if qt == 1 and j == 0:
                            rope_hi(2 * i + 1, 1)
                        if qt == 1 and j == 3 and kind != "last":
                            rope_hi(2 * i + 2, 0)
                        if qt == 2 and j == 0 and kind != "first":
                            wp_hi(2 * i - 1, 1)
                        if qt == 2 and j == 0 and kind != "last":
                            wr_hi(2 * i + 2, 0)
                        if qt == 2 and j == 1:
                            if kind != "first":
                                act.wait_ge(m_ps, at("o") + 1)
                            wv_hi(2 * i + 1, 1)
                        if qt == 2 and j == 2 and kind != "last":
                            wr_hi(2 * i + 3, 1)
                        if qt == 2 and j == 3 and kind != "last":
                            act.wait_ge(m_ps, at("o") + 1)
                            wv_hi(2 * i + 2, 0)
                        if qt == 2 and j == 3 and kind == "last":
                            act.wait_ge(m_ps, at("h7") + 1)
                            wp_hi(HEADS - 2, 0)
                        if qt == 3 and has_w:
                            if j == 3 and kind != "first":
                                act.wait_ge(m_ps, at("h7") + 1)
                            z_hi(w, (j // 2 + 1) % 2, j % 2, at("o") + 1)

            bodies(act, body)
            v = UNITS - 1
            for kt in range(NKT):
                turned_hi(v, kt)
                if kt == 0:
                    latent_hi(v - 1)
                if kt == 3:
                    z_hi(v - 1, 1, 0, TAIL0 + 2)
                if kt == 2:
                    wp_hi(HEADS - 1, 1)
            latent_hi(v)
            z_hi(v, 1, 1, TAIL0 + TAIL.index("o last") + 1)
            act.wait_ge(k.wo_in_sem, 16)
            for kt in range(SPLIT_EARLY):
                copy(k.woH[:, kt, :], k.wo_raw[:, kt, :]).then_inc(k.woH_rdy, 1)
            act.wait_ge(y0_rdy, 1)
            copy(k.yH[:, 0, :], k.yacc[:, 0, :]).then_inc(k.yH_rdy, 1)

        @block.vector
        def _(dve):
            def lo(out, x, hi):
                return nc.vector.tensor_tensor(out, x, hi.bitcast(F32), ALU.subtract)

            def small(name, at, b, half=0, slot=0, hi=None, unit=None):
                ps = ps_m[b]
                if hi is not None:
                    dve.wait_ge(mH_rdy, hi)
                if name == "turn":
                    lo(opL[:, 0:3 * P], ps[:, 0:3 * P], opH[:, 0:3 * P]).then_inc(m_free, 1)
                elif name == "absorb":
                    lo(wcL[:, slot, :], ps[:, 0:QL], wcH[:, slot, :]).then_inc(m_free, 1)
                elif name == "q":
                    lo(qpL[:, half, :], ps[:], qpH[:, half, :]).then_inc(m_free, 1)
                elif name == "R":
                    dve.wait_ge(m_ps, at + 1)
                    dve.wait_ge(sg_in, 16 * (unit + 1))
                    nc.vector.tensor_tensor(sg[:], sg[:], ps[:], ALU.mult).then_inc(m_free, 1)
                elif name == "o":
                    dve.wait_ge(m_ps, at + 1)
                    dve.wait_ge(m_free, at)
                    nc.vector.scalar_tensor_tensor(out=sg[:], in0=ps[:], scalar=0.5, in1=sg[:], op0=ALU.mult,
                                                   op1=ALU.mult).then_inc(m_free, 1)
                else:
                    y_half = int(name[0] == "h")
                    t = k.yacc[:, int(name[1]), y_half * HALF:(y_half + 1) * HALF]
                    dve.wait_ge(m_ps, at + 1)
                    nc.vector.tensor_tensor(t, t, ps[:], ALU.add).then_inc(m_free, 1)

            def rope(r, at, b):
                dve.wait_ge(sw_rdy, r + 1)
                dve.wait_ge(cs_in, 32 * r + 32)
                nc.vector.tensor_tensor(t1[:], ps_m[b][:], cs[:, 0, :], ALU.mult).then_inc(m_free, 1)

            def rope_lo(r, half):
                dve.wait_ge(q2H_rdy, r + 1)
                c = slice(half * HALF, (half + 1) * HALF)
                lo(q2[0][ROPE:P, c], t1[0:ROPE, :], q2[0][0:ROPE, c])
                lo(q2[1][0:ROPE, c], t1[ROPE:P, :], q2[1][ROPE:P, c]).then_inc(q2_rdy, 1)

            def turned_lo(v, kt):
                dve.wait_ge(ptH_rdy, NKT * v + (kt + 1))
                lo(ptL[:, kt % 2, :], ps_pt[kt % 2][:], ptH[:, kt % 2, :]).then_inc(ptL_rdy, 1)

            def maximum(u, j, qt, c):
                n = 4 * u + qt
                dve.wait_ge(s_chunk[c], n + 1)
                last = nc.vector.tensor_reduce(mx[:, j % 2, qt, c:c + 1], ps_s[:, slice(*QCHUNKS[c])], AX_X, ALU.max)
                if c == 2:
                    last.then_inc(mx_rdy, 1)
                    dve.wait_ge(mx_rdy, n + 1)
                    nc.vector.tensor_reduce(nm[:, j % 2, qt:qt + 1], mx[:, j % 2, qt, :], AX_X, ALU.max, negate=True
                                            ).then_inc(nm_rdy, 1)

            def inverse_sums(v, jv):
                dve.wait_ge(e_rdy, 4 * (v + 1))
                nc.vector.reciprocal(rinv[:, jv % 2, :], sums[:, jv % 2, :]).then_inc(rinv_rdy, 1)

            def latent_lo(v):
                dve.wait_ge(opH_rdy, v + 1)
                lo(opL[:], ps_o[:], opH[:]).then_inc(opL_rdy, 1)

            small("turn", 0, 0, hi=1)
            rope(0, 1, 1)
            small("absorb", 2, 0, hi=2)
            small("q", 3, 1, hi=3)
            rope_lo(0, 0)

            def body(i, kind):
                for j in range(4):
                    u = 4 * i + j
                    v, w = u - 1, u - 2
                    has_v = kind != "first" or j > 0
                    has_w = kind != "first" or j > 1

                    def filler(name):
                        at = product_index(i, j, name, kind)
                        b = product_bank(j, name, kind)
                        if name == "rope":
                            rope(2 * i + (1 if j == 0 else 2), at, b)
                            return
                        hi = mhi_count(i, kind, j, name) if name in ("turn", "absorb", "q") else None
                        small(name, at, b, half=(j + 1) % 2, slot=(j // 2 + 1) % 2, hi=hi, unit=w)

                    for qt in range(QT):
                        kts = QKT[j][qt] if has_v else ()
                        maximum(u, j, qt, 0)
                        if qt == 0 and has_v:
                            inverse_sums(v, (j - 1) % 4)
                        if has_v:
                            turned_lo(v, kts[0])
                        maximum(u, j, qt, 1)
                        if qt == 0 and has_w:
                            latent_lo(w)
                        maximum(u, j, qt, 2)
                        if kind == "first" and j == 0 and qt == 0:
                            for h in range(2):
                                dve.wait_ge(k.stored[h], 16 * (HEADS + 3 * KT))
                        if kind == "first":
                            nc.vector.memset(k.yacc[:, 2 * j + qt // 2, qt % 2 * HALF:(qt % 2 + 1) * HALF], 0.0)
                        if has_v:
                            turned_lo(v, kts[1])
                        for n, name in enumerate(unit_products(j, kind)[qt]):
                            if n == 1:
                                for kt in kts[2:]:
                                    turned_lo(v, kt)
                                kts = ()
                            filler(name)
                        for kt in kts[2:]:
                            turned_lo(v, kt)
                        if qt == 1 and j == 0:
                            rope_lo(2 * i + 1, 1)
                        if qt == 1 and j == 3 and kind != "last":
                            rope_lo(2 * i + 2, 0)

            bodies(dve, body)
            v = UNITS - 1
            inverse_sums(v, 3)

            def tail(n):
                name = TAIL[n].split()[0]
                small(name, TAIL0 + n, (TAIL0 + n) % 2, unit=v if "last" in TAIL[n] else v - 1)
                if name[0] in "yh":
                    if name in ("y0", f"y{KT // 2}"):
                        dve.wait_ge(th_in_sem[int(name != "y0")], 16)
                    c = slice((name[0] == "h") * HALF, ((name[0] == "h") + 1) * HALF)
                    t = k.yacc[:, int(name[1]), c]
                    dve.wait_ge(m_free, TAIL0 + n + 1)
                    nc.vector.scalar_tensor_tensor(out=t, in0=k.th_in[:, int(name[1]), c], scalar=1.0, in1=t,
                                                   op0=ALU.add, op1=ALU.mult).then_inc(ym_rdy, 1)

            for kt in range(NKT):
                turned_lo(v, kt)
                if kt == 0:
                    latent_lo(v - 1)
                if kt in (1, 2):
                    tail(kt - 1)
                if kt >= 6:
                    tail(kt - 4)
            for n in range(NKT - 4, len(TAIL)):
                if n == NKT - 2:
                    latent_lo(v)
                tail(n)

        @block.tensor
        def _(pe):
            def small(name, at, b, half=0, slot=0, unit=None, ju=None):
                if not (static(at) and at < 2):
                    pe.wait_ge(m_free, at - 1)
                ps = ps_m[b]
                if name == "turn":
                    for kt in range(QLT):
                        nc.tensor.transpose(ps[:, kt * P:(kt + 1) * P], wq_st[:, slot, kt, 0:NOPE], k.ident[:])
                    last = nc.tensor.transpose(ps[:, 2 * P:3 * P], wkv_st[:, slot, 0:NOPE], k.ident[:])
                elif name == "absorb":
                    for kt in range(QLT):
                        w = slice(kt * P, (kt + 1) * P)
                        last = mm3(nc, ps[:, w], opH[:, w], opL[:, w], opH[:, 2 * P:3 * P], opL[:, 2 * P:3 * P],
                                   True, True)
                elif name == "q":
                    for kt in range(QLT):
                        w = slice(kt * P, (kt + 1) * P)
                        c = slice(half * HALF, (half + 1) * HALF)
                        last = mm3(nc, ps[:], wcH[:, slot, w], wcL[:, slot, w], k.qnH[:, kt, c], k.qnL[:, kt, c],
                                   kt == 0, kt == QLT - 1)
                elif name == "rope":
                    for kt in range(QLT):
                        c = slice(half * HALF, (half + 1) * HALF)
                        last = mm3(nc, ps[:], wrH[:, kt, :, :].rearrange("p a b -> p (a b)"),
                                   wrL[:, kt, :, :].rearrange("p a b -> p (a b)"), k.qnH[:, kt, c], k.qnL[:, kt, c],
                                   kt == 0, kt == QLT - 1)
                elif name == "R":
                    pe.wait_ge(rinv_rdy, unit + 1)
                    for t in range(QT):
                        last = nc.tensor.transpose(ps[:, t * P:(t + 1) * P],
                                                   rinv[:, ju % 2, t:t + 1].to_broadcast([P, P]), k.ident[:])
                elif name == "o":
                    pe.wait_ge(opL_rdy, unit + 1)
                    last = mm3(nc, ps[:], wvH[:, slot, :], wvL[:, slot, :], opH[:], opL[:], True, True)
                else:
                    y_half = int(name[0] == "h")
                    w = slice(int(name[1]) * P, (int(name[1]) + 1) * P)
                    for hp in range(2):
                        last = mm3(nc, ps[:], wpH[:, hp, w], wpL[:, hp, w], zH[:, hp, y_half, :], zL[:, hp, y_half, :],
                                   hp == 0, hp == 1)
                last.then_inc(m_ps, 1)

            def scores(j, qt, c):
                half, hp = j % 2, j // 2
                lo_, hi_ = QCHUNKS[c]
                t = slice(qt * P, (qt + 1) * P)
                t2 = slice(half * HALF + qt * P, half * HALF + (qt + 1) * P)
                kc = slice(lo_, hi_)
                out = ps_s[:, kc]
                nc.tensor.matmul(out, qpH[:, half, t], k.cH[:, kc], start=True, stop=False)
                nc.tensor.matmul(out, qpH[:, half, t], k.cL[:, kc], start=False, stop=False)
                nc.tensor.matmul(out, qpL[:, half, t], k.cH[:, kc], start=False, stop=False)
                nc.tensor.matmul(out, q2[hp][:, t2], k.k2H[:, kc], start=False, stop=False)
                nc.tensor.matmul(out, q2[hp][:, t2], k.k2L[:, kc], start=False, stop=True).then_inc(s_chunk[c], 1)

            def turn_weights(v, jv, kt):
                if kt == 0:
                    pe.wait_ge(e_rdy, 4 * (v + 1))
                positive(pe, ptL_rdy, NKT * v + (kt - 1))
                for t in range(QT):
                    last = nc.tensor.transpose(ps_pt[kt % 2][:, t * P:(t + 1) * P],
                                               E[:, jv % 2, t, kt * P:(kt + 1) * P], k.ident[:])
                last.then_inc(pt_ps, 1)

            def values(v, kt):
                pe.wait_ge(ptL_rdy, NKT * v + (kt + 1))
                if kt == 0:
                    positive(pe, opL_rdy, v)
                mm3(nc, ps_o[:], k.ctokH[:, kt, :], k.ctokL[:, kt, :], ptH[:, kt % 2, :], ptL[:, kt % 2, :],
                    kt == 0, kt == NKT - 1).then_inc(pv, 1)

            pe.wait_ge(wq_in[0], 32)
            small("turn", 0, 0, slot=0)
            pe.wait_ge(wrL_rdy, 2)
            small("rope", 1, 1, half=0)
            pe.wait_ge(m_free, 1)
            small("absorb", 2, 0)
            pe.wait_ge(m_free, 3)
            small("q", 3, 1, half=0, slot=0)

            def body(i, kind):
                for j in range(4):
                    u = 4 * i + j
                    v, w = u - 1, u - 2
                    has_v = kind != "first" or j > 0
                    has_w = kind != "first" or j > 1

                    def at(name, jj=j):
                        return product_index(i, jj, name, kind)

                    def filler(name):
                        a, b = at(name), product_bank(j, name, kind)
                        if name == "turn":
                            slot = (j // 2 + 1) % 2
                            pe.wait_ge(wq_in[slot], 32 * i + (32 if j == 0 else 64))
                            small(name, a, b, slot=slot)
                        elif name == "absorb":
                            pe.wait_ge(m_free, at("turn") + 1)
                            small(name, a, b)
                        elif name == "q":
                            if j % 2:
                                pe.wait_ge(m_free, at("absorb", j - 1) + 1)
                            small(name, a, b, half=(j + 1) % 2, slot=((j + 1) // 2) % 2)
                        elif name == "rope":
                            pe.wait_ge(wrL_rdy, 2 * i + (2 if j == 0 else 4))
                            small(name, a, b, half=1 if j == 0 else 0)
                        elif name == "o":
                            pe.wait_ge(wvL_rdy, 2 * i + j // 2)
                            small(name, a, b, slot=(j // 2 + 1) % 2, unit=w)
                        elif name == "R":
                            small(name, a, b, unit=w, ju=j)
                        else:
                            if name == "y0":
                                pe.wait_ge(wpL_rdy, 2 * i)
                                pe.wait_ge(z_rdy, 4 * i - 1)
                            if name == "h0":
                                pe.wait_ge(z_rdy, 4 * i)
                            small(name, a, b)

                    for qt in range(QT):
                        n = 4 * u + qt
                        kts = QKT[j][qt] if has_v else ()
                        names = list(unit_products(j, kind)[qt])
                        positive(pe, e_rdy, n)
                        if qt == 0:
                            pe.wait_ge(m_free, at("q", j - 1) + 1 if j else M_PRO if kind == "first" else at("rope"))
                            if j < 2:
                                pe.wait_ge(q2_rdy, 2 * i + (j + 1))
                        scores(j, qt, 0)
                        if has_v:
                            turn_weights(v, (j - 1) % 4, kts[0])
                        scores(j, qt, 1)
                        if qt == 0 and has_w:
                            values(w, NKT - 1)
                        if qt and has_v:
                            values(v, kts[0] - 1)
                        if has_v:
                            turn_weights(v, (j - 1) % 4, kts[1])
                        scores(j, qt, 2)
                        for name in names[:1]:
                            filler(name)
                        if has_v:
                            values(v, kts[0])
                        for kt in kts[2:]:
                            turn_weights(v, (j - 1) % 4, kt)
                        for name in names[1:2]:
                            filler(name)
                        for kt in kts[2:]:
                            values(v, kt - 1)
                        for name in names[2:]:
                            filler(name)

            bodies(pe, body)
            v = UNITS - 1

            def tail(n):
                last = "last" in TAIL[n]
                small(TAIL[n].split()[0], TAIL0 + n, (TAIL0 + n) % 2, slot=1, unit=v if last else v - 1,
                      ju=3 if last else 2)

            for kt in range(NKT):
                turn_weights(v, 3, kt)
                values(v if kt else v - 1, kt - 1 if kt else NKT - 1)
                if kt in (1, 2):
                    if kt == 2:
                        pe.wait_ge(wvL_rdy, HEADS)
                    tail(kt - 1)
                if kt >= 6:
                    if kt == 6:
                        pe.wait_ge(wpL_rdy, HEADS)
                        pe.wait_ge(z_rdy, UNITS - 1)
                    tail(kt - 4)
            values(v, NKT - 1)
            for n in range(NKT - 4, len(TAIL)):
                if TAIL[n] == "h0":
                    pe.wait_ge(z_rdy, UNITS)
                tail(n)


def stage_output(nc, k):
    with ExitStack() as ctx:
        def sb(name, shape, dt=F32):
            return ctx.enter_context(nc.sbuf_tensor(name, shape, dt))

        def sem(name):
            return ctx.enter_context(nc.semaphore(name))

        yH, woH, woL = k.yH, k.woH, k.woL
        sb("yH_place", [P, KT, SEQ])
        junk = sb("junk4", [P, D], BF16)
        gate = sb("gate", [P, D])
        fg = sb("fg", [P, D])
        xr = [sb("xr0", [P, D])]
        assert KT * SEQ + D // 2 + 3 * D == 2 * QLT * SEQ + 4 * KEYS + 2 * NKT * KVL
        sb("woL_place", [P, KT, D])
        sb("woH_place", [P, KT, D])
        yp_in, yL = loaded_as(nc, ctx, "yp_in", "yL", [P, KT, SEQ])
        xr.append(sb("xr1", [P, D]))
        res = sb("res", [P, 2, D])
        fsq = sb("fsq", [P, XT, 3])
        ps_r = [ctx.enter_context(nc.psum_tensor(f"ps_r{b}", [P, HALF], F32)) for b in range(8)]
        ps_g = ps_r[6:8]

        YS = 4
        ypd_in = [sem(f"ypd_in{b}") for b in range(YS)]
        wo_in = [sem(f"wo_in{b}") for b in range(KT - WO_EARLY)]
        fg_in = sem("fg_in")
        xr_in = [sem("xr_in0"), sem("xr_in1")]
        y_rdy = sem("y_rdy")
        yL_rdy = sem("yL_rdy")
        yH_rdy, woH_rdy, woL_rdy = k.yH_rdy, k.woH_rdy, k.woL_rdy
        gt_ps = sem("gt_ps")
        gt_rdy = sem("gt_rdy")
        r_ps = sem("r_ps")
        r_read = sem("r_read")
        r_step = sem("r_step")
        sq_rdy = sem("sq_rdy")
        rt_rdy = sem("rt_rdy")
        ri_rdy = sem("ri_rdy")
        res_rdy = sem("res_rdy")
        out_done = [sem("out_done0"), sem("out_done1")]

        block = ctx.enter_context(nc.Block())

        @block.sync
        def _(sp):
            for kt in range(1, KT):
                if kt >= YS:
                    sp.wait_ge(yL_rdy, kt - YS + 1)
                sp.dma_start(yp_in[:, kt, :], k.yp_d[kt]).then_inc(ypd_in[kt % YS], 16)
                wt = WO_EARLY + kt - 1
                if wt < KT:
                    sp.dma_start(k.wo_raw[:, wt, :], k.w_out[wt * P:(wt + 1) * P, :]).then_inc(wo_in[wt - WO_EARLY], 16)
            sp.dma_start(fg[:], k.final_g.to_broadcast([P, D])).then_inc(fg_in, 16)
            for t in range(XT):
                if t >= 2:
                    sp.wait_ge(r_step, 2 * (t - 1))
                sp.dma_start(xr[t % 2][:], k.x[t * P:(t + 1) * P, :]).then_inc(xr_in[t % 2], 16)
                if t:
                    sp.wait_ge(res_rdy, t)
                    sp.dma_start(k.out[(t - 1) * P:t * P, :], res[:, (t - 1) % 2, :]).then_inc(out_done[(t - 1) % 2], 16)
            sp.wait_ge(res_rdy, XT)
            sp.dma_start(k.out[(XT - 1) * P:XT * P, :], res[:, (XT - 1) % 2, :]).then_inc(out_done[(XT - 1) % 2], 16)
            for b in range(2):
                sp.wait_ge(out_done[b], 16 * XT // 2)

        @block.gpsimd
        def _(pool):
            for kt in range(SPLIT_EARLY, KT):
                pool.wait_ge(woH_rdy, kt + 1)
                nc.gpsimd.tensor_tensor(woL[:, kt, :], k.wo_raw[:, kt, :], woH[:, kt, :].bitcast(F32), ALU.subtract
                                        ).then_inc(woL_rdy, 1)

        @block.scalar
        def _(act):
            for kt in range(1, KT):
                act.wait_ge(y_rdy, kt)
                nc.scalar.activation(yH[:, kt, :], k.yacc[:, kt, :], ACT.Copy).then_inc(yH_rdy, 1)
                wt = kt + SPLIT_EARLY - 1
                if wt < KT:
                    act.wait_ge(k.wo_in_sem if wt < WO_EARLY else wo_in[wt - WO_EARLY], 16)
                    nc.scalar.activation(woH[:, wt, :], k.wo_raw[:, wt, :], ACT.Copy).then_inc(woH_rdy, 1)
            for t in range(XT):
                act.wait_ge(r_step, 2 * (t + 1))
                if t:
                    act.wait_ge(rt_rdy, t)
                nc.scalar.activation(junk[:], res[:, t % 2, :], ACT.Square, accum_out=fsq[:, t, 0:1]).then_inc(sq_rdy, 1)
                act.wait_ge(sq_rdy, t + 1)
                nc.scalar.activation(fsq[:, t, 1:2], fsq[:, t, 0:1], ACT.Sqrt, scale=1.0 / D, bias=k.eps[:, 0:1]
                                     ).then_inc(rt_rdy, 1)

        @block.vector
        def _(dve):
            for kt in range(KT):
                t = k.yacc[:, kt, :]
                if kt:
                    dve.wait_ge(ypd_in[kt % YS], 16 * ((kt - (kt % YS or YS)) // YS + 1))
                    nc.vector.tensor_tensor(t, t, yp_in[:, kt, :], ALU.add).then_inc(y_rdy, 1)
                dve.wait_ge(yH_rdy, kt + 1)
                nc.vector.tensor_tensor(yL[:, kt, :], t, yH[:, kt, :].bitcast(F32), ALU.subtract).then_inc(yL_rdy, 1)
            for h in range(2):
                dve.wait_ge(gt_ps, h + 1)
                nc.vector.tensor_scalar(gate[:, h * HALF:(h + 1) * HALF], ps_g[h][:], 0.5, None, ALU.mult
                                        ).then_inc(gt_rdy, 1)
            dve.wait_ge(gt_rdy, 2)
            for t in range(XT):
                if t >= 2:
                    dve.wait_ge(out_done[t % 2], 16 * (t // 2))
                for h in range(2):
                    dve.wait_ge(r_ps, 2 * t + h + 1)
                    c = slice(h * HALF, (h + 1) * HALF)
                    nc.vector.tensor_tensor(res[:, t % 2, c], ps_r[(2 * t + h) % 8][:], gate[:, c], ALU.mult
                                            ).then_inc(r_read, 1)
                    dve.wait_ge(r_read, 2 * t + h + 1)
                    if h == 0:
                        dve.wait_ge(xr_in[t % 2], 16 * (t // 2 + 1))
                    nc.vector.tensor_tensor(res[:, t % 2, c], res[:, t % 2, c], xr[t % 2][:, c], ALU.add
                                            ).then_inc(r_step, 1)
                if t == 0:
                    dve.wait_ge(fg_in, 16)
                dve.wait_ge(rt_rdy, t + 1)
                nc.vector.reciprocal(fsq[:, t, 2:3], fsq[:, t, 1:2]).then_inc(ri_rdy, 1)
                dve.wait_ge(ri_rdy, t + 1)
                nc.vector.scalar_tensor_tensor(out=res[:, t % 2, :], in0=res[:, t % 2, :], scalar=fsq[:, t, 2:3],
                                               in1=fg[:], op0=ALU.mult, op1=ALU.mult).then_inc(res_rdy, 1)

        @block.tensor
        def _(pe):
            for h in range(2):
                for f in range(QT):
                    ft = h * QT + f
                    last = nc.tensor.transpose(ps_g[h][:, f * P:(f + 1) * P],
                                               k.gateT[:, ft:ft + 1].to_broadcast([P, P]), k.ident[:])
                last.then_inc(gt_ps, 1)
            def product(n, kt):
                ts, c = slice(n // 2 * P, (n // 2 + 1) * P), slice(n % 2 * HALF, (n % 2 + 1) * HALF)
                return mm3(nc, ps_r[n % 8][:], yH[:, kt, ts], yL[:, kt, ts], woH[:, kt, c], woL[:, kt, c],
                           kt == 0, kt == KT - 1)

            for kt in range(KT):
                pe.wait_ge(yL_rdy, kt + 1)
                pe.wait_ge(woL_rdy, kt + 1)
                for n in range(6):
                    last = product(n, kt)
                    if kt == KT - 1:
                        last.then_inc(r_ps, 1)
            for n in range(6, 2 * XT):
                if n == 6:
                    pe.wait_ge(gt_rdy, 2)
                if n >= 8:
                    pe.wait_ge(r_read, n - 7)
                for kt in range(KT):
                    last = product(n, kt)
                last.then_inc(r_ps, 1)


def build_program(nc, k):
    with ExitStack() as ctx:
        def sb(name, shape, dt=F32):
            return ctx.enter_context(nc.sbuf_tensor(name, shape, dt))

        k.ident = sb("ident", [P, P])
        k.vt = sb("vt", [P, R_END])
        k.eps = sb("eps", [P, 1])
        k.qgs = sb("qgs", [P, QLT])
        k.bgh = sb("bgh", [P, 2 * KT])
        k.gateT = sb("gateT", [P, KT])
        k.cond = sb("cond", [P, KT, 2])
        k.woH_rdy, k.woL_rdy, k.yH_rdy = (ctx.enter_context(nc.semaphore(n)) for n in ("woH_rdy", "woL_rdy", "yH_rdy"))
        k.stored = [ctx.enter_context(nc.semaphore(f"stored{h}")) for h in range(2)]
        k.wq_in = [ctx.enter_context(nc.semaphore(f"wq_in{b}")) for b in range(2)]
        k.cs_in = ctx.enter_context(nc.semaphore("cs_in"))
        k.wo_in_sem = ctx.enter_context(nc.semaphore("wo_in_sem"))
        with ExitStack() as place:
            k.th_in, k.yH = loaded_as(nc, place, "th_in", "yH", [P, KT, SEQ])
        with ExitStack() as latents:
            def lat(name, shape, dt=F32R):
                return latents.enter_context(nc.sbuf_tensor(name, shape, dt))

            k.qnH = lat("qnH", [P, QLT, SEQ])
            k.qnL = lat("qnL", [P, QLT, SEQ])
            k.cH = lat("cH", [P, KEYS])
            k.cL = lat("cL", [P, KEYS])
            k.k2H = lat("k2H", [P, KEYS])
            k.k2L = lat("k2L", [P, KEYS])
            k.ctokH = lat("ctokH", [P, NKT, KVL])
            k.ctokL = lat("ctokL", [P, NKT, KVL])
            with ExitStack() as early:
                k.hH = early.enter_context(nc.sbuf_tensor("hH", [P, KT, SEQ], F32R))
                k.h_raw, k.hL = loaded_as(nc, early, "h_raw", "hL", [P, KT, SEQ])
                k.wst = early.enter_context(nc.sbuf_tensor("wst", [P, 2, D], F32))
                k.w_in_sem = [early.enter_context(nc.semaphore(f"w_in{b}")) for b in range(2)]
                k.wH_rdy, k.wL_rdy = (early.enter_context(nc.semaphore(n)) for n in ("wH_rdy2", "wL_rdy2"))
                k.half_ps, k.used = (early.enter_context(nc.semaphore(n)) for n in ("half_ps", "w_used"))
                k.bank = [early.enter_context(nc.psum_tensor(f"bank{b}", [P, HALF], F32)) for b in range(4)]
                stage_tokens(nc, k)
                stage_gates(nc, k)
            k.yacc = ctx.enter_context(nc.sbuf_tensor("yacc", [P, KT, SEQ], F32, side="right"))
            stage_attention(nc, k)
        stage_output(nc, k)


def rope_tables():
    import numpy as np
    half = ROPE // 2
    inv = (1.0 / (np.float32(10000.0) ** (np.arange(0, half, 2, dtype=np.float32) / np.float32(half)))).astype(np.float32)
    t = np.arange(SEQ)
    ang = np.concatenate([(t // 64).astype(np.float32)[:, None] * inv, (t % 64).astype(np.float32)[:, None] * inv], axis=1)
    cos, sin = np.cos(ang).astype(np.float32), np.sin(ang).astype(np.float32)
    q_cos = np.tile(cos.T, (P // RH, 1))
    q_sin = np.concatenate([-sin.T, sin.T] * (P // ROPE), axis=0)
    return cos, sin, np.ascontiguousarray(q_cos), np.ascontiguousarray(q_sin)


def pool_counts():
    import numpy as np
    t = np.arange(SEQ)
    rows = [1.0 / (np.clip(t + w // 2, 0, SEQ) - np.clip(t - w // 2, 0, SEQ)).astype(np.float32) for w in WINDOWS]
    return np.stack(rows).astype(np.float32)


def kernel(x, c, ctx, c_ctx, ada_w, ada_b, norm_g, w_in, b_gate, w_pool, pool_scale, q_norm_g, w_qb,
           kv_norm_g, w_kvb, w_proj_pool, w_proj_mla, w_out, final_g):
    import numpy as np
    import concourse.bacc as bacc
    from concourse.bass_utils import run_bass_kernel_spmd

    nc = bacc.Bacc("TRN2", target_bir_lowering=False, num_devices=1)
    cos, sin, q_cos, q_sin = rope_tables()
    arrays = {
        "x": np.asarray(x).reshape(SEQ, D), "ctx": np.asarray(ctx).reshape(CTX, D),
        "c": np.asarray(c).reshape(KT, P), "c_ctx": np.asarray(c_ctx).reshape(KT, P),
        "ada_w": np.asarray(ada_w)[0], "ada_b": np.asarray(ada_b).reshape(3 * KT, P),
        "norm_g": np.asarray(norm_g).reshape(KT, P), "w_in": np.asarray(w_in)[0],
        "b_gate": np.asarray(b_gate).reshape(2 * KT, P), "w_pool": np.asarray(w_pool)[0],
        "pool_scale": np.asarray(pool_scale).reshape(KT, P), "q_norm_g": np.asarray(q_norm_g).reshape(QLT, P),
        "w_qb": np.asarray(w_qb)[0], "kv_norm_g": np.asarray(kv_norm_g).reshape(1, KVL),
        "w_kvb": np.asarray(w_kvb)[0], "w_proj_pool": np.asarray(w_proj_pool)[0],
        "w_proj_mla": np.asarray(w_proj_mla)[0], "w_out": np.asarray(w_out)[0],
        "final_g": np.asarray(final_g).reshape(1, D),
        "ident_d": np.eye(P, dtype=np.float32), "kcos_d": cos, "ksin_d": sin, "qcos_d": q_cos, "qsin_d": q_sin,
        "pool_inv": pool_counts(),
    }
    arrays = {n: np.ascontiguousarray(a) for n, a in arrays.items()}
    k = Chip()
    for n, a in arrays.items():
        k.__dict__[n] = nc.dram_tensor("in_" + n, a.shape, F32, kind="ExternalInput").ap()
    k.out = nc.dram_tensor("out", (SEQ, D), F32, kind="ExternalOutput").ap()
    k.sg_d = nc.dram_tensor("sg_scratch", (HEADS, P, SEQ), F32, kind="Internal").ap()
    k.yp_d = nc.dram_tensor("yp_scratch", (KT, P, SEQ), F32, kind="Internal").ap()
    k.thp_d = nc.dram_tensor("thp_scratch", (KT, P, SEQ), F32, kind="Internal").ap()
    k.th_d = nc.dram_tensor("th_scratch", (KT, P, SEQ), F32, kind="Internal").ap()
    build_program(nc, k)
    result = run_bass_kernel_spmd(nc, [{"in_" + n: a for n, a in arrays.items()}], core_ids=[0]).results[0]["out"]
    return result.reshape(1, SEQ, D)
```
